# Optimizing a Trainium2 kernel written in Bass

```python
import math
import jax, jax.numpy as jnp
from jax import lax
import numpy as np

D_MODEL = 1024
BATCH = 1
SEQ = 256
DEPTH = 1

MIX_WIDTH = D_MODEL
HEAD_DIM = 64
SWA_Q_HEADS = 8
SWA_KV_HEADS = 2
SWA_GROUP = SWA_Q_HEADS // SWA_KV_HEADS
WINDOW = 128
BLOCK = 128
DIFF_HEADS = 4
DIFF_VDIM = 2 * HEAD_DIM
Q_BLOCK = 128
SWA_Q_COLS = SWA_Q_HEADS * HEAD_DIM
SWA_KV_COLS = SWA_KV_HEADS * HEAD_DIM
DIFF_QK_COLS = DIFF_HEADS * 2 * HEAD_DIM
DIFF_V_COLS = DIFF_HEADS * DIFF_VDIM
IN_COLS = SWA_Q_COLS + 2 * SWA_KV_COLS + 2 * DIFF_QK_COLS + DIFF_V_COLS
SWA_OUT = SWA_Q_HEADS * HEAD_DIM
DIFF_OUT = DIFF_HEADS * DIFF_VDIM
MEM_LEN = 256
CROSS_HEADS = 4
CROSS_HEAD_DIM = D_MODEL // CROSS_HEADS
D_FF = 4 * D_MODEL
ROPE_THETA = 10000.0
NORM_EPS = 1e-5


def rms_norm(x, g, eps=NORM_EPS):
    xf = x.astype(jnp.float32)
    y = xf * lax.rsqrt(jnp.mean(xf * xf, axis=-1, keepdims=True) + eps)
    return (y * g.astype(jnp.float32)).astype(x.dtype)

def rope_tables(positions, dim):
    inv_freq = ROPE_THETA ** (-jnp.arange(0, dim, 2, dtype=jnp.float32) / dim)
    ang = positions.astype(jnp.float32)[..., None] * inv_freq
    return jnp.cos(ang), jnp.sin(ang)

def apply_rope(x, cos, sin):
    shp = cos.shape[:2] + (1,) * (x.ndim - 3) + cos.shape[-1:]
    c = cos.reshape(shp).astype(x.dtype)
    s = sin.reshape(shp).astype(x.dtype)
    x1, x2 = jnp.split(x, 2, axis=-1)
    return jnp.concatenate([x1 * c - x2 * s, x2 * c + x1 * s], axis=-1)

def sliding_window_sink_attention(q, k, v, sinks):
    Bn, S = q.shape[0], q.shape[1]
    nb = S // BLOCK
    scale = HEAD_DIM ** -0.5
    qb = q.reshape(Bn, nb, BLOCK, SWA_KV_HEADS, SWA_GROUP, HEAD_DIM)
    kb = k.reshape(Bn, nb, BLOCK, SWA_KV_HEADS, HEAD_DIM)
    vb = v.reshape(Bn, nb, BLOCK, SWA_KV_HEADS, HEAD_DIM)
    pad = ((0, 0), (1, 0), (0, 0), (0, 0), (0, 0))
    kw = jnp.concatenate([jnp.pad(kb, pad)[:, :-1], kb], axis=2)
    vw = jnp.concatenate([jnp.pad(vb, pad)[:, :-1], vb], axis=2)
    s = jnp.einsum('bnqhgd,bnkhd->bnhgqk', qb, kw).astype(jnp.float32) * scale
    qi = jnp.arange(BLOCK)[:, None]
    kj = jnp.arange(2 * BLOCK)[None, :]
    rel = qi + BLOCK - kj
    band = (rel >= 0) & (rel < WINDOW)
    exists = (jnp.arange(nb)[:, None, None] * BLOCK + kj[None]) >= BLOCK
    valid = band[None] & exists
    s = jnp.where(valid[None, :, None, None], s, -jnp.inf)
    sink = sinks.astype(jnp.float32).reshape(SWA_KV_HEADS, SWA_GROUP)[None, None, :, :, None, None]
    m = jnp.maximum(jnp.max(s, axis=-1, keepdims=True), sink)
    e = jnp.exp(s - m)
    p = e / (jnp.sum(e, axis=-1, keepdims=True) + jnp.exp(sink - m))
    o = jnp.einsum('bnhgqk,bnkhd->bnqhgd', p.astype(v.dtype), vw)
    return o.reshape(Bn, S, SWA_OUT)

def differential_attention(q, k, v, lam):
    Bn, S = q.shape[0], q.shape[1]
    nb = S // Q_BLOCK
    scale = HEAD_DIM ** -0.5
    qb = q.reshape(Bn, nb, Q_BLOCK, DIFF_HEADS, 2, HEAD_DIM).swapaxes(0, 1)
    starts = jnp.arange(nb) * Q_BLOCK
    kpos = jnp.arange(S)

    def one_block(args):
        qblk, start = args
        s = jnp.einsum('bqhcd,bkhcd->bhcqk', qblk, k).astype(jnp.float32) * scale
        mask = kpos[None, :] <= (start + jnp.arange(Q_BLOCK))[:, None]
        s = jnp.where(mask, s, -jnp.inf)
        p = jax.nn.softmax(s, axis=-1)
        a = p[:, :, 0] - lam * p[:, :, 1]
        return jnp.einsum('bhqk,bkhe->bqhe', a.astype(v.dtype), v)

    o = lax.map(one_block, (qb, starts))
    return o.swapaxes(0, 1).reshape(Bn, S, DIFF_HEADS, DIFF_VDIM)

def cross_attention(h, m, w_q, w_kv, w_o):
    Bn, S = h.shape[0], h.shape[1]
    q = (h @ w_q).reshape(Bn, S, CROSS_HEADS, CROSS_HEAD_DIM)
    kv = (m @ w_kv).reshape(Bn, m.shape[1], 2, CROSS_HEADS, CROSS_HEAD_DIM)
    k, v = kv[:, :, 0], kv[:, :, 1]
    s = jnp.einsum('bshd,bmhd->bhsm', q, k).astype(jnp.float32) * CROSS_HEAD_DIM ** -0.5
    p = jax.nn.softmax(s, axis=-1)
    o = jnp.einsum('bhsm,bmhd->bshd', p.astype(v.dtype), v).reshape(Bn, S, D_MODEL)
    return o @ w_o

def first_inputs(seed: int = 0) -> dict:
    key = jax.random.key(seed)
    ks = jax.random.split(key, 24)
    f32 = jnp.float32
    L = DEPTH

    def w(k, shape, fan_in):
        return jax.random.normal(k, shape, f32) * fan_in ** -0.5

    def gain(k, shape):
        return 1.0 + 0.02 * jax.random.normal(k, shape, f32)

    x = jax.random.normal(ks[0], (BATCH, SEQ, D_MODEL), f32)
    mem = jax.random.normal(ks[1], (BATCH, MEM_LEN, D_MODEL), f32)
    positions = (jnp.arange(SEQ, dtype=jnp.int32)[None, :]
                 + jax.random.randint(ks[2], (BATCH, 1), 0, 1024, dtype=jnp.int32))
    return {
        "x": x,
        "mem": mem,
        "positions": positions,
        "g_mix": gain(ks[3], (L, D_MODEL)),
        "w_in": w(ks[4], (L, D_MODEL, IN_COLS), D_MODEL),
        "sinks": 0.5 * jax.random.normal(ks[5], (L, SWA_Q_HEADS), f32),
        "lambda_q1": 0.1 * jax.random.normal(ks[6], (L, HEAD_DIM), f32),
        "lambda_k1": 0.1 * jax.random.normal(ks[7], (L, HEAD_DIM), f32),
        "lambda_q2": 0.1 * jax.random.normal(ks[8], (L, HEAD_DIM), f32),
        "lambda_k2": 0.1 * jax.random.normal(ks[9], (L, HEAD_DIM), f32),
        "g_diff": gain(ks[10], (L, DIFF_VDIM)),
        "w_out": w(ks[11], (L, MIX_WIDTH, D_MODEL), MIX_WIDTH),
        "g_cross": gain(ks[12], (L, D_MODEL)),
        "g_mem": gain(ks[13], (L, D_MODEL)),
        "w_cq": w(ks[14], (L, D_MODEL, D_MODEL), D_MODEL),
        "w_ckv": w(ks[15], (L, D_MODEL, 2 * D_MODEL), D_MODEL),
        "w_co": w(ks[16], (L, D_MODEL, D_MODEL), D_MODEL),
        "g_mlp": gain(ks[17], (L, D_MODEL)),
        "w_up": w(ks[18], (L, D_MODEL, D_FF), D_MODEL),
        "w_down": w(ks[19], (L, D_FF, D_MODEL), D_FF),
        "g_final": gain(ks[20], (D_MODEL,)),
    }

def first_block(x, mem, positions, g_mix, w_in, sinks, lambda_q1, lambda_k1, lambda_q2, lambda_k2,
              g_diff, w_out, g_cross, g_mem, w_cq, w_ckv, w_co, g_mlp, w_up, w_down, g_final):
    Bn, S = x.shape[0], x.shape[1]
    cos, sin = rope_tables(positions, HEAD_DIM)
    splits = np.cumsum([SWA_Q_COLS, SWA_KV_COLS, SWA_KV_COLS, DIFF_QK_COLS, DIFF_QK_COLS])
    for l in range(DEPTH):
        h = rms_norm(x, g_mix[l])
        proj = h @ w_in[l]
        qa, ka, va, qd, kd, vd = jnp.split(proj, splits, axis=-1)
        qa = apply_rope(qa.reshape(Bn, S, SWA_KV_HEADS, SWA_GROUP, HEAD_DIM), cos, sin)
        ka = apply_rope(ka.reshape(Bn, S, SWA_KV_HEADS, HEAD_DIM), cos, sin)
        va = va.reshape(Bn, S, SWA_KV_HEADS, HEAD_DIM)
        out_a = sliding_window_sink_attention(qa, ka, va, sinks[l])

        lam_init = 0.8 - 0.6 * math.exp(-0.3 * l)
        lam = (jnp.exp(jnp.sum(lambda_q1[l].astype(jnp.float32) * lambda_k1[l].astype(jnp.float32)))
               - jnp.exp(jnp.sum(lambda_q2[l].astype(jnp.float32) * lambda_k2[l].astype(jnp.float32)))
               + lam_init)
        qd = apply_rope(qd.reshape(Bn, S, DIFF_HEADS, 2, HEAD_DIM), cos, sin)
        kd = apply_rope(kd.reshape(Bn, S, DIFF_HEADS, 2, HEAD_DIM), cos, sin)
        vd = vd.reshape(Bn, S, DIFF_HEADS, DIFF_VDIM)
        od = differential_attention(qd, kd, vd, lam)
        out_b = (rms_norm(od, g_diff[l]) * (1.0 - lam_init)).reshape(Bn, S, DIFF_OUT)

        x = x + jnp.concatenate([out_a, out_b], axis=-1) @ w_out[l]

        x = x + cross_attention(rms_norm(x, g_cross[l]), rms_norm(mem, g_mem[l]),
                                w_cq[l], w_ckv[l], w_co[l])

        u = rms_norm(x, g_mlp[l]) @ w_up[l]
        x = x + jnp.square(jax.nn.relu(u)) @ w_down[l]
    return rms_norm(x, g_final)


DEPTH_2 = 2

D_FF_2 = 2816
N_EVEN = (DEPTH_2 + 1) // 2
N_ODD = DEPTH_2 // 2
N_ADA = 9
EPS = 1e-6
NEG_INF = -1e30

CONV_WIDTH = 512
CONV_GROUPS = 8
CONV_TAPS = 3
MLA_HEADS = 8
MLA_NOPE = 64
MLA_ROPE = 32
MLA_V = 64
Q_LORA = 256
KV_LORA = 128
HY_IN = 3 * CONV_WIDTH + Q_LORA + KV_LORA + MLA_ROPE
HY_MIX = CONV_WIDTH + MLA_HEADS * MLA_V
NSA_HEADS = 16
NSA_KV_HEADS = 2
NSA_GROUP = NSA_HEADS // NSA_KV_HEADS
NSA_DK = 64
CMP_BLOCK = 32
CMP_STRIDE = 16
CMP_HID = 128
SLC_BLOCK = 64
N_SEL = 8
WINDOW_2 = 512
FORCE_SCORE = 1e4
NSA_KV_W = 2 * NSA_KV_HEADS * NSA_DK
NSA_IN = NSA_HEADS * NSA_DK + 3 * NSA_KV_W + 3 * NSA_HEADS


def rms_norm_2(x, g):
    xf = x.astype(jnp.float32)
    y = xf * lax.rsqrt(jnp.mean(xf * xf, axis=-1, keepdims=True) + EPS)
    return (y * g.astype(jnp.float32)).astype(x.dtype)

def modulate(x, g, shift, scale):
    return rms_norm_2(x, g) * (1 + scale[:, None]) + shift[:, None]

def swiglu(h, w13, w2):
    a, b = jnp.split(h @ w13, 2, axis=-1)
    return (jax.nn.silu(a) * b) @ w2

def masked_softmax(s, mask):
    s = jnp.where(mask, s.astype(jnp.float32), NEG_INF)
    m = jnp.max(s, axis=-1, keepdims=True)
    p = jnp.exp(s - m) * mask
    return p / jnp.maximum(jnp.sum(p, axis=-1, keepdims=True), 1e-20)

def rope_tables_2(positions):
    half = MLA_ROPE // 2
    inv = ROPE_THETA ** (-jnp.arange(half, dtype=jnp.float32) / half)
    ang = positions.astype(jnp.float32)[..., None] * inv
    return jnp.cos(ang), jnp.sin(ang)

def apply_rope_2(t, cos, sin):
    half = t.shape[-1] // 2
    t1 = t[..., :half].astype(jnp.float32)
    t2 = t[..., half:].astype(jnp.float32)
    return jnp.concatenate([t1 * cos - t2 * sin, t1 * sin + t2 * cos], axis=-1).astype(t.dtype)

def to_blocks(t, nqb):
    return jnp.moveaxis(t.reshape(t.shape[0], nqb, Q_BLOCK, *t.shape[2:]), 1, 0)

def from_blocks(o):
    o = jnp.moveaxis(o, 0, 1)
    return o.reshape(o.shape[0], o.shape[1] * o.shape[2], *o.shape[3:])

def short_conv(u, conv_w):
    ch = u.shape[-1]
    return lax.conv_general_dilated(
        u, conv_w[:, None, :], window_strides=(1,), padding=((CONV_TAPS - 1, 0),),
        dimension_numbers=('NWC', 'WIO', 'NWC'), feature_group_count=ch)

def mla_attention(q_nope, q_rope, k_nope, k_rope, v):
    S = q_nope.shape[1]
    nqb = S // Q_BLOCK
    scale = (MLA_NOPE + MLA_ROPE) ** -0.5
    kpos = jnp.arange(S)

    def block(args):
        i, qn, qr = args
        s = (jnp.einsum('bqhd,bkhd->bhqk', qn, k_nope)
             + jnp.einsum('bqhd,bkd->bhqk', qr, k_rope)) * scale
        qpos = i * Q_BLOCK + jnp.arange(Q_BLOCK)
        p = masked_softmax(s, kpos[None, :] <= qpos[:, None])
        return jnp.einsum('bhqk,bkhd->bqhd', p.astype(v.dtype), v)

    o = lax.map(block, (jnp.arange(nqb), to_blocks(q_nope, nqb), to_blocks(q_rope, nqb)))
    return from_blocks(o)

def hybrid_conv_mla(h, cos, sin, w_in, conv_w, q_norm, kv_norm, w_uq, w_ukv, w_out):
    B, S, _ = h.shape
    z = h @ w_in
    cw = CONV_WIDTH
    u, gate_c, gate_b, cq, ckv, kr = jnp.split(
        z, [cw, 2 * cw, 3 * cw, 3 * cw + Q_LORA, 3 * cw + Q_LORA + KV_LORA], axis=-1)
    y_conv = gate_b * short_conv(gate_c * u, conv_w)
    q = (rms_norm_2(cq, q_norm) @ w_uq).reshape(B, S, MLA_HEADS, MLA_NOPE + MLA_ROPE)
    q_nope, q_rope = q[..., :MLA_NOPE], apply_rope_2(q[..., MLA_NOPE:], cos[:, :, None], sin[:, :, None])
    kv = (rms_norm_2(ckv, kv_norm) @ w_ukv).reshape(B, S, MLA_HEADS, MLA_NOPE + MLA_V)
    k_nope, v = kv[..., :MLA_NOPE], kv[..., MLA_NOPE:]
    k_rope = apply_rope_2(kr, cos, sin)
    y_att = mla_attention(q_nope, q_rope, k_nope, k_rope, v).reshape(B, S, MLA_HEADS * MLA_V)
    return jnp.concatenate([y_conv, y_att], axis=-1) @ w_out

def nsa_attention(h, w_in, cmp_pe, cmp_w1, cmp_w2, gate_b, w_out):
    B, S, _ = h.shape
    G, R, DK = NSA_KV_HEADS, NSA_GROUP, NSA_DK
    dt = h.dtype
    z = h @ w_in
    qd = NSA_HEADS * DK
    q, kv_c, kv_s, kv_w, g = jnp.split(
        z, [qd, qd + NSA_KV_W, qd + 2 * NSA_KV_W, qd + 3 * NSA_KV_W], axis=-1)
    q = q.reshape(B, S, G, R, DK)
    gates = jax.nn.sigmoid(g + gate_b).reshape(B, S, G, R, 3)
    kv_c = kv_c.reshape(B, S, 2, G, DK)
    kv_s = kv_s.reshape(B, S, 2, G, DK)
    kv_w = kv_w.reshape(B, S, 2, G, DK)

    nc = (S - CMP_BLOCK) // CMP_STRIDE + 1
    cidx = jnp.arange(nc)[:, None] * CMP_STRIDE + jnp.arange(CMP_BLOCK)[None, :]

    def compress(t, pe, w1, w2):
        blk = t[:, cidx] + pe[:, None, :]
        blk = jnp.moveaxis(blk, 3, 2).reshape(B, nc, G, CMP_BLOCK * DK)
        return jax.nn.silu(blk @ w1) @ w2

    k_cmp = compress(kv_c[:, :, 0], cmp_pe[0], cmp_w1[0], cmp_w2[0])
    v_cmp = compress(kv_c[:, :, 1], cmp_pe[1], cmp_w1[1], cmp_w2[1])
    cmp_end = jnp.arange(nc) * CMP_STRIDE + CMP_BLOCK - 1

    ns = S // SLC_BLOCK
    n_sel = min(N_SEL, ns)
    cs = jnp.arange(nc)[:, None] * CMP_STRIDE
    ss = jnp.arange(ns)[None, :] * SLC_BLOCK
    overlap = jnp.clip(jnp.minimum(cs + CMP_BLOCK, ss + SLC_BLOCK) - jnp.maximum(cs, ss), 0, None)
    agg = overlap.astype(jnp.float32) / CMP_BLOCK
    blk_idx = jnp.arange(ns)
    k_slc = kv_s[:, :, 0].reshape(B, ns, SLC_BLOCK, G, DK).transpose(0, 3, 1, 2, 4)
    v_slc = kv_s[:, :, 1].reshape(B, ns, SLC_BLOCK, G, DK).transpose(0, 3, 1, 2, 4)
    bi = jnp.arange(B)[:, None, None, None]
    gi = jnp.arange(G)[None, :, None, None]

    pad = ((0, 0), (WINDOW_2, 0), (0, 0), (0, 0))
    k_win = jnp.pad(kv_w[:, :, 0], pad)
    v_win = jnp.pad(kv_w[:, :, 1], pad)
    scale = DK ** -0.5
    nqb = S // Q_BLOCK

    def block(args):
        i, qb, gb = args
        t = i * Q_BLOCK + jnp.arange(Q_BLOCK)
        s_c = jnp.einsum('bqgrd,bngd->bgrqn', qb, k_cmp) * scale
        p_c = masked_softmax(s_c, cmp_end[None, :] <= t[:, None])
        o_c = jnp.einsum('bgrqn,bngd->bqgrd', p_c.astype(dt), v_cmp)
        imp = jnp.einsum('bgrqn,nj->bgqj', p_c, agg)
        cur = t // SLC_BLOCK
        forced = ((blk_idx[None, :] == 0) | (blk_idx[None, :] == cur[:, None])
                  | (blk_idx[None, :] == cur[:, None] - 1))
        causal_blk = blk_idx[None, :] * SLC_BLOCK <= t[:, None]
        imp = jnp.where(forced, FORCE_SCORE, jnp.where(causal_blk, imp, NEG_INF))
        _, sel = lax.top_k(imp, n_sel)
        ks = k_slc[bi, gi, sel].reshape(B, G, Q_BLOCK, n_sel * SLC_BLOCK, DK)
        vs = v_slc[bi, gi, sel].reshape(B, G, Q_BLOCK, n_sel * SLC_BLOCK, DK)
        kpos_s = (sel[..., None] * SLC_BLOCK + jnp.arange(SLC_BLOCK)).reshape(B, G, Q_BLOCK, -1)
        s_s = jnp.einsum('bqgrd,bgqkd->bgrqk', qb, ks) * scale
        p_s = masked_softmax(s_s, kpos_s[:, :, None] <= t[:, None])
        o_s = jnp.einsum('bgrqk,bgqkd->bqgrd', p_s.astype(dt), vs)
        kw = lax.dynamic_slice_in_dim(k_win, i * Q_BLOCK, WINDOW_2 + Q_BLOCK, axis=1)
        vw = lax.dynamic_slice_in_dim(v_win, i * Q_BLOCK, WINDOW_2 + Q_BLOCK, axis=1)
        kpos_w = i * Q_BLOCK - WINDOW_2 + jnp.arange(WINDOW_2 + Q_BLOCK)
        mask_w = ((kpos_w[None, :] <= t[:, None]) & (kpos_w[None, :] > t[:, None] - WINDOW_2)
                  & (kpos_w[None, :] >= 0))
        s_w = jnp.einsum('bqgrd,bkgd->bgrqk', qb, kw) * scale
        p_w = masked_softmax(s_w, mask_w)
        o_w = jnp.einsum('bgrqk,bkgd->bqgrd', p_w.astype(dt), vw)
        return gb[..., 0:1] * o_c + gb[..., 1:2] * o_s + gb[..., 2:3] * o_w

    o = lax.map(block, (jnp.arange(nqb), to_blocks(q, nqb), to_blocks(gates, nqb)))
    return from_blocks(o).reshape(B, S, NSA_HEADS * DK) @ w_out

def second_inputs(seed: int = 0) -> dict:
    key = jax.random.key(seed)
    ks = jax.random.split(key, 24)
    nrm = lambda k, shape, s: jax.random.normal(k, shape, jnp.float32) * s
    D = D_MODEL
    return {
        "x": nrm(ks[0], (BATCH, SEQ, D), 1.0),
        "c": nrm(ks[1], (BATCH, D), 1.0),
        "positions": (jnp.arange(SEQ, dtype=jnp.int32)[None, :]
                      + jax.random.randint(ks[2], (BATCH, 1), 0, 1024, dtype=jnp.int32)),
        "ada_w": nrm(ks[3], (DEPTH_2, D, N_ADA * D), 0.5 * D ** -0.5),
        "ada_b": nrm(ks[4], (DEPTH_2, N_ADA * D), 0.02),
        "norm_g": 1.0 + nrm(ks[5], (DEPTH_2, 3, D), 0.02),
        "final_g": 1.0 + nrm(ks[6], (D,), 0.02),
        "ff_w13": nrm(ks[7], (DEPTH_2, 2, D, 2 * D_FF_2), D ** -0.5),
        "ff_w2": nrm(ks[8], (DEPTH_2, 2, D_FF_2, D), D_FF_2 ** -0.5),
        "hy_w_in": nrm(ks[9], (N_EVEN, D, HY_IN), D ** -0.5),
        "hy_conv_w": nrm(ks[10], (N_EVEN, CONV_TAPS, CONV_WIDTH), CONV_TAPS ** -0.5),
        "hy_q_norm": 1.0 + nrm(ks[11], (N_EVEN, Q_LORA), 0.02),
        "hy_kv_norm": 1.0 + nrm(ks[12], (N_EVEN, KV_LORA), 0.02),
        "hy_w_uq": nrm(ks[13], (N_EVEN, Q_LORA, MLA_HEADS * (MLA_NOPE + MLA_ROPE)), Q_LORA ** -0.5),
        "hy_w_ukv": nrm(ks[14], (N_EVEN, KV_LORA, MLA_HEADS * (MLA_NOPE + MLA_V)), KV_LORA ** -0.5),
        "hy_w_out": nrm(ks[15], (N_EVEN, HY_MIX, D), HY_MIX ** -0.5),
        "nsa_w_in": nrm(ks[16], (N_ODD, D, NSA_IN), D ** -0.5),
        "nsa_cmp_pe": nrm(ks[17], (N_ODD, 2, CMP_BLOCK, NSA_DK), 0.1),
        "nsa_cmp_w1": nrm(ks[18], (N_ODD, 2, CMP_BLOCK * NSA_DK, CMP_HID), (CMP_BLOCK * NSA_DK) ** -0.5),
        "nsa_cmp_w2": nrm(ks[19], (N_ODD, 2, CMP_HID, NSA_DK), CMP_HID ** -0.5),
        "nsa_gate_b": nrm(ks[20], (N_ODD, 3 * NSA_HEADS), 0.1),
        "nsa_w_out": nrm(ks[21], (N_ODD, NSA_HEADS * NSA_DK, D), (NSA_HEADS * NSA_DK) ** -0.5),
    }

def second_block(x, c, positions, ada_w, ada_b, norm_g, final_g, ff_w13, ff_w2,
              hy_w_in, hy_conv_w, hy_q_norm, hy_kv_norm, hy_w_uq, hy_w_ukv, hy_w_out,
              nsa_w_in, nsa_cmp_pe, nsa_cmp_w1, nsa_cmp_w2, nsa_gate_b, nsa_w_out):
    cos, sin = rope_tables_2(positions)
    c_act = jax.nn.silu(c)
    for l in range(DEPTH_2):
        mod = c_act @ ada_w[l] + ada_b[l]
        sh1, sc1, g1, sh2, sc2, g2, sh3, sc3, g3 = jnp.split(mod, N_ADA, axis=-1)
        h = modulate(x, norm_g[l, 0], sh1, sc1)
        x = x + 0.5 * g1[:, None] * swiglu(h, ff_w13[l, 0], ff_w2[l, 0])
        h = modulate(x, norm_g[l, 1], sh2, sc2)
        m = l // 2
        if l % 2 == 0:
            y = hybrid_conv_mla(h, cos, sin, hy_w_in[m], hy_conv_w[m], hy_q_norm[m],
                                hy_kv_norm[m], hy_w_uq[m], hy_w_ukv[m], hy_w_out[m])
        else:
            y = nsa_attention(h, nsa_w_in[m], nsa_cmp_pe[m], nsa_cmp_w1[m], nsa_cmp_w2[m],
                              nsa_gate_b[m], nsa_w_out[m])
        x = x + g2[:, None] * y
        h = modulate(x, norm_g[l, 2], sh3, sc3)
        x = x + 0.5 * g3[:, None] * swiglu(h, ff_w13[l, 1], ff_w2[l, 1])
    return rms_norm_2(x, final_g)


def setup_inputs(seed=0):
    out = dict(first_inputs(seed))
    for name, value in second_inputs(seed + 1).items():
        if name != "x":
            out[name + "_2"] = value
    return out


def reference(
    x, mem, positions, g_mix, w_in, sinks, lambda_q1, lambda_k1, lambda_q2, lambda_k2, g_diff,
    w_out, g_cross, g_mem, w_cq, w_ckv, w_co, g_mlp, w_up, w_down, g_final, c_2, positions_2,
    ada_w_2, ada_b_2, norm_g_2, final_g_2, ff_w13_2, ff_w2_2, hy_w_in_2, hy_conv_w_2,
    hy_q_norm_2, hy_kv_norm_2, hy_w_uq_2, hy_w_ukv_2, hy_w_out_2, nsa_w_in_2, nsa_cmp_pe_2,
    nsa_cmp_w1_2, nsa_cmp_w2_2, nsa_gate_b_2, nsa_w_out_2,
):
    x = first_block(
        x, mem, positions, g_mix, w_in, sinks, lambda_q1, lambda_k1, lambda_q2, lambda_k2,
        g_diff, w_out, g_cross, g_mem, w_cq, w_ckv, w_co, g_mlp, w_up, w_down, g_final,
    )
    return second_block(
        x, c_2, positions_2, ada_w_2, ada_b_2, norm_g_2, final_g_2, ff_w13_2, ff_w2_2,
        hy_w_in_2, hy_conv_w_2, hy_q_norm_2, hy_kv_norm_2, hy_w_uq_2, hy_w_ukv_2, hy_w_out_2,
        nsa_w_in_2, nsa_cmp_pe_2, nsa_cmp_w1_2, nsa_cmp_w2_2, nsa_gate_b_2, nsa_w_out_2,
    )


_drawn_inputs = setup_inputs


def setup_inputs(seed=0):
    import zlib

    import numpy as np

    out = dict(_drawn_inputs(seed))
    spreads = {}
    factors = {'g_mix': 3.006,
     'sinks': 7.919,
     'lambda_q1': 3.711,
     'lambda_k2': 8.0,
     'g_diff': 4.324,
     'g_cross': 8.0,
     'g_mem': 8.0,
     'g_mlp': 3.185,
     'g_final': 2.747,
     'norm_g_2': 5.022,
     'final_g_2': 8.43,
     'hy_q_norm_2': 60.353,
     'hy_kv_norm_2': 64.0,
     'nsa_cmp_pe_2': 57.976,
     'nsa_gate_b_2': 64.0,
     'nsa_cmp_w1_2': 3.115}
    for name, (base, spread) in spreads.items():
        noise = np.random.default_rng([zlib.crc32(name.encode()), seed]).standard_normal(out[name].shape)
        drawn = base * np.exp(spread * noise) if base else spread * noise
        out[name] = __import__('jax').numpy.asarray(drawn.astype(out[name].dtype))
    for name, factor in factors.items():
        out[name] = (out[name] * factor).astype(out[name].dtype)
    return out
```

```python
import math
from contextlib import ExitStack

import numpy as np

import concourse.bass as bass
from concourse import mybir

F32 = mybir.dt.float32
F32R = mybir.dt.float32r
I32 = mybir.dt.int32
ALU = mybir.AluOpType
ACT = mybir.ActivationFunctionType
AX = mybir.AxisListType

P = 128
S = 256
NT = S // P
D = 1024
KC = D // P
HD = 64
ROPE_HALF, ROPE_HALF_2 = 32, 16
F1, F2 = 4 * D, 2816
HB1, HB2 = 512, 256
N1, N2 = F1 // HB1, F2 // HB2
CONV = 512
UNIT = 2048
RING = 3
LEAD = RING - 1
ADA_W = 256
ADA_N = 9 * D // ADA_W
NEG = -1e30
MAGIC = 1.5 * 2.0 ** 23
TWO_PI = 2.0 * math.pi
C1 = 6.28125
C2 = float(np.floor((TWO_PI - C1) * 2.0 ** 21) / 2.0 ** 21)
C3 = TWO_PI - C1 - C2
PI_LOW = 3.1415925
LAM_INIT = 0.8 - 0.6 * math.exp(0.0)
SWA_SCALE = HD ** -0.5
CROSS_SCALE = 256 ** -0.5
MLA_SCALE = 96 ** -0.5
NC = (S - 32) // 16 + 1
G_MIX, G_CROSS, G_MEM, G_MLP, NORM_G, C_COL, Q_NORM, KV_NORM, CONV_W = 0, 8, 16, 24, 32, 80, 88, 90, 91
N_PRM = CONV_W + 12


class Turns:

    def __init__(self):
        self.who = []

    def add(self, who):
        self.who.append(who)
        return len(self.who) - 1

    def emptied(self, engine, n):
        return sum(engine in w for w in self.who[:n + 1])


def at(j, f):
    if isinstance(j, int):
        return f(j)
    step = f(3) - f(2)
    assert f(4) - f(3) == step
    return f(2) if step == 0 else j * step + (f(2) - 2 * step)


class Plan:

    def __init__(self, A):
        self.A = A
        self.T, self.U = Turns(), Turns()
        self.units = []
        self.used = []
        self.w_used = 0
        self.stages = []
        self.groups = []
        self.norms = 0
        self.x_ready = 0
        self.x_event = ("x", 0)
        self.norm_rounds = 0
        self.norm_i = 0
        self.mixed = 0
        self.ada_todo = []
        self.ada_last = [None] * 2
        self.last_fill = None
        self.n_gates = 0
        self.r_done = 0
        self.keys_turned = []

    def unit(self, ap, a, b, transfers=1):
        self.units.append((ap, a, b, transfers))
        self.used.append(None)
        return len(self.units) - 1

    def mark_w(self, u):
        self.w_used += 1
        self.used[u] = ("w", self.w_used)

    def stage(self, kind, **kw):
        kw["kind"] = kind
        self.stages.append(kw)
        return kw

    def rounds(self, n, who):
        return [self.T.add(w) for w in (who if isinstance(who, (list, tuple)) else [who] * n)]

    def linear(self, w, K, N, dst, name, chunk0=0, gate=None, side=None):
        kcs = K // P
        out = []
        wv = w.rearrange("(k p) n -> p k n", p=P)
        for c0 in range(0, N, 512):
            w_ = min(512, N - c0)
            per = kcs if kcs * w_ <= UNIT else 4
            fills = [self.U.add("D" if dst == "x" else "A") for _ in range(NT)]
            parts = []
            for k0 in range(0, kcs, per):
                u = self.unit(lambda j, k0=k0, c0=c0, w_=w_, per=per: wv[:, k0:k0 + per, c0:c0 + w_], per, w_)
                parts.append((u, k0, per))
                if k0 + per < kcs:
                    self.mark_w(u)
            self.used[parts[-1][0]] = ("u", fills[-1] + 1)
            out.append((c0, w_, parts, fills))
        left = list(self.left)
        if dst == "x":
            if gate:
                self.x_ready += NT
                self.x_event = ("x", self.x_ready)
            else:
                self.x_event = ("U", fills[-1])
        self.last_fill = fills[-1]
        return self.stage("linear", blocks=out, dst=dst, chunk0=chunk0, name=name, gate=gate, left=left, side=side)

    def norm(self, src, width, scale, shift=None, chunk0=0, eps=1e-6):
        n = self.norms
        self.norms += 1
        r = self.rounds((width // P + 1) // 2, "D")
        lo0 = self.norm_rounds
        self.norm_i += 1
        self.norm_rounds += len(r)
        self.left = [("norm", self.norm_rounds)]
        return self.stage("norm", n=n, src=src, width=width, scale=scale, shift=shift, chunk0=chunk0, eps=eps,
                          rounds=r, lo0=lo0, i=self.norm_i, need=self.x_event if src == "x" else ("U", self.last_fill))

    def next_gate(self):
        self.n_gates += 1
        return self.n_gates

    def turned(self, kind, n, who, **kw):
        r = self.rounds(n, who)
        self.keys_turned = r[-2:]
        return self.stage(kind, rounds=r, after=self.last_fill, **kw)

    def o_turn(self, c0, c1, ready):
        r = self.rounds((c1 - c0) // 2, "AD")
        self.left = [("T", r[-1])] + ([("conv", 1)] if c0 else [])
        self.stage("o_T", chunk0=c0, rounds=r, ready=ready, fill=self.groups[-1]["fill"])

    def ada_unit(self, mods):
        layer, i = self.ada_todo.pop(0)
        v = self.A["ada_w_2"][layer].rearrange("(k p) n -> p k n", p=P)
        first, per = i - len(mods), None
        u = self.unit(lambda c: v[:, :, bass.ds(c, ADA_W)], KC, ADA_W)
        t = self.T.add("A")
        self.used[u] = ("t", t + 1)
        mods.append(dict(layer=layer, i=i, u=u, t=t, pos=len(mods)))
        return ("ada", mods[-1])

    def ada_cols(self, m):
        m["tc"] = self.T.add("D")
        self.ada_last[m["layer"]] = m["tc"]
        return ("ada_cols", m)

    def mlp(self, kind, w_up, w_down, n, hb, gate, name, ada=0):
        up_v = w_up.rearrange("(k p) n -> p k n", p=P)
        down_v = w_down.rearrange("(k p) n -> p k n", p=P)
        steps = []
        nd = hb // 256

        def up_unit(half):
            rows = up_v[:, 4 * half:4 * half + 4, :]
            if kind == "relu2":
                return self.unit(lambda j: rows[:, :, bass.ds(j * hb, hb)], 4, hb)
            both = rows.rearrange("p a (s f) -> p a s f", s=2)
            return self.unit(lambda j: both[:, :, :, bass.ds(j * hb, hb)], 4, 512, 2)

        for j in range(n + 1):
            e, mods = [], []

            def slot(most=1):
                for _ in range(most):
                    if j < n and len(mods) < ada and self.ada_todo:
                        e.append(self.ada_unit(mods))
                        if len(mods) > 1:
                            e.append(self.ada_cols(mods[-2]))

            fills = [self.U.add("D"), self.U.add("D")] if j < n else None
            if j > 0:
                e.append(("hidT", dict(tt=0, t=self.T.add("AD"), fill=steps[-1][0][1])))
            if j < n:
                u = up_unit(0)
                self.mark_w(u)
                e.append(("up", dict(half=0, u=u, fills=fills)))
                slot(2 if ada > 3 else 1)
            if j > 0:
                t_last = self.T.add("AD")
                e.append(("hidT", dict(tt=1, t=t_last, fill=steps[-1][0][1])))
            if j < n:
                u = up_unit(1)
                self.used[u] = ("u", fills[1] + 1)
                e.append(("up", dict(half=1, u=u, fills=fills)))
                slot()
            if j > 0:
                for k in range(nd):
                    u = self.unit(lambda j, k=k: down_v[:, bass.ds((j - 1) * (2 * nd) + 2 * k, 2), :], 2, D)
                    self.mark_w(u)
                    e.append(("down", dict(half=k, u=u, t=t_last)))
                    if k < nd - 1:
                        slot()
            slot(8)
            if mods:
                e.append(self.ada_cols(mods[-1]))
            steps.append([("fills", fills)] + e)
        self.x_ready += NT
        self.x_event = ("x", self.x_ready)
        self.r_done += NT * n
        steps = [s_[1:] for s_ in steps]
        lo = hi = 2
        while hi < n and [e[0] for e in steps[hi]] == [e[0] for e in steps[2]]:
            hi += 1
        hi -= 1
        return self.stage("mlp", mlp=kind, steps=steps, n=n, hb=hb, gate=gate, name=name, lo=lo, hi=hi,
                          acc_ready=self.w_used, left=list(self.left), r0=self.r_done - NT * n)


def make_plan(A):
    p = Plan(A)
    p.ada_todo = [(l, i) for l in range(2) for i in range(ADA_N)]
    p.stage("params", rounds=p.rounds(2, "D"))
    p.norm("x", D, ("prm", G_MIX), eps=1e-5)
    p.linear(A["w_in"][0], D, 2304, "z", "w_in")
    after_in = p.last_fill
    p.norm("mem", D, ("prm", G_MEM), eps=1e-5)
    p.linear(A["w_ckv"][0], D, 2 * D, "zc", "w_ckv", side=after_in)
    p.turned("qk1", 7, ["A", "D", "A", "D", "D", "A", "D"])
    p.stage("attend", groups=attention_groups(p, "first"), which="first", turned=list(p.keys_turned))
    p.stage("diff_norm", fill=p.groups[-1]["fill"])
    p.o_turn(0, 8, "diff")
    p.linear(A["w_out"][0], D, D, "x", "w_out")
    p.norm("x", D, ("prm", G_CROSS), eps=1e-5)
    p.linear(A["w_cq"][0], D, D, "z", "w_cq")
    p.turned("qk_cross", 8, ["A", "D"] * 4)
    p.stage("attend", groups=attention_groups(p, "cross"), which="cross", turned=list(p.keys_turned))
    p.o_turn(0, 8, "U")
    p.linear(A["w_co"][0], D, D, "x", "w_co")
    p.norm("x", D, ("prm", G_MLP), eps=1e-5)
    p.mlp("relu2", A["w_up"][0], A["w_down"][0], N1, HB1, None, "mlp", ada=5)
    p.stage("scale_x", n=p.norms, need=p.x_event, turn=len(p.T.who), eps=1e-5)
    p.norms += 1
    p.x_ready += NT
    p.x_event = ("x", p.x_ready)
    for layer in range(2):
        p.stage("mod_cols", layer=layer, last=p.ada_last[layer])
        p.stage("gate", need=p.x_event, diag=p.next_gate(), layer=layer, m=2, factor=0.5, rounds=p.rounds(2, "D"))
        p.norm("x", D, ("mod", 0), (layer, 0))
        p.mlp("swiglu", A["ff_w13_2"][layer, 0], A["ff_w2_2"][layer, 0], N2, HB2, True, f"ff{layer}0",
              ada=3 if layer == 0 else 0)
        p.stage("gate", need=p.x_event, diag=p.next_gate(), layer=layer, m=5, factor=1.0, rounds=p.rounds(2, "D"))
        p.norm("x", D, ("mod", 1), (layer, 3))
        if layer == 0:
            p.linear(A["hy_w_in_2"][0], D, 1952, "z", "hy_in")
            p.turned("conv_T", 6, ["A", "D"] * 3)
            p.stage("conv", turned=list(p.keys_turned))
            p.norm("cq", 256, ("prm", Q_NORM), chunk0=4)
            p.norm("ckv", 128, ("prm", KV_NORM), chunk0=6)
            p.linear(A["hy_w_uq_2"][0], 256, 768, "z", "uq", chunk0=4)
            p.linear(A["hy_w_ukv_2"][0], 128, 1024, "z768", "ukv", chunk0=6)
            p.stage("mla_pack", after=p.last_fill)
            p.turned("qk_mla", 8, ["A", "D"] * 4)
            p.stage("attend", groups=attention_groups(p, "mla"), which="mla", turned=list(p.keys_turned))
            p.o_turn(4, 8, "U")
            p.linear(A["hy_w_out_2"][0], D, D, "x", "hy_out", gate=True)
        else:
            p.linear(A["nsa_w_in_2"][0], D, 1840, "z", "nsa_in")
            qk = p.turned("qk_nsa", 7, ["A", "D", "A", "D", "A", "D", "A"])
            us = []
            for kv in range(2):
                w1 = A["nsa_cmp_w1_2"][0, kv].rearrange("(c p) n -> p c n", p=P)
                us.append(p.unit(lambda j, w1=w1: w1, 16, P))
            r = p.rounds(4, ["A", "D", "A", "D"])
            for kv in range(2):
                p.used[us[kv]] = ("t", r[2 * kv] + 1)
            p.stage("compress", units=us, rounds=r, after=p.last_fill, turned=qk["rounds"])
            p.keys_turned += r
            p.stage("attend", groups=attention_groups(p, "nsa"), which="nsa", turned=list(p.keys_turned))
            p.o_turn(0, 8, "nsa")
            p.linear(A["nsa_w_out_2"][0], D, D, "x", "nsa_out", gate=True)
        p.stage("gate", need=p.x_event, diag=p.next_gate(), layer=layer, m=8, factor=0.5, rounds=p.rounds(2, "D"))
        p.norm("x", D, ("mod", 2), (layer, 6))
        p.mlp("swiglu", A["ff_w13_2"][layer, 1], A["ff_w2_2"][layer, 1], N2, HB2, True, f"ff{layer}1",
              ada=3 if layer == 0 else 0)
    p.stage("scale_x", n=p.norms, need=p.x_event, turn=len(p.T.who), eps=1e-6)
    p.norms += 1
    assert not p.ada_todo
    return p


def attention_groups(p, which):
    spec = []
    if which == "first":
        for t in range(NT):
            spec += [dict(kind="swa", t=t, h0=h, nh=4) for h in (0, 4)]
        for t in range(NT):
            spec += [dict(kind="diff", t=t, h0=h, nh=4) for h in (0, 2)]
    elif which == "cross":
        spec = [dict(kind="cross", t=t, h0=h, nh=2) for t in range(NT) for h in (0, 2)]
    elif which == "mla":
        spec = [dict(kind="mla", t=t, h0=h, nh=4) for t in range(NT) for h in (0, 4)]
    else:
        for br in (0, 1):
            spec += [dict(kind="nsa", br=br, t=t, h0=h, nh=4) for t in range(NT) for h in (0, 4, 8, 12)]
        spec += [dict(kind="cmp", t=t, h0=h, nh=8) for t in range(NT) for h in (0, 8)]
    first = len(p.groups)
    for i, g in enumerate(spec):
        g["g"] = first + i
        g["nk"] = S if g["kind"] == "cross" else (NC if g["kind"] == "cmp" else (g["t"] + 1) * P)
        nkc = 1 if g["kind"] == "cmp" else g["nk"] // P
        heads = {"diff": [0, 2], "cmp": [0, 1]}.get(g["kind"], list(range(g["nh"])))
        g["turn"] = [(h, kc) for h in heads for kc in range(nkc)]
        g["nkc"] = nkc
    p.groups += spec
    for i in range(len(spec) + 2):
        if 1 <= i <= len(spec):
            g = spec[i - 1]
            n = (len(g["turn"]) + 3) // 4
            g["rounds"] = [p.T.add("AD"[k] if n == 2 else "D" if g["kind"] == "diff" else "A") for k in range(n)]
            if g["kind"] in ("diff", "cmp"):
                p.mixed += 1
                g["mixed"] = p.mixed
        if i >= 2:
            spec[i - 2]["fill"] = p.U.add("D")
    return spec


def build(nc, A, out):
    p = make_plan(A)
    ctx = ExitStack()
    with ctx:
        def sb(name, shape, dt=F32):
            return ctx.enter_context(nc.sbuf_tensor(name, [P] + shape, dt))

        def sem(name):
            return ctx.enter_context(nc.semaphore(name))

        raw = sb("raw", [RING, UNIT])
        whi = sb("whi", [RING, UNIT], F32R)
        wlo = sb("wlo", [RING, UNIT], F32R)
        x = sb("x", [NT, D])
        xn = sb("xn", [NT, D])
        aT = sb("aT", [KC, S], F32R)
        aTl = sb("aTl", [KC, S], F32R)
        hT = sb("hT", [4, S], F32R)
        hTl = sb("hTl", [4, S], F32R)
        z = sb("z", [NT, 2304])
        zc = sb("zc", [NT, 2048])
        qT = sb("qT", [8, S])
        kz = sb("kz", [12, S])
        sp = sb("sp", [2, 1024])
        pT = sb("pT", [2, 8, P])
        tmp = sb("tmp", [2, 512])
        gbc = sb("gbc", [D])
        row = sb("row", [2, ADA_W])
        ident = sb("ident", [P])
        ones = sb("ones", [P])
        pick = sb("pick", [2])
        causal = sb("causal", [S])
        band = sb("band", [S])
        cmask = sb("cmask", [NT, NC])
        cneg = sb("cneg", [NT, NC])
        prm_rows = sb("prm_rows", [P])
        ab_rows = sb("ab_rows", [2, P])
        pe_rows = sb("pe_rows", [P])
        prm = sb("prm", [N_PRM])
        prm2 = sb("prm2", [176])
        mod = sb("mod", [2, 72])
        msc = sb("msc", [3, 8])
        c_hl = sb("c_hl", [2 * KC + P], F32R)
        cact = sb("cact", [2, KC])
        lamb = sb("lamb", [4, HD])
        lam2 = sb("lam2", [2, HD])
        lam = sb("lam", [4])
        sink = sb("sink", [8])
        nsink = sb("nsink", [8])
        gdiff = sb("gdiff", [P])
        gateb = sb("gateb", [48])
        gates = sb("gates", [NT, 48])
        pos = sb("pos", [2, NT], I32)
        posf = sb("posf", [2, NT])
        freq = sb("freq", [48])
        ang = sb("ang", [2, NT, 48])
        kk = sb("kk", [2, NT, 48])
        trig = sb("trig", [2, NT, 48])
        ss = sb("ss", [p.norms, NT])
        ms = sb("ms", [2, NT])
        rstd = sb("rstd", [p.norms, NT])
        mhalf = sb("mhalf", [8])
        dss = sb("dss", [3, 8])
        rmax = sb("rmax", [2, 8])
        negm = sb("negm", [2, 8])
        dsk = sb("dsk", [2, 2, 4])
        sums = sb("sums", [2, 8])
        rinv = sb("rinv", [2, 8])
        rg = sb("rg", [2, 8])
        w2s = sb("w2s", [2, P])
        hidc = sb("hidc", [2, 32])
        hbias = sb("hbias", [2])
        kcz = sb("kcz", [2, 2 * NC])
        vcb = kz[:, 10:12, :]
        R, Rl, Rf = [v.rearrange("p (a b) -> p a b", b=32) for v in
                     (hT[:, 0:2, :].rearrange("p a b -> p (a b)"), hTl[:, 0:2, :].rearrange("p a b -> p (a b)"),
                      tmp[:, 0, :])]

        ps = ctx.enter_context(nc.psum_tensor("ps", [P, 8, 512], F32))
        ACC = ps[:, 0:4, :]

        def ubank(n):
            return ps[:, 4 + n % 2, :]

        def tbank(n):
            return ps[:, 6 + n % 2, :]

        def sbank(g):
            return ps[:, 2 * (g % 2):2 * (g % 2) + 2, :].rearrange("p a b -> p (a b)")

        w_raw = [sem(f"w_raw{i}") for i in range(RING)]
        w_hi, w_lo, w_used = sem("w_hi"), sem("w_lo"), sem("w_used")
        t_ready, t_act, t_dve = sem("t_ready"), sem("t_act"), sem("t_dve")
        u_ready, u_act, u_dve = sem("u_ready"), sem("u_act"), sem("u_dve")
        x_loaded, mem_loaded, small_loaded = sem("x_loaded"), sem("mem_loaded"), sem("small_loaded")
        prm_loaded, gain_loaded = sem("prm_loaded"), sem("gain_loaded")
        consts_set = sem("consts_set")
        cact_ready, cz_ready, trig_ready, ang_ready = sem("cact_ready"), sem("cz_ready"), sem("trig_ready"), sem("ang_ready")
        lam_sums, lam_exps = sem("lam_sums"), sem("lam_exps")
        ss_act, ss_dve, rstd_ready = sem("ss_act"), sem("ss_dve"), sem("rstd_ready")
        xn_act, xn_dve = sem("xn_act"), sem("xn_dve")
        nt_ready, nhi_ready, nlo_ready = sem("nt_ready"), sem("nhi_ready"), sem("nlo_ready")
        x_ready = sem("x_ready")
        z_roped, v_done, a_done, g_done = sem("z_roped"), sem("vector_steps"), sem("scalar_steps"), sem("pool_steps")
        s_ready, s_taken, m_ready = sem("scores_ready"), sem("scores_taken"), sem("max_ready")
        p_ready, p_mixed, o_stored = sem("probs_ready"), sem("probs_mixed"), sem("o_stored")
        h_ready, r_ready = sem("hidden_ready"), sem("act_part_ready")
        dn_ss, dn_r, dn_done = sem("diff_ss"), sem("diff_rstd"), sem("diff_normed")
        diag_ready, mods_ready = sem("diag_ready"), sem("mods_ready")
        conv_y, conv_hi = sem("conv_y"), sem("conv_hi")
        conv_done, packed, kz_zero = sem("conv_done"), sem("packed"), sem("kz_zero")
        cmp_r, cmp_rhi, cmp_rlo, cmp_b, cmp_h, cmp_kv = (sem("cmp_rows"), sem("cmp_rows_hi"), sem("cmp_rows_lo"),
                                                         sem("cmp_bias"), sem("cmp_hidden"), sem("cmp_kv"))
        gl_ready, gates_ready, out_ready, stored = sem("gate_logits"), sem("gates_ready"), sem("out_ready"), sem("stored")

        T, U = p.T, p.U
        last_emptied = {"first": 0}

        def wait_used(eng, u, j):
            kind = p.used[u(j if isinstance(j, int) else 2)][0]
            eng.wait_ge({"w": w_used, "u": u_ready, "t": t_ready}[kind], at(j, lambda j: p.used[u(j)][1]))

        def wait_emptied(eng, turns, n, j=0):
            n_ = n(j if isinstance(j, int) else 2)
            for who, s in (("A", t_act if turns is T else u_act), ("D", t_dve if turns is T else u_dve)):
                if who in turns.who[n_]:
                    eng.wait_ge(s, at(j, lambda j: turns.emptied(who, n(j))))

        def wait_free(eng, turns, n, j=0):
            if not isinstance(j, int) or n(j) >= 2:
                wait_emptied(eng, turns, lambda j: n(j) - 2, j)

        def wait_x(eng, need):
            if need[0] == "U":
                wait_emptied(eng, U, lambda j: need[1])
            elif need[1] == 0:
                eng.wait_ge(x_loaded, 16)
            else:
                eng.wait_ge(x_ready, need[1])

        def run_steps(eng, st, body):
            for j in range(st["lo"]):
                body(j)
            with eng.Fori(st["lo"], st["hi"]) as j:
                body(j)
            for j in range(st["hi"], st["n"] + 1):
                body(j)

        def events(st, j):
            j_ = j if isinstance(j, int) else st["lo"]
            for k, (what, e) in enumerate(st["steps"][j_]):
                yield what, e, (lambda jj, k=k: st["steps"][jj][k][1])

        def src_of(st):
            return {"x": x[:, :, :], "mem": zc[:, :, 0:D], "cq": z[:, :, 1536:1792], "ckv": z[:, :, 1792:1920]}[st["src"]]

        def norm_dst(st):
            return {"cq": xn[:, :, 0:256], "ckv": xn[:, :, 256:384]}.get(st["src"], xn[:, :, :])

        zcf = zc[:, :, :].rearrange("p t (a b) -> p (t a) b", b=S)
        kfull = zcf[:, 0:6, :].rearrange("p a b -> p (a b)").rearrange("p (t n) -> p t n", t=NT)

        def hid(tt):
            return sp[:, tt, 0:512]

        def part(tt):
            return sp[:, tt, 512:1024]

        def flat(t):
            t = t if len(t.shape) < 4 else t[:, :, :, :]
            return t.rearrange("p k t f -> p (k t f)") if len(t.shape) == 4 else t.rearrange("p t f -> p (t f)")

        def view(bank, like):
            return bank.rearrange("p (a b) -> p a b", b=like.shape[-1]) if len(like.shape) == 3 else bank

        def wait_src(eng, st):
            if st["src"] == "mem":
                eng.wait_ge(mem_loaded, 16)
            else:
                wait_x(eng, st["need"])

        def transposes(st):
            items, dst = [], []

            def pair(src, c0, to):
                items.append([(src[:, tt, c0 + k * P:c0 + (k + 1) * P], k * S + tt * P, P)
                              for k in range(2) for tt in range(NT)])
                if to is not None:
                    dst.append([(to, 0, P, 0, 512)])

            def shared_keys(c0, k0):
                items.append([(z[:, tt, c0:c0 + P], tt * P, P) for tt in range(NT)])
                dst.append([(kz[HD * (i % 2):HD * (i % 2) + HD, k0 + i:k0 + i + 1, :], HD * (i // 2), HD, 0, S)
                            for i in range(4)])

            kind = st["kind"]
            if kind == "qk1":
                for r in range(4):
                    pair(z, 256 * r + (0 if r < 2 else 256), qT[:, 2 * r:2 * r + 2, :])
                shared_keys(512, 0)
                for r in range(2):
                    pair(z, 1280 + 256 * r, None)
                    dst.append([(kz[HD * c:HD * c + HD, 4 + 4 * r + c:4 + 4 * r + c + 3:2, :], HD * c, HD, 0, 512)
                                for c in range(2)])
            elif kind == "qk_cross":
                for r in range(4):
                    pair(z, 256 * r, qT[:, 2 * r:2 * r + 2, :])
                for r in range(4):
                    pair(zc, 256 * r, kz[:, 2 * r:2 * r + 2, :])
            elif kind == "conv_T":
                for r in range(6):
                    pair(z, 256 * r, zcf[:, 2 * r:2 * r + 2, :])
            elif kind == "qk_mla":
                for src, to in ((z, qT), (kfull, kz)):
                    for r in range(4):
                        items.append([(src[:, tt, (2 * r + k) * 96:(2 * r + k + 1) * 96], k * S + tt * P, P)
                                      for k in range(2) for tt in range(NT)])
                        dst.append([(to[0:96, 2 * r:2 * r + 2, :], 0, 96, 0, 512)])
            elif kind == "qk_nsa":
                for r in range(4):
                    pair(z, 256 * r, qT[:, 2 * r:2 * r + 2, :])
                pair(z, 1024, kz[:, 8:10, :])
                shared_keys(1280, 0)
                shared_keys(1536, 4)
            elif kind == "o_T":
                for r in range(len(st["rounds"])):
                    pair(xn, 256 * r + P * st["chunk0"], None)
            return items, dst

        arrived, count = [], [0] * RING
        for u, (_, _, _, transfers) in enumerate(p.units):
            count[u % RING] += 16 * transfers
            arrived.append(count[u % RING])

        def split_hi(act, u, j=0):
            if isinstance(j, int) and u(j) >= len(p.units):
                return
            slot = u(j if isinstance(j, int) else 2) % RING
            act.wait_ge(w_raw[slot], at(j, lambda j: arrived[u(j)]))
            if not isinstance(j, int) or u(j) >= RING:
                wait_used(act, lambda j: u(j) - RING, j)
            act.activation(whi[:, slot, :], raw[:, slot, :], ACT.Copy).then_inc(w_hi, 1)

        def split_lo(dve, u, j=0):
            if isinstance(j, int) and u(j) >= len(p.units):
                return
            slot = u(j if isinstance(j, int) else 2) % RING
            dve.wait_ge(w_hi, at(j, lambda j: u(j) + 1))
            dve.tensor_tensor(wlo[:, slot, :], raw[:, slot, :], whi[:, slot, :].bitcast(F32),
                              ALU.subtract).then_inc(w_lo, 1)

        N_PRM_DMA, N_SMALL, N_CONST = 12, 15, 17

        block = ctx.enter_context(nc.Block())

        @block.sync
        def _(sy):
            sy.dma_start(x[:, :, :], A["x"][0].rearrange("(t p) d -> p t d", p=P)).then_inc(x_loaded, 16)

            def load(u, arg, j=0):
                u_ = u(j if isinstance(j, int) else 2)
                src, a, b, _ = p.units[u_]
                slot = u_ % RING
                if not isinstance(j, int) or u_ >= RING:
                    sy.wait_ge(w_lo, at(j, lambda j: u(j) - RING + 1))
                dst = raw[:, slot, 0:a * b].rearrange("p (a b) -> p a b", a=a)
                ap = src(arg)
                if len(ap.shape) == 4:
                    dst = dst.rearrange("p a (s f) -> p a s f", s=2)
                    for s in range(2):
                        sy.dma_start(dst[:, :, s, :], ap[:, :, s, :]).then_inc(w_raw[slot], 16)
                else:
                    sy.dma_start(dst, ap).then_inc(w_raw[slot], 16)

            for st in p.stages:
                if st["kind"] == "linear":
                    for _, _, parts, _ in st["blocks"]:
                        for u, _, _ in parts:
                            load(lambda j: u, None)
                elif st["kind"] == "compress":
                    for u in st["units"]:
                        load(lambda j: u, None)
                elif st["kind"] == "mlp":
                    def body(j):
                        for what, e, get in events(st, j):
                            if what in ("up", "down"):
                                load(lambda j: get(j)["u"], j, j)
                            elif what == "ada":
                                load(lambda j: get(j)["u"], at(j, lambda j: get(j)["i"] * ADA_W), j)
                    run_steps(sy, st, body)
            for tt in range(NT):
                sy.wait_ge(out_ready, tt + 1)
                sy.dma_start(out[0].rearrange("(t p) d -> p t d", p=P)[:, tt], xn[:, tt]).then_inc(stored, 16)
            sy.wait_ge(stored, 16 * NT)

        @block.tensor
        def _(pe):
            def three(out_ap, hi, lo, w, wl, start, stop):
                pe.matmul(out_ap, hi, w, start=start, stop=False)
                pe.matmul(out_ap, lo, w, start=False, stop=False)
                return pe.matmul(out_ap, hi, wl, start=False, stop=stop)

            def turn(t, items, rows=P):
                wait_free(pe, T, lambda j: t)
                for k, (src, col, kp) in enumerate(items):
                    m = src.shape[-1]
                    last = pe.transpose(tbank(t)[0:m, col:col + kp], src, ident[0:kp, 0:kp])
                last.then_inc(t_ready, 1)

            def use(u, j=1):
                pe.wait_ge(w_lo, at(j, lambda j: u(j) + 1))

            def params(st):
                pe.wait_ge(prm_loaded, 16 * N_PRM_DMA)
                pe.wait_ge(consts_set, N_CONST)
                turn(st["rounds"][0], [(prm_rows[0:N_PRM, :], 0, N_PRM)])
                turn(st["rounds"][1], [(ab_rows[0:72, 0, :], 0, 72), (ab_rows[0:72, 1, :], 72, 72),
                                       (pe_rows[0:32, :], 144, 32)])

            def norm(st):
                n, nch = st["n"], st["width"] // P
                pe.wait_ge(xn_act, st["i"])
                pe.wait_ge(xn_dve, st["i"])
                dst = norm_dst(st)
                for r, t in enumerate(st["rounds"]):
                    items = []
                    for k in range(min(2, nch - 2 * r)):
                        for tt in range(NT):
                            items.append((dst[:, tt, (2 * r + k) * P:(2 * r + k + 1) * P], k * S + tt * P, P))
                    turn(t, items)

            def wait_left(st):
                for kind, n in st["left"]:
                    if kind == "norm":
                        pe.wait_ge(nlo_ready, n)
                    elif kind == "T":
                        wait_emptied(pe, T, lambda j: n)
                    else:
                        pe.wait_ge(conv_done, n)

            def linear(st):
                wait_left(st)
                c0 = st["chunk0"]
                for n0, w, parts, fills in st["blocks"]:
                    for i, (u, k0, per) in enumerate(parts):
                        use(lambda j: u)
                        wv = whi[:, u % RING, 0:per * w].rearrange("p (a b) -> p a b", a=per)
                        wl = wlo[:, u % RING, 0:per * w].rearrange("p (a b) -> p a b", a=per)
                        for tt in range(NT):
                            if i == 0:
                                wait_free(pe, U, lambda j: fills[tt])
                            for k in range(per):
                                kc = c0 + k0 + k
                                last = three(ubank(fills[tt])[:, 0:w], aT[:, kc, tt * P:(tt + 1) * P],
                                             aTl[:, kc, tt * P:(tt + 1) * P], wv[:, k], wl[:, k],
                                             i == 0 and k == 0, i == len(parts) - 1 and k == per - 1)
                            if i == len(parts) - 1:
                                last.then_inc(u_ready, 1)
                        if i < len(parts) - 1:
                            last.then_inc(w_used, 1)

            def ada(m, j):
                m_ = m(j if isinstance(j, int) else 2)
                use(lambda j: m(j)["u"], j)
                wait_free(pe, T, lambda j: m(j)["t"], j)
                slot, bank = m_["u"] % RING, tbank(m_["t"])
                wv = whi[:, slot, :].rearrange("p (a b) -> p a b", a=KC)
                wl = wlo[:, slot, :].rearrange("p (a b) -> p a b", a=KC)
                if m_["i"] == 0 and m_["layer"] == 0:
                    pe.wait_ge(cz_ready, 2)
                for kc in range(KC):
                    pe.matmul(bank[:, 0:ADA_W], c_hl[:, 2 * kc:2 * kc + P], wv[:, kc],
                              start=kc == 0, stop=False)
                    last = pe.matmul(bank[:, 0:ADA_W], c_hl[:, 2 * kc:2 * kc + P],
                                     wl[:, kc], start=False, stop=kc == KC - 1)
                last.then_inc(t_ready, 1)

            def ada_cols(m, j):
                m_ = m(j if isinstance(j, int) else 2)
                wait_emptied(pe, T, lambda j: m(j)["t"], j)
                wait_free(pe, T, lambda j: m(j)["tc"], j)
                for c in range(2):
                    last = pe.matmul(tbank(m_["tc"])[:, c:c + 1], row[:, m_["pos"] % 2, c * P:(c + 1) * P],
                                     pick[:, 0:1], start=True, stop=True)
                last.then_inc(t_ready, 1)

            def mlp(st):
                wait_left(st)
                hb = st["hb"]

                def body(j):
                    for what, e, get in events(st, j):
                        if what == "hidT":
                            tt = e["tt"]
                            wait_emptied(pe, U, lambda j: get(j)["fill"][tt], j)
                            wait_free(pe, T, lambda j: get(j)["t"], j)
                            for c in range(hb // P):
                                last = pe.transpose(tbank(e["t"])[:, c * P:(c + 1) * P],
                                                    hid(tt)[:, c * P:(c + 1) * P], ident[:, :])
                            last.then_inc(t_ready, 1)
                        elif what == "up":
                            half, slot = e["half"], e["u"] % RING
                            use(lambda j: get(j)["u"], j)
                            wv = whi[:, slot, :].rearrange("p (a b) -> p a b", a=4)
                            wl = wlo[:, slot, :].rearrange("p (a b) -> p a b", a=4)
                            for tt in range(NT):
                                if half == 0:
                                    wait_free(pe, U, lambda j: get(j)["fills"][tt], j)
                                for c in range(4):
                                    kc = 4 * half + c
                                    last = three(ubank(e["fills"][tt]), aT[:, kc, tt * P:(tt + 1) * P],
                                                 aTl[:, kc, tt * P:(tt + 1) * P], wv[:, c], wl[:, c],
                                                 kc == 0, kc == KC - 1)
                                if half == 1:
                                    last.then_inc(u_ready, 1)
                            if half == 0:
                                last.then_inc(w_used, 1)
                        elif what == "down":
                            half, slot = e["half"], e["u"] % RING
                            use(lambda j: get(j)["u"], j)
                            wait_emptied(pe, T, lambda j: get(j)["t"], j)
                            wv = whi[:, slot, :].rearrange("p (a b) -> p a b", a=2)
                            wl = wlo[:, slot, :].rearrange("p (a b) -> p a b", a=2)
                            first = isinstance(j, int) and j == 1 and half == 0
                            final = isinstance(j, int) and j == st["n"] and half == hb // 256 - 1
                            for c in range(2):
                                kc = 2 * half + c
                                for tt in range(NT):
                                    for nb in range(2):
                                        last = three(ACC[:, 2 * tt + nb, :], hT[:, kc, tt * P:(tt + 1) * P],
                                                     hTl[:, kc, tt * P:(tt + 1) * P], wv[:, c, nb * 512:(nb + 1) * 512],
                                                     wl[:, c, nb * 512:(nb + 1) * 512], first and c == 0,
                                                     final and c == 1)
                            last.then_inc(w_used, 1)
                        elif what == "ada":
                            ada(get, j)
                        else:
                            ada_cols(get, j)
                run_steps(pe, st, body)

            def turns_of(st):
                kind = st["kind"]
                if kind == "qk1":
                    pe.wait_ge(z_roped, 2)
                elif kind == "qk_mla":
                    pe.wait_ge(packed, 1)
                elif kind == "o_T":
                    if st["ready"] == "diff":
                        pe.wait_ge(dn_done, NT)
                    elif st["ready"] == "nsa":
                        pe.wait_ge(o_stored, sum(g["kind"] == "cmp" or g.get("br") == 1 for g in p.groups))
                    else:
                        wait_emptied(pe, U, lambda j: st["fill"])
                else:
                    wait_emptied(pe, U, lambda j: st["after"])
                for t, items in zip(st["rounds"], transposes(st)[0]):
                    turn(t, items)

            def attend(st):
                gs = st["groups"]
                for t in st["turned"]:
                    wait_emptied(pe, T, lambda j: t)
                if st["which"] == "nsa":
                    pe.wait_ge(kz_zero, 1)

                def scores(g):
                    n = g["g"]
                    if n >= 2:
                        pe.wait_ge(s_taken, n - 1)
                    nk, t, h0, kind = g["nk"], g["t"], g["h0"], g["kind"]
                    q = slice(t * P, (t + 1) * P)
                    if kind == "cmp":
                        sv = sbank(n)[:, 0:8 * 32].rearrange("p (h k) -> p h k", k=32)
                        for i in range(4):
                            last = pe.matmul(sv[:, 2 * i:2 * i + 2, 0:NC], qT[:, h0 // 2 + i, q],
                                             kcz[:, h0 // 8, :].rearrange("p (h k) -> p h k", k=NC),
                                             start=True, stop=True)
                    else:
                        sv = sbank(n).rearrange("p (h k) -> p h k", k=S)
                        if kind == "cross":
                            for i in range(2):
                                for c in range(2):
                                    last = pe.matmul(sv[:, i, :], qT[:, 2 * (h0 + i) + c, q], kz[:, 2 * (h0 + i) + c, :],
                                                     start=c == 0, stop=c == 1)
                        elif kind == "mla":
                            for i in range(4):
                                last = pe.matmul(sv[:, i, 0:nk], qT[0:96, h0 + i, q], kz[0:96, h0 + i, 0:nk],
                                                 start=True, stop=True)
                        else:
                            for i in range(2):
                                if kind == "swa":
                                    qc, k0 = h0 // 2 + i, 2 * (h0 // 4)
                                elif kind == "diff":
                                    qc, k0 = 4 + h0 + i, 4 + 2 * (h0 + i)
                                else:
                                    qc, k0 = h0 // 2 + i, 4 * g["br"] + 2 * (h0 // 8)
                                last = pe.matmul(sv[:, 2 * i:2 * i + 2, 0:nk], qT[:, qc, q], kz[:, k0:k0 + 2, 0:nk],
                                                 start=True, stop=True)
                    last.then_inc(s_ready, 1)

                def turn_probs(g):
                    n = g["g"]
                    if g["kind"] in ("diff", "cmp"):
                        pe.wait_ge(p_mixed, g["mixed"])
                    else:
                        pe.wait_ge(p_ready, n + 1)
                    for r, t in enumerate(g["rounds"]):
                        items = []
                        for k, (h, kc) in enumerate(g["turn"][4 * r:4 * r + 4]):
                            if g["kind"] == "cmp":
                                src = sp[:, n % 2, h * P:(h + 1) * P]
                            else:
                                src = sp[:, n % 2, h * S + kc * P:h * S + (kc + 1) * P]
                            items.append((src, k * P, P))
                        turn(t, items)

                def values(g):
                    n, t, h0, kind, f = g["g"], g["t"], g["h0"], g["kind"], g["fill"]
                    for tr in g["rounds"]:
                        wait_emptied(pe, T, lambda j: tr)
                    wait_free(pe, U, lambda j: f)
                    o = ubank(f)
                    if kind == "cmp":
                        for k in range(2):
                            last = pe.matmul(o[:, k * S:(k + 1) * S], pT[:, n % 2, k, :], vcb[:, h0 // 8, :],
                                             start=True, stop=True)
                        last.then_inc(u_ready, 1)
                        return
                    heads = [h for h, kc in g["turn"] if kc == 0]
                    for i, h in enumerate(heads):
                        if kind == "swa":
                            dv, v0, zt = HD, 640 + HD * (h0 // 4), z
                        elif kind == "diff":
                            dv, v0, zt = P, 1792 + P * (h0 + i), z
                        elif kind == "cross":
                            dv, v0, zt = S, D + S * (h0 + i), zc
                        elif kind == "mla":
                            dv, v0, zt = HD, 768 + P * (h0 + i) + HD, z
                        else:
                            dv, v0, zt = HD, D + 256 * (1 + g["br"]) + P + HD * (h0 // 8), z
                        for kc in range(g["nkc"]):
                            last = pe.matmul(o[:, i * dv:(i + 1) * dv], pT[:, n % 2, i * g["nkc"] + kc, :],
                                             zt[:, kc, v0:v0 + dv], start=kc == 0, stop=kc == g["nkc"] - 1)
                    last.then_inc(u_ready, 1)

                for i in range(len(gs) + 2):
                    if i < len(gs):
                        scores(gs[i])
                    if 1 <= i <= len(gs):
                        turn_probs(gs[i - 1])
                    if i >= 2:
                        values(gs[i - 2])

            def gate(st):
                pe.wait_ge(diag_ready, st["diag"])
                for r, t in enumerate(st["rounds"]):
                    wait_free(pe, T, lambda j: t)
                    for c in range(4):
                        last = pe.matmul(tbank(t)[:, c * P:(c + 1) * P], ones[:, :],
                                         tmp[:, r, c * P:(c + 1) * P], start=True, stop=True)
                    last.then_inc(t_ready, 1)

            def compress(st):
                for kv in range(2):
                    t, t2 = st["rounds"][2 * kv:2 * kv + 2]
                    u = st["units"][kv]
                    pe.wait_ge(cmp_rlo, kv + 1)
                    use(lambda j: u)
                    wait_free(pe, T, lambda j: t)
                    wv = whi[:, u % RING, :].rearrange("p (a b) -> p a b", a=16)
                    wl = wlo[:, u % RING, :].rearrange("p (a b) -> p a b", a=16)
                    for c in range(16):
                        pe.matmul(tbank(t)[:, 0:32], wv[:, c], R[:, c, :], start=c == 0, stop=False)
                        pe.matmul(tbank(t)[:, 0:32], wl[:, c], R[:, c, :], start=False, stop=False)
                        last = pe.matmul(tbank(t)[:, 0:32], wv[:, c], Rl[:, c, :], start=False, stop=c == 15)
                    last.then_inc(t_ready, 1)
                    wait_emptied(pe, T, lambda j: t)
                    wait_free(pe, T, lambda j: t2)
                    if kv == 0:
                        last = pe.matmul(tbank(t2)[:, 0:2 * NC], w2s[:, 0, :], hidc[:, 0, 0:2 * NC], start=True, stop=True)
                    else:
                        for g in range(2):
                            last = pe.matmul(tbank(t2)[0:NC, g * HD:(g + 1) * HD], hidc[:, 1, g * NC:(g + 1) * NC],
                                             w2s[:, 1, 0:HD], start=True, stop=True)
                    last.then_inc(t_ready, 1)

            table = dict(params=params, norm=norm, linear=linear, mlp=mlp, qk1=turns_of, qk_cross=turns_of,
                         conv_T=turns_of, qk_mla=turns_of, qk_nsa=turns_of, o_T=turns_of, attend=attend,
                         gate=gate, compress=compress)
            for st in p.stages:
                if st["kind"] in table:
                    table[st["kind"]](st)

        @block.scalar
        def _(act):
            def rows(dst, r0, n, src):
                act.dma_start(dst[r0:r0 + n], src).then_inc(prm_loaded, 16)

            pr = prm_rows[:, :]
            for r0, name in ((G_MIX, "g_mix"), (G_CROSS, "g_cross"), (G_MEM, "g_mem"), (G_MLP, "g_mlp")):
                rows(pr, r0, 8, A[name][0].rearrange("(a b) -> a b", b=P))
            rows(pr, NORM_G, 48, A["norm_g_2"].rearrange("l i (a b) -> (l i a) b", b=P))
            rows(pr, C_COL, 8, A["c_2"][0].rearrange("(a b) -> a b", b=P))
            rows(pr, Q_NORM, 2, A["hy_q_norm_2"][0].rearrange("(a b) -> a b", b=P))
            rows(pr, KV_NORM, 1, A["hy_kv_norm_2"])
            rows(pr, CONV_W, 12, A["hy_conv_w_2"][0].rearrange("k (a b) -> (k a) b", b=P))
            act.dma_start(pe_rows[0:32, :], A["nsa_cmp_pe_2"][0].rearrange("v (c q) d -> (v c) (q d)", q=2)).then_inc(prm_loaded, 16)
            for l in range(2):
                act.dma_start(ab_rows[0:72, l, :], A["ada_b_2"][l].rearrange("(a b) -> a b", b=P)).then_inc(prm_loaded, 16)
            act.dma_start(zc[:, :, 0:D], A["mem"][0].rearrange("(t p) d -> p t d", p=P)).then_inc(mem_loaded, 16)

            for u in range(LEAD):
                split_hi(act, lambda j: u)

            def params(st):
                act.wait_ge(ang_ready, 1)
                act.activation(trig[:, :, :, :], ang[:, :, :, :], ACT.Sin).then_inc(trig_ready, 1)
                act.wait_ge(lam_sums, 2)
                act.activation(lam[:, 0:2], lam[:, 2:4], ACT.Exp).then_inc(lam_exps, 1)
                wait_emptied(act, T, lambda j: st["rounds"][0])
                act.activation(cact[:, 0, :], prm[:, C_COL:C_COL + KC], ACT.Silu).then_inc(cact_ready, 1)
                act.wait_ge(cact_ready, 1)
                act.wait_ge(cz_ready, 1)
                act.activation(c_hl[:, 0:2 * KC:2], cact[:, 0, :], ACT.Copy).then_inc(cact_ready, 1)

            def norm(st):
                n, w = st["n"], st["width"]
                src, dst = src_of(st), norm_dst(st)
                wait_src(act, st)
                if st["rounds"][0] > 2:
                    act.wait_ge(t_ready, st["rounds"][0])
                act.activation(dst[:, 1, :], src[:, 1, :], ACT.Square, accum_out=ss[:, n, 1:2]).then_inc(ss_act, 1)
                act.wait_ge(rstd_ready, n + 1)
                act.activation(dst[:, 1, :], src[:, 1, :], ACT.Copy, scale=rstd[:, n, 1:2]).then_inc(xn_act, 1)
                for r, t in enumerate(st["rounds"]):
                    m = min(2, w // P - 2 * r)
                    wait_emptied(act, T, lambda j: t)
                    k = st["chunk0"] + 2 * r
                    act.activation(aT[:, k:k + m, :].rearrange("p a b -> p (a b)"),
                                   tmp[:, (st["lo0"] + r) % 2, 0:m * S], ACT.Copy).then_inc(nhi_ready, 1)

            def linear(st):
                for n0, w, parts, fills in st["blocks"]:
                    for u, _, _ in parts:
                        split_hi(act, lambda j: u + LEAD)
                    if st["dst"] == "x":
                        continue
                    dst = zc if st["dst"] == "zc" else z
                    off = n0 + (768 if st["dst"] == "z768" else 0)
                    for tt in range(NT):
                        act.wait_ge(u_ready, fills[tt] + 1)
                        act.activation(dst[:, tt, off:off + w], ubank(fills[tt])[:, 0:w], ACT.Copy).then_inc(u_act, 1)

            def mlp(st):
                nk = st["hb"] // P

                def body(j):
                    for what, e, get in events(st, j):
                        if what in ("up", "down", "ada"):
                            split_hi(act, lambda j: get(j)["u"] + LEAD, j)
                        if what == "hidT":
                            act.wait_ge(t_ready, at(j, lambda j: get(j)["t"] + 1))
                            act.activation(hT[:, 0:nk, e["tt"] * P:(e["tt"] + 1) * P],
                                           tbank(e["t"])[:, 0:nk * P].rearrange("p (a b) -> p a b", b=P),
                                           ACT.Copy).then_inc(t_act, 1)
                        elif what == "up" and e["half"] == 1:
                            for tt in range(NT):
                                act.wait_ge(u_ready, at(j, lambda j: get(j)["fills"][tt] + 1))
                                if not isinstance(j, int) or j > 0:
                                    act.wait_ge(u_dve, at(j, lambda j: U.emptied("D", get(j)["fills"][tt] - 2)))
                                bank = ubank(e["fills"][tt])
                                if st["mlp"] == "relu2":
                                    act.activation(part(tt), bank, ACT.Relu).then_inc(r_ready, 1)
                                else:
                                    act.activation(part(tt)[:, 0:HB2], bank[:, 0:HB2], ACT.Silu).then_inc(r_ready, 1)
                        elif what == "ada":
                            act.wait_ge(t_ready, at(j, lambda j: get(j)["t"] + 1))
                            act.activation(row[:, e["pos"] % 2, :], tbank(e["t"])[:, 0:ADA_W], ACT.Copy).then_inc(t_act, 1)
                run_steps(act, st, body)

            def turns_of(st):
                for t, dst in zip(st["rounds"], transposes(st)[1]):
                    if "A" in T.who[t]:
                        act.wait_ge(t_ready, t + 1)
                        for i, (to, r0, n, c0, c1) in enumerate(dst):
                            ins = act.activation(to, view(tbank(t)[r0:r0 + n, c0:c1], to), ACT.Copy)
                        ins.then_inc(t_act, 1)

            def o_T(st):
                for r, t in enumerate(st["rounds"]):
                    k = st["chunk0"] + 2 * r
                    act.wait_ge(t_ready, t + 1)
                    act.activation(aT[:, k:k + 2, :].rearrange("p a b -> p (a b)"), tbank(t), ACT.Copy).then_inc(t_act, 1)

            def exps(g):
                n, kind = g["g"], g["kind"]
                sb_ = n % 2
                act.wait_ge(m_ready, n + 1)
                if kind == "cmp":
                    v = sp[:, sb_, 0:S].rearrange("p (h k) -> p h k", k=32)[:, :, 0:NC]
                    act.activation(v, v, ACT.Exp, scale=SWA_SCALE).then_inc(p_ready, 1)
                    return
                scale = {"cross": CROSS_SCALE, "mla": MLA_SCALE}.get(kind, SWA_SCALE)
                if kind == "swa":
                    act.activation(dsk[:, sb_, 1, :], dsk[:, sb_, 0, :], ACT.Exp)
                for h in range(g["nh"]):
                    v = sp[:, sb_, h * S:h * S + g["nk"]]
                    ins = act.activation(v, v, ACT.Exp, bias=negm[:, sb_, h:h + 1], scale=scale,
                                         accum_out=sums[:, sb_, h:h + 1])
                ins.then_inc(p_ready, 1)

            def probs_out(g):
                for r, t in enumerate(g["rounds"]):
                    if "A" in T.who[t]:
                        m = len(g["turn"][4 * r:4 * r + 4])
                        act.wait_ge(t_ready, t + 1)
                        act.activation(pT[:, g["g"] % 2, 4 * r:4 * r + m, :].rearrange("p a b -> p (a b)"),
                                       tbank(t)[:, 0:m * P], ACT.Copy).then_inc(t_act, 1)

            def attend(st):
                gs = st["groups"]
                for i in range(len(gs) + 1):
                    if i < len(gs):
                        exps(gs[i])
                    if i >= 1:
                        g = gs[i - 1]
                        if i >= 3:
                            act.wait_ge(u_ready, gs[i - 3]["fill"] + 1)
                        probs_out(g)

            def conv(st):
                act.wait_ge(conv_y, 1)
                act.activation(aT[:, 0:4, :], zcf[:, 4:8, :], ACT.Copy).then_inc(conv_hi, 1)

            def compress(st):
                act.wait_ge(gl_ready, 1)
                act.activation(gates[:, :, :], gates[:, :, :], ACT.Sigmoid).then_inc(gates_ready, 1)
                for kv in range(2):
                    act.wait_ge(cmp_r, kv + 1)
                    act.activation(R[:, :, :], Rf[:, :, :], ACT.Copy).then_inc(cmp_rhi, 1)
                    t = st["rounds"][2 * kv]
                    split_hi(act, lambda j: st["units"][kv] + LEAD)
                    act.wait_ge(t_ready, t + 1)
                    act.activation(hbias[:, kv:kv + 1], tbank(t)[:, 30:31], ACT.Copy).then_inc(cmp_b, 1)
                    act.wait_ge(cmp_b, kv + 1)
                    act.activation(hidc[:, kv, 0:2 * NC], tbank(t)[:, 0:2 * NC], ACT.Silu,
                                   bias=hbias[:, kv:kv + 1]).then_inc(t_act, 1)

            def scale_x(st):
                n = st["n"]
                wait_x(act, st["need"])
                act.wait_ge(t_ready, st["turn"])
                act.activation(xn[:, 1, :], x[:, 1, :], ACT.Square, accum_out=ss[:, n, 1:2]).then_inc(ss_act, 1)

            table = dict(params=params, norm=norm, linear=linear, mlp=mlp, qk1=turns_of, qk_cross=turns_of,
                         conv_T=turns_of, qk_mla=turns_of, qk_nsa=turns_of, o_T=o_T, attend=attend,
                         conv=conv, compress=compress, scale_x=scale_x)
            for st in p.stages:
                if st["kind"] in table:
                    table[st["kind"]](st)

        @block.vector
        def _(dve):
            steps = [0]

            def step(ins):
                steps[0] += 1
                ins.then_inc(v_done, 1)
                return steps[0]

            def link(ins):
                dve.wait_ge(v_done, step(ins))

            def params(st):
                dve.wait_ge(small_loaded, 16 * N_SMALL)
                link(dve.tensor_copy(posf[:, :, :], pos[:, :, :]))
                for k in range(2):
                    for tt in range(NT):
                        for i, (f0, f1) in enumerate(((0, 32), (32, 48))):
                            n = step(dve.tensor_scalar(ang[:, k, tt, f0:f1], freq[:, f0:f1], posf[:, i, tt:tt + 1], None, ALU.mult))
                dve.wait_ge(v_done, n)
                for k in range(2):
                    n = step(dve.tensor_scalar(flat(kk[:, k]), flat(ang[:, k]), 1 / TWO_PI, 0.25 if k == 0 else 0.0, ALU.mult, ALU.add))
                dve.wait_ge(v_done, n)
                link(dve.tensor_scalar(flat(kk), flat(kk), MAGIC, None, ALU.add))
                link(dve.tensor_scalar(flat(kk), flat(kk), -MAGIC, None, ALU.add))
                for c in (C1, C2):
                    link(dve.scalar_tensor_tensor(flat(ang), flat(kk), -c, flat(ang), ALU.mult, ALU.add))
                link(dve.tensor_scalar(flat(ang[:, 0]), flat(ang[:, 0]), math.pi / 2, None, ALU.add))
                link(dve.scalar_tensor_tensor(flat(ang), flat(kk), -C3, flat(ang), ALU.mult, ALU.add))
                dve.tensor_scalar(flat(ang), flat(ang), -PI_LOW, PI_LOW, ALU.max, ALU.min).then_inc(ang_ready, 1)
                for i in range(2):
                    link(dve.tensor_tensor(lam2[:, i, :], lamb[:, 2 * i, :], lamb[:, 2 * i + 1, :], ALU.mult))
                    dve.tensor_reduce(lam[:, 2 + i:3 + i], lam2[:, i, :], AX.X, ALU.add).then_inc(lam_sums, 1)
                dve.wait_ge(lam_exps, 1)
                link(dve.tensor_tensor(lam[:, 2:3], lam[:, 1:2], lam[:, 0:1], ALU.subtract))
                link(dve.tensor_scalar(lam[:, 2:3], lam[:, 2:3], -LAM_INIT, None, ALU.add))
                step(dve.tensor_scalar(nsink[:, :], sink[:, :], -1.0, None, ALU.mult))
                step(dve.tensor_scalar(gdiff[:, :], gdiff[:, :], 1.0 - LAM_INIT, None, ALU.mult))
                r0, r1 = st["rounds"]
                dve.wait_ge(t_ready, r0 + 1)
                dve.tensor_copy(prm[:, :], tbank(r0)[:, 0:N_PRM]).then_inc(t_dve, 1)
                dve.wait_ge(t_ready, r1 + 1)
                dve.tensor_copy(prm2[:, :], tbank(r1)[:, 0:176]).then_inc(t_dve, 1)
                dve.memset(c_hl[:, :].bitcast(F32), 0.0).then_inc(cz_ready, 1)
                dve.wait_ge(cact_ready, 2)
                dve.tensor_tensor(c_hl[:, 1:2 * KC:2], cact[:, 0, :], c_hl[:, 0:2 * KC:2].bitcast(F32), ALU.subtract).then_inc(cz_ready, 1)
                for u in range(LEAD):
                    split_lo(dve, lambda j: u)

            def norm(st):
                n, w = st["n"], st["width"]
                src, dst = src_of(st), norm_dst(st)
                wait_src(dve, st)
                if st["lo0"] > 0:
                    dve.wait_ge(nlo_ready, st["lo0"])
                if st["src"] == "cq":
                    dve.wait_ge(conv_done, 1)
                if st["rounds"][0] > 2:
                    dve.wait_ge(t_ready, st["rounds"][0])
                dve.scalar_tensor_tensor(dst[:, 0, :], src[:, 0, :], 1.0, src[:, 0, :], ALU.mult, ALU.mult,
                                         accum_out=ss[:, n, 0:1]).then_inc(ss_dve, 1)
                dve.wait_ge(rstd_ready, n + 1)
                dve.tensor_scalar(dst[:, 0, :], src[:, 0, :], rstd[:, n, 0:1], None, ALU.mult).then_inc(xn_dve, 1)
                kind, i = st["scale"]

                def low(r):
                    m = min(2, w // P - 2 * r)
                    k = st["chunk0"] + 2 * r
                    dve.wait_ge(nhi_ready, st["lo0"] + r + 1)
                    dve.tensor_tensor(aTl[:, k:k + m, :].rearrange("p a b -> p (a b)"),
                                      tmp[:, (st["lo0"] + r) % 2, 0:m * S],
                                      aT[:, k:k + m, :].rearrange("p a b -> p (a b)").bitcast(F32),
                                      ALU.subtract).then_inc(nlo_ready, 1)

                for r, t in enumerate(st["rounds"]):
                    m = min(2, w // P - 2 * r)
                    dve.wait_ge(t_ready, t + 1)
                    if st["lo0"] + r >= 2:
                        dve.wait_ge(nlo_ready, st["lo0"] + r - 1)
                    for c in range(m):
                        k = 2 * r + c
                        scale = prm[:, i + k:i + k + 1] if kind == "prm" else msc[:, i, k:k + 1]
                        if st["shift"] is None:
                            args = (scale, None, ALU.mult)
                        else:
                            layer, part_ = st["shift"]
                            args = (scale, mod[:, layer, part_ * 8 + k:part_ * 8 + k + 1], ALU.mult, ALU.add)
                        ins = dve.tensor_scalar(tmp[:, (st["lo0"] + r) % 2, c * S:(c + 1) * S],
                                                tbank(t)[:, c * S:(c + 1) * S], *args)
                        if c < m - 1:
                            continue
                        ins.then_inc(t_dve, 1)
                    if r > 0:
                        low(r - 1)
                low(len(st["rounds"]) - 1)

            def rope(x1, x2, cos, sin, shape, last):
                n = int(np.prod(shape))
                names = " ".join("abc"[:len(shape)])
                dims = {k: v for k, v in zip("abc", shape[:-1])}
                t1, t2, t3 = [f[:, 0:n].rearrange(f"p ({names}) -> p {names}", **dims)
                              for f in (sp[:, 0, :], sp[:, 1, :], pT[:, 0, :, :].rearrange("p a b -> p (a b)"))]
                return [lambda: step(dve.tensor_tensor(t1, x1, cos, ALU.mult)),
                        lambda: step(dve.tensor_tensor(t2, x2, sin, ALU.mult)),
                        lambda: link(dve.tensor_tensor(t3, x1, sin, ALU.mult)),
                        lambda: link(dve.tensor_tensor(x1, t1, t2, ALU.subtract)),
                        lambda: link(dve.tensor_tensor(t1, x2, cos, ALU.mult)),
                        lambda: last(dve.tensor_tensor(x2, t1, t3, ALU.add))]

            def rope_first():
                jobs = []
                for c0, h in ((0, 10), (768, 16)):
                    v = z[:, :, c0:c0 + HD * h].rearrange("p t (h s f) -> p t h s f", s=2, f=ROPE_HALF)
                    cos, sin = [trig[:, i, :, 0:ROPE_HALF].unsqueeze(2).broadcast_to([P, NT, h, ROPE_HALF])
                                for i in range(2)]
                    jobs += rope(v[:, :, :, 0, :], v[:, :, :, 1, :], cos, sin, (NT, h, ROPE_HALF),
                                 lambda ins: roped(ins))
                return jobs

            n_roped = [0]

            def roped(ins):
                n_roped[0] += 1
                ins.then_inc(z_roped, 1)
                dve.wait_ge(z_roped, n_roped[0])

            def add_to_x(src, tt, c0, w, k, gated, free, signal):
                xs = x[:, tt, c0:c0 + w]
                if gated:
                    tm = tmp[:, k % 2, 0:w]
                    ins = dve.tensor_tensor(tm, src, gbc[:, c0:c0 + w], ALU.mult)
                    if free is None:
                        link(ins)
                    else:
                        ins.then_inc(u_dve, 1)
                        dve.wait_ge(u_dve, free)
                    ins = dve.tensor_tensor(xs, tm, xs, ALU.add)
                    ins.then_inc(x_ready, 1) if signal else step(ins)
                else:
                    ins = dve.tensor_tensor(xs, src, xs, ALU.add)
                    if free is not None:
                        ins.then_inc(u_dve, 1)
                    else:
                        ins.then_inc(x_ready, 1) if signal else step(ins)

            def linear(st):
                jobs = []
                if st["side"] is not None:
                    dve.wait_ge(trig_ready, 1)
                    wait_emptied(dve, U, lambda j: st["side"])
                    jobs = rope_first()
                k = 0
                for b, (n0, w, parts, fills) in enumerate(st["blocks"]):
                    for u, _, _ in parts:
                        split_lo(dve, lambda j: u + LEAD)
                        for job in jobs[:2]:
                            job()
                        jobs = jobs[2:]
                    if st["dst"] != "x":
                        continue
                    for tt in range(NT):
                        dve.wait_ge(u_ready, fills[tt] + 1)
                        add_to_x(ubank(fills[tt])[:, 0:w], tt, n0, w, k, st["gate"],
                                 U.emptied("D", fills[tt]), b == len(st["blocks"]) - 1)
                        k += 1
                for job in jobs:
                    job()

            def mlp(st):
                nk = st["hb"] // P

                def body(j):
                    for what, e, get in events(st, j):
                        if what in ("up", "down", "ada"):
                            split_lo(dve, lambda j: get(j)["u"] + LEAD, j)
                        if what == "hidT":
                            to = slice(e["tt"] * P, (e["tt"] + 1) * P)
                            dve.wait_ge(t_act, at(j, lambda j: T.emptied("A", get(j)["t"])))
                            dve.tensor_tensor(hTl[:, 0:nk, to], tbank(e["t"])[:, 0:nk * P].rearrange("p (a b) -> p a b", b=P),
                                              hT[:, 0:nk, to].bitcast(F32), ALU.subtract).then_inc(t_dve, 1)
                        elif what == "up" and e["half"] == 1:
                            for tt in range(NT):
                                dve.wait_ge(r_ready, at(j, lambda j: st["r0"] + NT * j + tt + 1))
                                bank = ubank(e["fills"][tt])
                                if st["mlp"] == "relu2":
                                    ins = dve.scalar_tensor_tensor(hid(tt), bank, 0.0, part(tt), ALU.max, ALU.mult)
                                else:
                                    ins = dve.tensor_tensor(hid(tt)[:, 0:HB2], bank[:, HB2:2 * HB2],
                                                            part(tt)[:, 0:HB2], ALU.mult)
                                ins.then_inc(u_dve, 1)
                        elif what == "ada_cols":
                            dve.wait_ge(t_ready, at(j, lambda j: get(j)["tc"] + 1))
                            c = at(j, lambda j: 2 * get(j)["i"])
                            dve.tensor_tensor(mod[:, e["layer"], bass.ds(c, 2)], tbank(e["tc"])[:, 0:2],
                                              prm2[:, bass.ds(c + 72 * e["layer"], 2)], ALU.add).then_inc(t_dve, 1)
                run_steps(dve, st, body)
                dve.wait_ge(w_used, st["acc_ready"])
                k = 0
                for tt in range(NT):
                    for nb in range(2):
                        add_to_x(ACC[:, 2 * tt + nb, :], tt, nb * 512, 512, k, st["gate"], None, nb == 1)
                        k += 1

            def turns_of(st):
                for t, dst in zip(st["rounds"], transposes(st)[1]):
                    if "D" in T.who[t]:
                        dve.wait_ge(t_ready, t + 1)
                        for i, (to, r0, n, c0, c1) in enumerate(dst):
                            ins = dve.tensor_copy(to, view(tbank(t)[r0:r0 + n, c0:c1], to))
                        ins.then_inc(t_dve, 1)

            def o_T(st):
                for r, t in enumerate(st["rounds"]):
                    k = st["chunk0"] + 2 * r
                    dve.wait_ge(t_act, T.emptied("A", t))
                    dve.tensor_tensor(aTl[:, k:k + 2, :].rearrange("p a b -> p (a b)"), tbank(t),
                                      aT[:, k:k + 2, :].rearrange("p a b -> p (a b)").bitcast(F32),
                                      ALU.subtract).then_inc(t_dve, 1)

            def smax(g, prev):
                n, nh, nk, kind, t = g["g"], g["nh"], g["nk"], g["kind"], g["t"]
                b = n % 2
                dve.wait_ge(s_ready, n + 1)
                if prev is not None:
                    dve.wait_ge(t_ready, prev["rounds"][-1] + 1)
                if kind == "cmp":
                    full = sp[:, b, 0:S]
                    link(dve.memset(full, 0.0))
                    s_ = full.rearrange("p (h k) -> p h k", k=32)[:, :, 0:NC]
                    ps_ = sbank(n)[:, 0:S].rearrange("p (h k) -> p h k", k=32)[:, :, 0:NC]
                    mask = cneg[:, t, :]
                else:
                    s_ = sp[:, b, 0:nh * S].rearrange("p (h k) -> p h k", k=S)[:, :, 0:nk]
                    ps_ = sbank(n)[:, 0:nh * S].rearrange("p (h k) -> p h k", k=S)[:, :, 0:nk]
                    mask = (band if kind == "swa" else causal)[:, 0:S] if t else causal[:, P:S]
                if kind == "cross":
                    dve.tensor_copy(s_, ps_).then_inc(s_taken, 1)
                else:
                    dve.tensor_tensor(s_, ps_, mask.unsqueeze(1).broadcast_to([P, nh, s_.shape[2]]),
                                      ALU.add).then_inc(s_taken, 1)
                dve.wait_ge(s_taken, n + 1)
                link(dve.tensor_reduce(rmax[:, b, 0:nh], s_, AX.X, ALU.max))
                if kind == "cmp":
                    dve.tensor_tensor(s_, s_, rmax[:, b, 0:nh].unsqueeze(2).broadcast_to([P, nh, NC]),
                                      ALU.subtract).then_inc(m_ready, 1)
                    return
                scale = {"cross": CROSS_SCALE, "mla": MLA_SCALE}.get(kind, SWA_SCALE)
                ins = dve.tensor_scalar(negm[:, b, 0:nh], rmax[:, b, 0:nh], -scale, None, ALU.mult)
                if kind == "swa":
                    h0 = g["h0"]
                    link(ins)
                    link(dve.tensor_tensor(negm[:, b, 0:4], negm[:, b, 0:4], nsink[:, h0:h0 + 4], ALU.min))
                    ins = dve.tensor_tensor(dsk[:, b, 0, :], sink[:, h0:h0 + 4], negm[:, b, 0:4], ALU.add)
                ins.then_inc(m_ready, 1)

            def after(g):
                n, nh, kind, t, h0 = g["g"], g["nh"], g["kind"], g["t"], g["h0"]
                b = n % 2
                dve.wait_ge(p_ready, n + 1)
                if kind == "cmp":
                    v = sp[:, b, 0:S].rearrange("p (h k) -> p h k", k=32)[:, :, 0:NC]
                    dve.tensor_tensor(v, v, cmask[:, t, :].unsqueeze(1).broadcast_to([P, nh, NC]),
                                      ALU.mult).then_inc(p_mixed, 1)
                    dve.wait_ge(p_mixed, g["mixed"])
                    link(dve.tensor_reduce(sums[:, b, 0:nh], v, AX.X, ALU.add))
                if kind == "swa":
                    link(dve.tensor_tensor(sums[:, b, 0:4], sums[:, b, 0:4], dsk[:, b, 1, :], ALU.add))
                if kind in ("mla", "nsa", "cmp"):
                    link(dve.tensor_scalar(sums[:, b, 0:nh], sums[:, b, 0:nh], 1e-20, None, ALU.max))
                n_ = step(dve.reciprocal(rinv[:, b, 0:nh], sums[:, b, 0:nh]))
                if kind == "diff":
                    dve.wait_ge(v_done, n_)
                    link(dve.tensor_scalar(rg[:, b, 0:2], rinv[:, b, 1:4:2], lam[:, 2:3], None, ALU.mult))
                    nk = g["nk"]
                    for i in range(2):
                        p0 = sp[:, b, 2 * i * S:2 * i * S + nk]
                        p1 = sp[:, b, (2 * i + 1) * S:(2 * i + 1) * S + nk]
                        link(dve.tensor_scalar(p1, p1, rg[:, b, i:i + 1], None, ALU.mult))
                        ins = dve.scalar_tensor_tensor(p0, p0, rinv[:, b, 2 * i:2 * i + 1], p1, ALU.mult, ALU.add)
                        if i == 0:
                            step(ins)
                    ins.then_inc(p_mixed, 1)
                if kind in ("nsa", "cmp"):
                    dve.wait_ge(v_done, n_)
                    branch = 0 if kind == "cmp" else 1 + g["br"]
                    dve.wait_ge(gates_ready, 1)
                    gv = gates[:, t, :].rearrange("p (h b) -> p h b", b=3)[:, h0:h0 + nh, branch]
                    n_ = step(dve.tensor_tensor(rg[:, b, 0:nh], rinv[:, b, 0:nh], gv, ALU.mult))
                g["scaled"] = n_

            def probs_out(g):
                for r, t in enumerate(g["rounds"]):
                    if "D" in T.who[t]:
                        m = len(g["turn"][4 * r:4 * r + 4])
                        dve.wait_ge(t_ready, t + 1)
                        dve.tensor_copy(pT[:, g["g"] % 2, 4 * r:4 * r + m, :].rearrange("p a b -> p (a b)"),
                                        tbank(t)[:, 0:m * P]).then_inc(t_dve, 1)

            stored_o = [0]

            def o_out(g):
                n, nh, kind, t, h0, f = g["g"], g["nh"], g["kind"], g["t"], g["h0"], g["fill"]
                b = n % 2
                dve.wait_ge(u_ready, f + 1)
                dve.wait_ge(v_done, g["scaled"])
                if kind == "diff":
                    dve.tensor_copy(xn[:, t, 512 + P * h0:512 + P * h0 + S], ubank(f)[:, 0:S]).then_inc(u_dve, 1)
                    return
                dv = S if kind == "cross" else HD
                c0 = dv * h0 + (512 if kind == "mla" else 0)
                o = xn[:, t, c0:c0 + nh * dv]
                bank = ubank(f)[:, 0:nh * dv].rearrange("p (h d) -> p h d", d=dv)
                r = rg if kind in ("nsa", "cmp") else rinv
                to = o
                if kind == "cmp" or g.get("br") == 1:
                    to = tmp[:, b, 0:nh * dv]
                dve.tensor_tensor(to.rearrange("p (h d) -> p h d", d=dv), bank,
                                  r[:, b, 0:nh].unsqueeze(2).broadcast_to([P, nh, dv]), ALU.mult).then_inc(u_dve, 1)
                if to is not o:
                    dve.wait_ge(u_dve, U.emptied("D", f))
                    dve.tensor_tensor(o, o, to, ALU.add).then_inc(o_stored, 1)

            def attend(st):
                gs = st["groups"]
                for i in range(len(gs) + 2):
                    if i < len(gs):
                        smax(gs[i], gs[i - 2] if i >= 2 else None)
                    if 1 <= i <= len(gs):
                        g = gs[i - 1]
                        if i >= 3:
                            dve.wait_ge(u_dve, U.emptied("D", gs[i - 3]["fill"]))
                        after(g)
                        if i >= 3:
                            dve.wait_ge(u_ready, gs[i - 3]["fill"] + 1)
                        probs_out(g)
                    if i >= 2:
                        o_out(gs[i - 2])

            def diff_norm(st):
                dve.wait_ge(u_dve, U.emptied("D", st["fill"]))
                for tt in range(NT):
                    od = xn[:, tt, 512:D]
                    link(dve.tensor_tensor(tmp[:, tt, :], od, od, ALU.mult))
                    dve.tensor_reduce(dss[:, 0, 4 * tt:4 * tt + 4], tmp[:, tt, :].rearrange("p (h d) -> p h d", d=P),
                                      AX.X, ALU.add).then_inc(dn_ss, 1)
                dve.wait_ge(dn_r, 1)
                for tt in range(NT):
                    od = xn[:, tt, 512:D].rearrange("p (h d) -> p h d", d=P)
                    link(dve.tensor_tensor(od, od, dss[:, 2, 4 * tt:4 * tt + 4].unsqueeze(2).broadcast_to([P, 4, P]), ALU.mult))
                    dve.tensor_tensor(od, od, gdiff[:, :].unsqueeze(1).broadcast_to([P, 4, P]), ALU.mult).then_inc(dn_done, 1)

            def scale_x(st):
                n, last = st["n"], st is p.stages[-1]
                wait_x(dve, st["need"])
                dve.wait_ge(t_ready, st["turn"])
                dve.scalar_tensor_tensor(xn[:, 0, :], x[:, 0, :], 1.0, x[:, 0, :], ALU.mult, ALU.mult,
                                         accum_out=ss[:, n, 0:1]).then_inc(ss_dve, 1)
                dve.wait_ge(rstd_ready, n + 1)
                dve.wait_ge(gain_loaded, 32 if last else 16)
                dve.wait_ge(ss_dve, n + 1)
                for tt in range(NT):
                    dve.scalar_tensor_tensor((xn if last else x)[:, tt, :], x[:, tt, :], rstd[:, n, tt:tt + 1], gbc[:, :],
                                             ALU.mult, ALU.mult).then_inc(out_ready if last else x_ready, 1)

            def mod_cols(st):
                layer = st["layer"]
                dve.wait_ge(t_dve, T.emptied("D", st["last"]))
                for k in range(3):
                    g0 = NORM_G + 8 * (3 * layer + k)
                    n = step(dve.scalar_tensor_tensor(msc[:, k, :], mod[:, layer, 8 * (3 * k + 1):8 * (3 * k + 2)], 1.0,
                                                      prm[:, g0:g0 + 8], ALU.add, ALU.mult))
                dve.wait_ge(v_done, n)

            def gate(st):
                wait_x(dve, st["need"])
                for k in range(8):
                    c = 8 * st["m"] + k
                    ins = dve.tensor_scalar(tmp[:, k // 4, (k % 4) * P:(k % 4 + 1) * P], ident[:, :],
                                            mod[:, st["layer"], c:c + 1], st["factor"], ALU.mult, ALU.mult)
                ins.then_inc(diag_ready, 1)
                for r, t in enumerate(st["rounds"]):
                    dve.wait_ge(t_ready, t + 1)
                    dve.tensor_copy(gbc[:, r * 512:(r + 1) * 512], tbank(t)).then_inc(t_dve, 1)
                dve.wait_ge(t_dve, T.emptied("D", st["rounds"][-1]))

            def conv(st):
                for t in st["turned"][-2:]:
                    wait_emptied(dve, T, lambda j: t)
                u_, t_, y_ = zcf[:, 0:4, :], zcf[:, 12:16, :], zcf[:, 4:8, :]
                link(dve.tensor_tensor(t_, zcf[:, 4:8, :], u_, ALU.mult))
                for k in range(4):
                    n = step(dve.tensor_scalar(u_[:, k, :], t_[:, k, :], prm[:, CONV_W + 8 + k:CONV_W + 9 + k], None, ALU.mult))
                for tap in (1, 0):
                    d = 2 - tap
                    dve.wait_ge(v_done, n)
                    for k in range(4):
                        c = CONV_W + 4 * tap + k
                        n = step(dve.scalar_tensor_tensor(u_[:, k, d:S], t_[:, k, 0:S - d], prm[:, c:c + 1],
                                                          u_[:, k, d:S], ALU.mult, ALU.add))
                dve.wait_ge(v_done, n)
                dve.tensor_tensor(y_, u_, zcf[:, 8:12, :], ALU.mult).then_inc(conv_y, 1)
                dve.wait_ge(conv_y, 1)
                dve.wait_ge(conv_hi, 1)
                dve.tensor_tensor(aTl[:, 0:4, :], y_, aT[:, 0:4, :].bitcast(F32), ALU.subtract).then_inc(conv_done, 1)

            def mla_pack(st):
                wait_emptied(dve, U, lambda j: st["after"])
                h = 8
                q = z[:, :, 0:768].rearrange("p t (h w) -> p t h w", w=96)
                cos, sin = [trig[:, i, :, 32:48] for i in range(2)]
                cb, sb_ = [v.unsqueeze(2).broadcast_to([P, NT, h, ROPE_HALF_2]) for v in (cos, sin)]
                for job in rope(q[:, :, :, 64:80], q[:, :, :, 80:96], cb, sb_, (NT, h, ROPE_HALF_2), link):
                    job()
                for job in rope(z[:, :, 1920:1936], z[:, :, 1936:1952], cos, sin, (NT, ROPE_HALF_2), link):
                    job()
                for tt in range(NT):
                    kf = kfull[:, tt, :].rearrange("p (h w) -> p h w", w=96)
                    kv = z[:, tt, 768:1792].rearrange("p (h w) -> p h w", w=P)
                    step(dve.tensor_copy(kf[:, :, 0:HD], kv[:, :, 0:HD]))
                    ins = dve.tensor_copy(kf[:, :, HD:96], z[:, tt, 1920:1952].unsqueeze(1).broadcast_to([P, 8, 32]))
                    if tt == 0:
                        step(ins)
                ins.then_inc(packed, 1)

            def compress(st):
                wait_emptied(dve, U, lambda j: st["after"])
                dve.tensor_tensor(gates[:, :, :], z[:, :, 1792:1840], gateb[:, :].unsqueeze(1).broadcast_to([P, NT, 48]),
                                  ALU.add).then_inc(gl_ready, 1)
                wait_emptied(dve, T, lambda j: st["turned"][4])
                for kv in range(2):
                    if kv == 1:
                        dve.wait_ge(cmp_rlo, 1)
                    cT = kz[:, 8 + kv, :]
                    for g in range(2):
                        for par in range(2):
                            for ch in range(2):
                                src = cT[HD * g:HD * g + HD, :].rearrange("p (a c q) -> p c a q", c=8, q=2)
                                dve.tensor_copy(Rf[HD * par:HD * par + HD, 8 * ch:8 * ch + 8, g * NC:(g + 1) * NC],
                                                src[:, :, ch:ch + NC, par])
                    if kv == 0:
                        dve.memset(Rf[:, :, 31], 0.0)
                    dve.tensor_copy(Rf[:, :, 30], prm2[:, 144 + 16 * kv:160 + 16 * kv]).then_inc(cmp_r, 1)
                    dve.wait_ge(cmp_r, kv + 1)
                    dve.wait_ge(cmp_rhi, kv + 1)
                    if kv == 1:
                        dve.wait_ge(t_ready, st["rounds"][0] + 1)
                    dve.tensor_tensor(Rl[:, :, :], Rf[:, :, :], R[:, :, :].bitcast(F32), ALU.subtract).then_inc(cmp_rlo, 1)
                    split_lo(dve, lambda j: st["units"][kv] + LEAD)
                    t = st["rounds"][2 * kv + 1]
                    bank = tbank(t)
                    dve.wait_ge(t_ready, t + 1)
                    if kv == 0:
                        for g in range(2):
                            for par in range(2):
                                ins = dve.tensor_copy(kcz[HD * par:HD * par + HD, g, par * NC:(par + 1) * NC],
                                                      bank[HD * par:HD * par + HD, g * NC:(g + 1) * NC])
                    else:
                        dve.wait_ge(kz_zero, 1)
                        for g in range(2):
                            for i in range(4):
                                ins = dve.tensor_copy(vcb[32 * i:32 * i + NC, g, i * HD:(i + 1) * HD],
                                                      bank[0:NC, g * HD:(g + 1) * HD])
                    ins.then_inc(t_dve, 1)

            table = dict(params=params, norm=norm, linear=linear, mlp=mlp, qk1=turns_of, qk_cross=turns_of,
                         conv_T=turns_of, qk_mla=turns_of, qk_nsa=turns_of, o_T=o_T, attend=attend, diff_norm=diff_norm,
                         conv=conv, compress=compress, scale_x=scale_x, mod_cols=mod_cols, gate=gate, mla_pack=mla_pack)
            for st in p.stages:
                table[st["kind"]](st)

        @block.gpsimd
        def _(pool):
            def small(dst, src):
                pool.dma_start(dst, src).then_inc(small_loaded, 16)

            for i in range(2):
                for t in range(NT):
                    small(pos[:, i, t:t + 1], A["positions_2" if i else "positions"][0, t * P:(t + 1) * P].rearrange("(p a) -> p a", a=1))
            small(freq[:, :], A["rope_freq"].partition_broadcast(P))
            for i, name in enumerate(("lambda_q1", "lambda_k1", "lambda_q2", "lambda_k2")):
                small(lamb[:, i, :], A[name][0].partition_broadcast(P))
            small(sink[:, :], A["sinks"][0].partition_broadcast(P))
            small(gdiff[:, :], A["g_diff"][0].partition_broadcast(P))
            small(gateb[:, :], A["nsa_gate_b_2"][0].partition_broadcast(P))
            for i in range(2):
                small(w2s[:, 0, i * HD:(i + 1) * HD], A["nsa_cmp_w2_2"][0, 0])
            small(w2s[:, 1, 0:HD], A["nsa_cmp_w2_2"][0, 1])
            pool.dma_start(gbc[:, :], A["g_final"].partition_broadcast(P)).then_inc(gain_loaded, 16)

            n_set = [0]

            def const(ins, wait=False):
                n_set[0] += 1
                ins.then_inc(consts_set, 1)
                if wait:
                    pool.wait_ge(consts_set, n_set[0])

            const(pool.memset(ident[:, :], 0.0), True)
            const(pool.affine_select(out=ident[:, :], in_=ident[:, :], compare_op=ALU.not_equal, fill=1.0, base=0,
                                     pattern=[[-1, P]], channel_multiplier=1))
            const(pool.memset(ones[:, :], 1.0))
            const(pool.memset(mhalf[:, :], -0.5))
            const(pool.memset(pick[:, :], 0.0), True)
            const(pool.memset(pick[0:2, :], 1.0))
            const(pool.memset(causal[:, :], 0.0))
            const(pool.memset(band[:, :], 0.0))
            const(pool.memset(cmask[:, :, :], 1.0), True)
            const(pool.affine_select(out=causal[:, P:S], in_=causal[:, P:S], compare_op=ALU.is_ge, fill=NEG, base=0,
                                     pattern=[[-1, P]], channel_multiplier=1))
            const(pool.affine_select(out=band[:, P:S], in_=band[:, P:S], compare_op=ALU.is_ge, fill=NEG, base=0,
                                     pattern=[[-1, P]], channel_multiplier=1))
            const(pool.affine_select(out=band[:, 0:P], in_=band[:, 0:P], compare_op=ALU.is_gt, fill=NEG, base=0,
                                     pattern=[[1, P]], channel_multiplier=-1))
            for tt in range(NT):
                const(pool.affine_select(out=cmask[:, tt, :], in_=cmask[:, tt, :], compare_op=ALU.is_ge, fill=0.0,
                                         base=tt * P - 31, pattern=[[-16, NC]], channel_multiplier=1), tt == 1)
            const(pool.tensor_scalar(cneg[:, :, :], cmask[:, :, :], -1.0, -NEG, ALU.add, ALU.mult))
            const(pool.memset(kz[:, :, :], 0.0))
            const(pool.memset(kcz[:, :, :], 0.0), True)
            assert n_set[0] == N_CONST

            def rms(st):
                n = st["n"]
                pool.wait_ge(ss_act, n + 1)
                pool.wait_ge(ss_dve, n + 1)
                g_step(pool.tensor_scalar(ms[:, n % 2, :], ss[:, n, :], 1.0 / st.get("width", D), st["eps"], ALU.mult, ALU.add))
                pool.tensor_tensor(rstd[:, n, :], ms[:, n % 2, :], mhalf[:, 0:NT], ALU.pow).then_inc(rstd_ready, 1)

            n_steps = [0]

            def g_step(ins):
                n_steps[0] += 1
                ins.then_inc(g_done, 1)
                pool.wait_ge(g_done, n_steps[0])

            for st in p.stages:
                if st["kind"] == "scale_x" and st is p.stages[-1]:
                    pool.wait_ge(x_ready, st["need"][1])
                    pool.dma_start(gbc[:, :], A["final_g_2"].partition_broadcast(P)).then_inc(gain_loaded, 16)
                if st["kind"] in ("norm", "scale_x"):
                    rms(st)
                elif st["kind"] == "diff_norm":
                    pool.wait_ge(dn_ss, NT)
                    g_step(pool.tensor_scalar(dss[:, 1, :], dss[:, 0, :], 1.0 / P, 1e-5, ALU.mult, ALU.add))
                    pool.tensor_tensor(dss[:, 2, :], dss[:, 1, :], mhalf[:, 0:8], ALU.pow).then_inc(dn_r, 1)
                elif st["kind"] == "attend" and st["which"] == "mla":
                    pool.wait_ge(s_ready, st["groups"][-1]["g"] + 1)
                    g_step(pool.memset(vcb, 0.0))
                    g_step(pool.memset(kz[HD:P, 0:8:2, :], 0.0))
                    pool.memset(kz[0:HD, 1:8:2, :], 0.0).then_inc(kz_zero, 1)


_INS = ["x", "mem", "positions", "g_mix", "w_in", "sinks", "lambda_q1", "lambda_k1", "lambda_q2", "lambda_k2",
        "g_diff", "w_out", "g_cross", "g_mem", "w_cq", "w_ckv", "w_co", "g_mlp", "w_up", "w_down", "g_final", "c_2",
        "positions_2", "ada_w_2", "ada_b_2", "norm_g_2", "final_g_2", "ff_w13_2", "ff_w2_2", "hy_w_in_2",
        "hy_conv_w_2", "hy_q_norm_2", "hy_kv_norm_2", "hy_w_uq_2", "hy_w_ukv_2", "hy_w_out_2", "nsa_w_in_2",
        "nsa_cmp_pe_2", "nsa_cmp_w1_2", "nsa_cmp_w2_2", "nsa_gate_b_2", "nsa_w_out_2"]


def kernel(**inputs):
    import concourse.bacc as bacc
    from concourse.bass_utils import run_bass_kernel_spmd

    nc = bacc.Bacc("TRN2", target_bir_lowering=False, num_devices=1)
    arrays = {name: np.ascontiguousarray(inputs[name]) for name in _INS}
    arrays["rope_freq"] = np.array([10000.0 ** (-i / 32) for i in range(32)] + [10000.0 ** (-i / 16) for i in range(16)],
                                   np.float32)
    A = {name: nc.dram_tensor("in_" + name, a.shape, mybir.dt.from_np(a.dtype), kind="ExternalInput").ap()
         for name, a in arrays.items()}
    out = nc.dram_tensor("out", (1, S, D), F32, kind="ExternalOutput").ap()
    build(nc, A, out)
    r = run_bass_kernel_spmd(nc, [{"in_" + name: a for name, a in arrays.items()}], core_ids=[0])
    return r.results[0]["out"]
```

```python
import math
from contextlib import ExitStack

import numpy as np

import concourse.bass as bass
from concourse import mybir

F32 = mybir.dt.float32
F32R = mybir.dt.float32r
I32 = mybir.dt.int32
ALU = mybir.AluOpType
ACT = mybir.ActivationFunctionType
AX = mybir.AxisListType

P = 128
S = 256
NT = S // P
D = 1024
KC = D // P
HD = 64
ROPE_HALF, ROPE_HALF_2 = 32, 16
F1, F2 = 4 * D, 2816
HB1, HB2 = 512, 256
N1, N2 = F1 // HB1, F2 // HB2
UNIT = 2048
RING = 3
LEAD = RING - 1
ADA_W = 512
ADA_N = 9 * D // ADA_W
ADA_POOL = 4
NEG = -1e30
MAGIC = 1.5 * 2.0 ** 23
TWO_PI = 2.0 * math.pi
C1 = 6.28125
C2 = float(np.floor((TWO_PI - C1) * 2.0 ** 21) / 2.0 ** 21)
C3 = TWO_PI - C1 - C2
PI_LOW = 3.1415925
LAM_INIT = 0.8 - 0.6 * math.exp(0.0)
SWA_SCALE = HD ** -0.5
CROSS_SCALE = 256 ** -0.5
MLA_SCALE = 96 ** -0.5
NC = (S - 32) // 16 + 1
G_MIX, G_CROSS, G_MEM, G_MLP, NORM_G, C_COL, Q_NORM, KV_NORM, CONV_W = 0, 8, 16, 24, 32, 80, 88, 90, 91
N_PRM = CONV_W + 12


class Turns:

    def __init__(self):
        self.who = []

    def add(self, who):
        self.who.append(who)
        return len(self.who) - 1

    def emptied(self, engine, n):
        return sum(engine in w for w in self.who[:n + 1])


def at(j, f):
    if isinstance(j, int):
        return f(j)
    step = f(3) - f(2)
    assert f(4) - f(3) == step
    return f(2) if step == 0 else j * step + (f(2) - 2 * step)


class Plan:

    def __init__(self, A):
        self.A = A
        self.T, self.U = Turns(), Turns()
        self.units = []
        self.used = []
        self.w_used = 0
        self.stages = []
        self.groups = []
        self.left = [None] * KC
        self.norms = 0
        self.x_ready = 0
        self.x_event = ("x", 0)
        self.norm_rounds = 0
        self.norm_i = 0
        self.mixed = 0
        self.ada_todo = []
        self.ada_n = 0
        self.ada_open = None
        self.ada_t = None
        self.last_fill = None
        self.n_gates = 0
        self.r_done = 0
        self.keys_turned = []

    def unit(self, ap, a, b, transfers=1):
        self.units.append((ap, a, b, transfers))
        self.used.append(None)
        return len(self.units) - 1

    def mark_w(self, u):
        self.w_used += 1
        self.used[u] = ("w", self.w_used)

    def stage(self, kind, **kw):
        kw["kind"] = kind
        self.stages.append(kw)
        return kw

    def rounds(self, n, who):
        return [self.T.add(w) for w in (who if isinstance(who, (list, tuple)) else [who] * n)]

    def linear(self, w, K, N, dst, name, chunk0=0, gate=None, side=None, ada=0, next_gate=None, tables=False):
        kcs = K // P
        out = []
        wv = w.rearrange("(k p) n -> p k n", p=P)
        for c0 in range(0, N, 512):
            w_ = min(512, N - c0)
            per = kcs if kcs * w_ <= UNIT else 4
            mods = self.ada_start() if ada > len(out) // 2 and len(out) % 2 == 0 else []
            fills = [self.U.add("D" if dst == "x" else "A") for _ in range(NT)]
            parts = []
            for k0 in range(0, kcs, per):
                u = self.unit(lambda j, k0=k0, c0=c0, w_=w_, per=per: wv[:, k0:k0 + per, c0:c0 + w_], per, w_)
                parts.append((u, k0, per))
                if k0 + per < kcs:
                    self.mark_w(u)
            self.used[parts[-1][0]] = ("u", fills[-1] + 1)
            if tables and len(out) == 2:
                mods = mods + [("tables", {})]
            if next_gate and len(out) == 1:
                mods = self.gate_diag(*next_gate)
            if len(out) % 2:
                mods = mods + self.ada_mid() + self.ada_close()
            if next_gate and len(out) == 2:
                mods = mods + self.gate_rows()
            out.append((c0, w_, parts, fills, mods))
        left = self.left[chunk0:chunk0 + kcs]
        if dst == "x":
            if gate:
                self.x_ready += NT
                self.x_event = ("x", self.x_ready)
            else:
                self.x_event = ("U", fills[-1])
        self.last_fill = fills[-1]
        return self.stage("linear", blocks=out, dst=dst, chunk0=chunk0, name=name, gate=gate, left=left, side=side)

    def norm(self, src, width, scale, shift=None, chunk0=0, eps=1e-6):
        n = self.norms
        self.norms += 1
        r = self.rounds((width // P + 1) // 2, "D")
        lo0 = self.norm_rounds
        self.norm_i += 1
        self.norm_rounds += len(r)
        for c in range(width // P):
            self.left[chunk0 + c] = ("norm", lo0 + c // 2 + 1)
        return self.stage("norm", n=n, src=src, width=width, scale=scale, shift=shift, chunk0=chunk0, eps=eps,
                          rounds=r, lo0=lo0, i=self.norm_i, need=self.x_event if src == "x" else ("U", self.last_fill))

    def gate_diag(self, layer, m, factor):
        self.n_gates += 1
        self.gate_open = dict(last=self.ada_t, need=self.x_event, diag=self.n_gates,
                              layer=layer, m=m, factor=factor)
        return [("gate_diag", self.gate_open)]

    def gate_rows(self):
        return [("gate", dict(self.gate_open, rounds=self.rounds(2, "D")))]

    def turned(self, kind, n, who, **kw):
        r = self.rounds(n, who)
        self.keys_turned = r[-2:]
        return self.stage(kind, rounds=r, after=self.last_fill, **kw)

    def o_turn(self, c0, c1, ready):
        r = self.rounds((c1 - c0) // 2, "AD")
        for c in range(KC):
            self.left[c] = ("T", r[(c - c0) // 2]) if c >= c0 else ("conv", 1)
        self.stage("o_T", chunk0=c0, rounds=r, ready=ready, fill=self.groups[-1]["fill"])

    def ada_close(self):
        if self.ada_open is None:
            return []
        m, self.ada_open = self.ada_open, None
        out = []
        for half in range(2):
            t = self.T.add("D")
            self.ada_t = t
            out.append(("ada_out", dict(m, half=half, t=t)))
        return out

    def ada_mid(self):
        return [("ada_mid", self.ada_open)] if self.ada_open else []

    def ada_start(self):
        layer, b = self.ada_todo.pop(0)
        m = dict(layer=layer, b=b, n=self.ada_n, prev=self.ada_t, scores=len(self.groups), norms=self.norm_rounds)
        self.ada_n += 1
        self.ada_open = m
        return [("ada_in", m)]

    def mlp(self, kind, w_up, w_down, n, hb, gate, name, ada=()):
        up_v = w_up.rearrange("(k p) n -> p k n", p=P)
        down_v = w_down.rearrange("(k p) n -> p k n", p=P)
        steps = []
        ups, downs = ((3, 3, 2), (2, 1, 1)) if kind == "relu2" else ((4, 4), (2,))
        assert (len(ups) + len(downs)) % RING == 0

        def up_unit(k0, nk):
            rows = up_v[:, k0:k0 + nk, :]
            if kind == "relu2":
                return self.unit(lambda j: rows[:, :, bass.ds(j * hb, hb)], nk, hb)
            both = rows.rearrange("p a (s f) -> p a s f", s=2)
            return self.unit(lambda j: both[:, :, :, bass.ds(j * hb, hb)], nk, 512, 2)

        for j in range(n + 1):
            e = self.ada_start() if j == 0 and j in ada else []

            fills = [self.U.add("D"), self.U.add("D")] if j < n else None
            if j > 0:
                e.append(("hidT", dict(tt=0, t=self.T.add("AD"), fill=steps[-1][0][1])))
            if j == 1 and gate:
                e += self.gate_diag(*gate)
            for i, nk in enumerate(ups):
                if j < n:
                    k0 = sum(ups[:i])
                    u = up_unit(k0, nk)
                    if i < len(ups) - 1:
                        self.mark_w(u)
                    else:
                        self.used[u] = ("u", fills[1] + 1)
                    e.append(("up", dict(k0=k0, nk=nk, u=u, fills=fills)))
                if j > 0 and i == 0:
                    t_last = self.T.add("AD")
                    e.append(("hidT", dict(tt=1, t=t_last, fill=steps[-1][0][1])))
                    e += self.ada_mid()
            if j == 1 and gate:
                e += self.gate_rows()
            closing = self.ada_close() if 0 < j < n else []
            e += self.ada_start() if 0 < j and j in ada else []
            for i, nk in enumerate(downs if j else ()):
                if kind == "relu2" and i == 0:
                    e, closing = e + closing, []
                k0 = sum(downs[:i])
                u = self.unit(lambda j, k0=k0, nk=nk: down_v[:, bass.ds((j - 1) * (hb // P) + k0, nk), :], nk, D)
                if j == n and i == len(downs) - 1:
                    self.w_used += 3
                self.mark_w(u)
                e.append(("down", dict(k0=k0, nk=nk, u=u, t=t_last, last=i == len(downs) - 1)))
            steps.append([("fills", fills)] + e + closing)
        tail = self.ada_close()
        self.x_ready += NT
        self.x_event = ("x", self.x_ready)
        self.r_done += NT * n
        steps = [s_[1:] for s_ in steps]
        lo = hi = 2
        while hi < n and [e[0] for e in steps[hi]] == [e[0] for e in steps[2]]:
            hi += 1
        hi -= 1
        return self.stage("mlp", mlp=kind, steps=steps, n=n, hb=hb, gate=gate, name=name, lo=lo, hi=hi, tail=tail,
                          acc_ready=self.w_used, left=list(self.left), r0=self.r_done - NT * n)


def make_plan(A):
    p = Plan(A)
    p.ada_todo = ([(0, b) for b in range(15)] + [(1, b) for b in range(9)] + [(0, b) for b in range(15, ADA_N)] +
                  [(1, b) for b in range(9, ADA_N)])
    p.stage("params", rounds=p.rounds(2, "D"))
    p.norm("x", D, ("prm", G_MIX), eps=1e-5)
    p.linear(A["w_in"][0], D, 2304, "z", "w_in", ada=2, tables=True)
    after_in = p.last_fill
    p.norm("mem", D, ("prm", G_MEM), eps=1e-5)
    p.linear(A["w_ckv"][0], D, 2 * D, "zc", "w_ckv", side=after_in, ada=2)
    p.turned("qk1", 7, ["A", "D", "A", "D", "D", "A", "D"])
    p.stage("attend", groups=attention_groups(p, "first"), which="first", turned=list(p.keys_turned), side=None)
    p.stage("diff_norm", fill=p.groups[-1]["fill"])
    p.o_turn(0, 8, "diff")
    p.linear(A["w_out"][0], D, D, "x", "w_out", ada=1)
    p.norm("x", D, ("prm", G_CROSS), eps=1e-5)
    p.linear(A["w_cq"][0], D, D, "z", "w_cq", ada=1)
    p.turned("qk_cross", 8, ["A", "D"] * 4)
    p.stage("attend", groups=attention_groups(p, "cross"), which="cross", turned=list(p.keys_turned), side=None)
    p.o_turn(0, 8, "U")
    p.linear(A["w_co"][0], D, D, "x", "w_co", ada=1)
    p.norm("x", D, ("prm", G_MLP), eps=1e-5)
    p.mlp("relu2", A["w_up"][0], A["w_down"][0], N1, HB1, None, "mlp", ada=range(N1 - 1))
    p.stage("scale_x", n=p.norms, need=p.x_event, turn=len(p.T.who), eps=1e-5)
    p.norms += 1
    p.x_ready += NT
    p.x_event = ("x", p.x_ready)
    for layer in range(2):
        p.stage("mod_cols", layer=layer, k=0, last=p.ada_t)
        p.norm("x", D, ("mod", 0), (layer, 0))
        p.mlp("swiglu", A["ff_w13_2"][layer, 0], A["ff_w2_2"][layer, 0], N2, HB2, (layer, 2, 0.5), f"ff{layer}0",
              ada=range(N2 - 1) if layer == 0 else (0, N2 - 3, N2 - 2))
        p.stage("mod_cols", layer=layer, k=1, last=p.ada_t)
        p.norm("x", D, ("mod", 1), (layer, 3))
        if layer == 0:
            p.linear(A["hy_w_in_2"][0], D, 1952, "z", "hy_in", ada=2, next_gate=(layer, 5, 1.0))
            p.norm("cq", 256, ("prm", Q_NORM), chunk0=4)
            p.norm("ckv", 128, ("prm", KV_NORM), chunk0=6)
            p.turned("conv_T", 6, ["A", "D"] * 3)
            conv_turned = list(p.keys_turned)
            p.linear(A["hy_w_uq_2"][0], 256, 768, "z", "uq", chunk0=4)
            p.linear(A["hy_w_ukv_2"][0], 128, 1024, "z768", "ukv", chunk0=6)
            p.stage("mla_pack", after=p.last_fill)
            p.turned("qk_mla", 8, ["A", "D"] * 4)
            p.stage("attend", groups=attention_groups(p, "mla"), which="mla", turned=list(p.keys_turned),
                    side=conv_turned)
            p.stage("conv")
            p.o_turn(4, 8, "U")
            p.linear(A["hy_w_out_2"][0], D, D, "x", "hy_out", gate=True, ada=1)
        else:
            p.linear(A["nsa_w_in_2"][0], D, 1840, "z", "nsa_in", ada=2, next_gate=(layer, 5, 1.0))
            qk = p.turned("qk_nsa", 7, ["A", "D", "A", "D", "A", "D", "A"])
            us = []
            for kv in range(2):
                w1 = A["nsa_cmp_w1_2"][0, kv].rearrange("(c p) n -> p c n", p=P)
                us.append(p.unit(lambda j, w1=w1: w1, 16, P))
            r = p.rounds(6, list("AADDDD"))
            for kv in range(2):
                p.used[us[kv]] = ("t", r[kv] + 1)
            p.stage("compress", units=us, rounds=r, after=p.last_fill, turned=qk["rounds"])
            p.keys_turned += r
            p.stage("attend", groups=attention_groups(p, "nsa"), which="nsa", turned=list(p.keys_turned), side=None)
            p.o_turn(0, 8, "nsa")
            p.linear(A["nsa_w_out_2"][0], D, D, "x", "nsa_out", gate=True, ada=1)
        p.stage("mod_cols", layer=layer, k=2, last=p.ada_t)
        p.norm("x", D, ("mod", 2), (layer, 6))
        p.mlp("swiglu", A["ff_w13_2"][layer, 1], A["ff_w2_2"][layer, 1], N2, HB2, (layer, 8, 0.5), f"ff{layer}1",
              ada=(0, N2 - 3, N2 - 2) if layer == 0 else ())
    p.stage("scale_x", n=p.norms, need=p.x_event, turn=len(p.T.who), eps=1e-6)
    p.norms += 1
    assert not p.ada_todo
    return p


def attention_groups(p, which):
    spec = []
    if which == "first":
        for t in range(NT):
            spec += [dict(kind="swa", t=t, h0=h, nh=4) for h in (0, 4)]
        for t in range(NT):
            spec += [dict(kind="diff", t=t, h0=h, nh=4) for h in (0, 2)]
    elif which == "cross":
        spec = [dict(kind="cross", t=t, h0=h, nh=2) for t in range(NT) for h in (0, 2)]
    elif which == "mla":
        spec = [dict(kind="mla", t=t, h0=h, nh=4) for t in range(NT) for h in (0, 4)]
    else:
        for br in (0, 1):
            spec += [dict(kind="nsa", br=br, t=t, h0=h, nh=4) for t in range(NT) for h in (0, 4, 8, 12)]
        spec += [dict(kind="cmp", t=t, h0=h, nh=8) for t in range(NT) for h in (0, 8)]
    first = len(p.groups)
    for i, g in enumerate(spec):
        g["g"] = first + i
        g["nk"] = S if g["kind"] == "cross" else (NC if g["kind"] == "cmp" else (g["t"] + 1) * P)
        nkc = 1 if g["kind"] == "cmp" else g["nk"] // P
        heads = {"diff": [0, 2], "cmp": [0, 1]}.get(g["kind"], list(range(g["nh"])))
        g["turn"] = [(h, kc) for h in heads for kc in range(nkc)]
        g["nkc"] = nkc
    p.groups += spec
    for i in range(len(spec) + 2):
        if 1 <= i <= len(spec):
            g = spec[i - 1]
            n = (len(g["turn"]) + 3) // 4
            g["rounds"] = [p.T.add("A") for k in range(n)]
            if g["kind"] in ("diff", "cmp"):
                p.mixed += 1
                g["mixed"] = p.mixed
        if i >= 2:
            spec[i - 2]["fill"] = p.U.add("D")
    return spec


def build(nc, A, out):
    p = make_plan(A)
    ctx = ExitStack()
    with ctx:
        def sb(name, shape, dt=F32):
            return ctx.enter_context(nc.sbuf_tensor(name, [P] + shape, dt))

        def sem(name):
            return ctx.enter_context(nc.semaphore(name))

        raw = sb("raw", [RING, UNIT])
        whi = sb("whi", [RING, UNIT], F32R)
        wlo = sb("wlo", [RING, UNIT], F32R)
        x = sb("x", [NT, D])
        xn = sb("xn", [NT, D])
        aT = sb("aT", [KC, S], F32R)
        aTl = sb("aTl", [KC, S], F32R)
        hT = sb("hT", [4, S], F32R)
        hTl = sb("hTl", [4, S], F32R)
        z = sb("z", [NT, 2304])
        zc = sb("zc", [NT, 2048])
        qT = sb("qT", [8, S])
        kz = sb("kz", [12, S])
        sp = sb("sp", [2, 1024])
        pT = sb("pT", [2, 8, P])
        tmp = sb("tmp", [2, 512])
        gbc = sb("gbc", [D])
        prow = sb("prow", [4, P])
        prm_rows, ab_rows, pe_rows = prow[:, 0, :], prow[:, 1:3, :], prow[:, 3, :]
        asum = prow[:, :, :].rearrange("p a b -> p (a b)")
        ident = sb("ident", [P])
        ones = sb("ones", [P])
        causal = sb("causal", [S])
        band = sb("band", [S])
        cmask = sb("cmask", [NT, NC])
        cneg = sb("cneg", [NT, NC])
        prm = sb("prm", [N_PRM])
        prm2 = sb("prm2", [176])
        mod = sb("mod", [2, 72])
        msc = sb("msc", [3, 8])
        cact = sb("cact", [KC])
        lamb = sb("lamb", [4, HD])
        lam2 = sp[:, 0, 256:256 + 2 * HD].rearrange("p (a b) -> p a b", b=HD)
        lam = sb("lam", [4])
        sink = sb("sink", [8])
        nsink = sb("nsink", [8])
        gdiff = sb("gdiff", [P])
        gateb = sb("gateb", [48])
        gates = sb("gates", [NT, 48])
        pos = sb("pos", [2, NT], I32)
        posf = sb("posf", [2, NT])
        freq = sb("freq", [48])
        ang, kk = [sp[:, i, 0:192].rearrange("p (a b c) -> p a b c", a=2, b=NT) for i in range(2)]
        trig = sb("trig", [2, NT, 48])
        ss = sb("ss", [p.norms, NT])
        ms = sb("ms", [2, NT])
        rstd = sb("rstd", [p.norms, NT])
        mhalf = sb("mhalf", [8])
        dss = sb("dss", [3, 8])
        rmax = sb("rmax", [3, 8])
        negm = sb("negm", [3, 8])
        dsk = sb("dsk", [3, 2, 4])
        sums = sb("sums", [3, 8])
        rinv = sb("rinv", [3, 8])
        rg = sb("rg", [3, 8])
        w2s = sb("w2s", [2, P])
        hidc = sb("hidc", [2, 32])
        hid_rows = sb("hid_rows", [2, P])
        kcz = sb("kcz", [2, 2 * NC])
        vcb = kz[:, 10:12, :]
        R, Rl = [[t[:, 2 * kv:2 * kv + 2, :].rearrange("p a (b c) -> p (a b) c", c=32) for kv in range(2)]
                 for t in (hT, hTl)]
        Rf = [tmp[:, kv, :].rearrange("p (a b) -> p a b", b=32) for kv in range(2)]

        ps = ctx.enter_context(nc.psum_tensor("ps", [P, 8, 512], F32))
        ACC = ps[:, 0:4, :]

        def ubank(n):
            return ps[:, 4 + n % 2, :]

        def tbank(n):
            return ps[:, 6 + n % 2, :]

        def sbank(g):
            return ps[:, 2 * (g % 2):2 * (g % 2) + 2, :].rearrange("p a b -> p (a b)")

        w_raw = [sem(f"w_raw{i}") for i in range(RING)]
        w_hi, w_lo, w_used = sem("w_hi"), sem("w_lo"), sem("w_used")
        ada_loaded, ada_sum = [sem(f"ada_loaded{i}") for i in range(2)], sem("ada_sum")
        ada_mid = sem("ada_sum_vector")
        t_ready, t_act, t_dve = sem("t_ready"), sem("t_act"), sem("t_dve")
        u_ready, u_act, u_dve = sem("u_ready"), sem("u_act"), sem("u_dve")
        x_loaded, mem_loaded, small_loaded = sem("x_loaded"), sem("mem_loaded"), sem("small_loaded")
        prm_loaded, gain_loaded = sem("prm_loaded"), sem("gain_loaded")
        consts_set = sem("consts_set")
        cact_ready, trig_ready, ang_ready = sem("cact_ready"), sem("trig_ready"), sem("ang_ready")
        lam_sums, lam_exps = sem("lam_sums"), sem("lam_exps")
        ss_act, ss_dve, rstd_ready = sem("ss_act"), sem("ss_dve"), sem("rstd_ready")
        xn_act, xn_dve = sem("xn_act"), sem("xn_dve")
        nhi_ready, nlo_ready = sem("norm_hi_ready"), sem("norm_lo_ready")
        x_ready = sem("x_ready")
        z_roped, v_done, g_done = sem("z_roped"), sem("vector_steps"), sem("pool_steps")
        s_ready, s_taken, m_ready = sem("scores_ready"), sem("scores_taken"), sem("max_ready")
        p_ready, p_mixed, o_stored = sem("probs_ready"), sem("probs_mixed"), sem("o_stored")
        r_ready = sem("act_part_ready")
        dn_ss, dn_r, dn_done = sem("diff_ss"), sem("diff_rstd"), sem("diff_normed")
        diag_ready = sem("diag_ready")
        conv_y, conv_hi = sem("conv_y"), sem("conv_hi")
        conv_done, packed, kz_zero = sem("conv_done"), sem("packed"), sem("kz_zero")
        cmp_r, cmp_rhi, cmp_rlo = sem("cmp_rows"), sem("cmp_rows_hi"), sem("cmp_rows_lo")
        gl_ready, gates_ready, out_ready, stored = sem("gate_logits"), sem("gates_ready"), sem("out_ready"), sem("stored")

        T, U = p.T, p.U

        def wait_used(eng, u, j):
            kind = p.used[u(j if isinstance(j, int) else 2)][0]
            eng.wait_ge({"w": w_used, "u": u_ready, "t": t_ready}[kind], at(j, lambda j: p.used[u(j)][1]))

        def wait_emptied(eng, turns, n, j=0):
            n_ = n(j if isinstance(j, int) else 2)
            for who, s in (("A", t_act if turns is T else u_act), ("D", t_dve if turns is T else u_dve)):
                if who in turns.who[n_]:
                    eng.wait_ge(s, at(j, lambda j: turns.emptied(who, n(j))))

        def wait_free(eng, turns, n, j=0):
            if not isinstance(j, int) or n(j) >= 2:
                wait_emptied(eng, turns, lambda j: n(j) - 2, j)

        def wait_x(eng, need, tt=1):
            if need[0] == "U":
                wait_emptied(eng, U, lambda j: need[1] - 1 + tt)
            elif need[1] == 0:
                eng.wait_ge(x_loaded, 16)
            else:
                eng.wait_ge(x_ready, need[1] - 1 + tt)

        def run_steps(eng, st, body):
            for j in range(st["lo"]):
                body(j)
            with eng.Fori(st["lo"], st["hi"]) as j:
                body(j)
            for j in range(st["hi"], st["n"] + 1):
                body(j)

        def events(st, j):
            j_ = j if isinstance(j, int) else st["lo"]
            for k, (what, e) in enumerate(st["steps"][j_]):
                yield what, e, (lambda jj, k=k: st["steps"][jj][k][1])

        def src_of(st):
            return {"x": x[:, :, :], "mem": zc[:, :, 0:D], "cq": z[:, :, 1536:1792], "ckv": z[:, :, 1792:1920]}[st["src"]]

        def norm_dst(st):
            return {"cq": xn[:, :, 0:256], "ckv": xn[:, :, 256:384]}.get(st["src"], xn[:, :, :])

        zcf = zc[:, :, :].rearrange("p t (a b) -> p (t a) b", b=S)
        kfull = xn[:, :, 0:768]

        third = {"swa": z[:, 0, 768:1792], "diff": z[:, 0, 768:1792], "mla": zc[:, 1, 1024:2048]}

        def probs(g):
            n = g["g"] % 3
            return sp[:, n, :] if n < 2 else third.get(g["kind"], z[:, 0, 0:1024])

        def hid(tt):
            return sp[:, tt, 0:512]

        def part(tt):
            return sp[:, tt, 512:1024]

        def flat(t):
            t = t if len(t.shape) < 4 else t[:, :, :, :]
            return t.rearrange("p k t f -> p (k t f)") if len(t.shape) == 4 else t.rearrange("p t f -> p (t f)")

        def view(bank, like):
            return bank.rearrange("p (a b) -> p a b", b=like.shape[-1]) if len(like.shape) == 3 else bank

        def wait_src(eng, st, tt):
            if st["src"] == "mem":
                eng.wait_ge(mem_loaded, 16)
            else:
                wait_x(eng, st["need"], tt if st["src"] == "x" else 1)

        def transposes(st):
            items, dst = [], []

            def pair(src, c0, to):
                items.append([(src[:, tt, c0 + k * P:c0 + (k + 1) * P], k * S + tt * P, P)
                              for k in range(2) for tt in range(NT)])
                if to is not None:
                    dst.append([(to, 0, P, 0, 512)])

            def shared_keys(c0, k0):
                items.append([(z[:, tt, c0:c0 + P], tt * P, P) for tt in range(NT)])
                dst.append([(kz[HD * (i % 2):HD * (i % 2) + HD, k0 + i:k0 + i + 1, :], HD * (i // 2), HD, 0, S)
                            for i in range(4)])

            kind = st["kind"]
            if kind == "qk1":
                for r in range(4):
                    pair(z, 256 * r + (0 if r < 2 else 256), qT[:, 2 * r:2 * r + 2, :])
                shared_keys(512, 0)
                for r in range(2):
                    pair(z, 1280 + 256 * r, None)
                    dst.append([(kz[HD * c:HD * c + HD, 4 + 4 * r + c:4 + 4 * r + c + 3:2, :], HD * c, HD, 0, 512)
                                for c in range(2)])
            elif kind == "qk_cross":
                for r in range(4):
                    pair(z, 256 * r, qT[:, 2 * r:2 * r + 2, :])
                for r in range(4):
                    pair(zc, 256 * r, kz[:, 2 * r:2 * r + 2, :])
            elif kind == "conv_T":
                for r in range(6):
                    pair(z, 256 * r, zcf[:, 2 * r:2 * r + 2, :])
            elif kind == "qk_mla":
                for src, to in ((z, qT), (kfull, kz)):
                    for r in range(4):
                        items.append([(src[:, tt, (2 * r + k) * 96:(2 * r + k + 1) * 96], k * S + tt * P, P)
                                      for k in range(2) for tt in range(NT)])
                        dst.append([(to[0:96, 2 * r:2 * r + 2, :], 0, 96, 0, 512)])
            elif kind == "qk_nsa":
                for r in range(4):
                    pair(z, 256 * r, qT[:, 2 * r:2 * r + 2, :])
                pair(z, 1024, kz[:, 8:10, :])
                shared_keys(1280, 0)
                shared_keys(1536, 4)
            elif kind == "o_T":
                for r in range(len(st["rounds"])):
                    pair(xn, 256 * r + P * st["chunk0"], None)
            return items, dst

        arrived, count = [], [0] * RING
        for u, (_, _, _, transfers) in enumerate(p.units):
            count[u % RING] += 16 * transfers
            arrived.append(count[u % RING])

        def words(u, j):
            _, a, b, _ = p.units[u(j if isinstance(j, int) else 2)]
            return a * b

        def split_hi(act, u, j=0):
            if isinstance(j, int) and u(j) >= len(p.units):
                return
            slot = u(j if isinstance(j, int) else 2) % RING
            act.wait_ge(w_raw[slot], at(j, lambda j: arrived[u(j)]))
            if not isinstance(j, int) or u(j) >= RING:
                wait_used(act, lambda j: u(j) - RING, j)
            m = words(u, j)
            act.activation(whi[:, slot, 0:m], raw[:, slot, 0:m], ACT.Copy).then_inc(w_hi, 1)

        def split_lo(dve, u, j=0):
            if isinstance(j, int) and u(j) >= len(p.units):
                return
            slot = u(j if isinstance(j, int) else 2) % RING
            dve.wait_ge(w_hi, at(j, lambda j: u(j) + 1))
            m = words(u, j)
            dve.tensor_tensor(wlo[:, slot, 0:m], raw[:, slot, 0:m], whi[:, slot, 0:m].bitcast(F32),
                              ALU.subtract).then_inc(w_lo, 1)

        araw = [t.rearrange("p a b -> p (a b)").rearrange("p (a b) -> p a b", b=ADA_W)
                for t in (qT[:, :, :], pT[:, :, :, :].rearrange("p a b c -> p (a b) c"))]

        def ada_count(n, q):
            return 2 * ADA_POOL * n + 2 * q + 1

        N_PRM_DMA, N_SMALL, N_CONST = 12, 15, 15

        block = ctx.enter_context(nc.Block())

        @block.sync
        def _(sy):
            sy.dma_start(x[:, :, :], A["x"][0].rearrange("(t p) d -> p t d", p=P)).then_inc(x_loaded, 16)

            def load(u, arg, j=0):
                u_ = u(j if isinstance(j, int) else 2)
                src, a, b, _ = p.units[u_]
                slot = u_ % RING
                if not isinstance(j, int) or u_ >= RING:
                    sy.wait_ge(w_lo, at(j, lambda j: u(j) - RING + 1))
                dst = raw[:, slot, 0:a * b].rearrange("p (a b) -> p a b", a=a)
                ap = src(arg)
                if len(ap.shape) == 4:
                    dst = dst.rearrange("p a (s f) -> p a s f", s=2)
                    for s in range(2):
                        sy.dma_start(dst[:, :, s, :], ap[:, :, s, :]).then_inc(w_raw[slot], 16)
                else:
                    sy.dma_start(dst, ap).then_inc(w_raw[slot], 16)

            for st in p.stages:
                if st["kind"] == "linear":
                    for _, _, parts, _, _ in st["blocks"]:
                        for u, _, _ in parts:
                            load(lambda j: u, None)
                elif st["kind"] == "compress":
                    for u in st["units"]:
                        load(lambda j: u, None)
                elif st["kind"] == "mlp":
                    def body(j):
                        for what, e, get in events(st, j):
                            if what in ("up", "down"):
                                load(lambda j: get(j)["u"], j, j)
                    run_steps(sy, st, body)
            for tt in range(NT):
                sy.wait_ge(out_ready, tt + 1)
                sy.dma_start(out[0].rearrange("(t p) d -> p t d", p=P)[:, tt], xn[:, tt]).then_inc(stored, 16)
            sy.wait_ge(stored, 16 * NT)

        @block.tensor
        def _(pe):
            def three(out_ap, hi, lo, w, wl, start, stop):
                pe.matmul(out_ap, hi, w, start=start, stop=False)
                pe.matmul(out_ap, lo, w, start=False, stop=False)
                return pe.matmul(out_ap, hi, wl, start=False, stop=stop)

            def turn(t, items, rows=P):
                wait_free(pe, T, lambda j: t)
                for k, (src, col, kp) in enumerate(items):
                    m = src.shape[-1]
                    last = pe.transpose(tbank(t)[0:m, col:col + kp], src, ident[0:kp, 0:kp])
                last.then_inc(t_ready, 1)

            def use(u, j=0):
                pe.wait_ge(w_lo, at(j, lambda j: u(j) + 1))

            def params(st):
                pe.wait_ge(prm_loaded, 16 * N_PRM_DMA)
                pe.wait_ge(consts_set, N_CONST)
                turn(st["rounds"][0], [(prm_rows[0:N_PRM, :], 0, N_PRM)])
                turn(st["rounds"][1], [(ab_rows[0:72, 0, :], 0, 72), (ab_rows[0:72, 1, :], 72, 72),
                                       (pe_rows[0:32, :], 144, 32)])

            def norm(st):
                n, nch = st["n"], st["width"] // P
                dst = norm_dst(st)

                def some(r, tt):
                    for k in range(min(2, nch - 2 * r)):
                        last = pe.transpose(tbank(st["rounds"][r])[:, k * S + tt * P:k * S + (tt + 1) * P],
                                            dst[:, tt, (2 * r + k) * P:(2 * r + k + 1) * P], ident[:, :])
                    return last

                pe.wait_ge(xn_act, st["i"])
                early = range(min(2, len(st["rounds"])))
                for r in early:
                    wait_free(pe, T, lambda j: st["rounds"][r])
                    some(r, 0)
                pe.wait_ge(xn_dve, st["i"])
                for r, t in enumerate(st["rounds"]):
                    if r not in early:
                        wait_free(pe, T, lambda j: t)
                        some(r, 0)
                    some(r, 1).then_inc(t_ready, 1)

            def wait_left(st, k):
                if k and st["left"][k] == st["left"][k - 1]:
                    return
                kind, n = st["left"][k]
                if kind == "norm":
                    pe.wait_ge(nlo_ready, n)
                elif kind == "T":
                    wait_emptied(pe, T, lambda j: n)
                else:
                    pe.wait_ge(conv_done, n)

            def linear(st):
                c0 = st["chunk0"]
                for n0, w, parts, fills, mods in st["blocks"]:
                    for i, (u, k0, per) in enumerate(parts):
                        use(lambda j: u)
                        wv = whi[:, u % RING, 0:per * w].rearrange("p (a b) -> p a b", a=per)
                        wl = wlo[:, u % RING, 0:per * w].rearrange("p (a b) -> p a b", a=per)
                        for tt in range(NT):
                            if i == 0:
                                wait_free(pe, U, lambda j: fills[tt])
                            for k in range(per):
                                kc = c0 + k0 + k
                                if n0 == 0 and tt == 0:
                                    wait_left(st, k0 + k)
                                last = three(ubank(fills[tt])[:, 0:w], aT[:, kc, tt * P:(tt + 1) * P],
                                             aTl[:, kc, tt * P:(tt + 1) * P], wv[:, k], wl[:, k],
                                             i == 0 and k == 0, i == len(parts) - 1 and k == per - 1)
                            if i == len(parts) - 1:
                                last.then_inc(u_ready, 1)
                        if i < len(parts) - 1:
                            last.then_inc(w_used, 1)
                    ada_outs(mods)

            def ada_out(m, j=0):
                m_ = m(j if isinstance(j, int) else 2)
                pe.wait_ge(ada_sum, at(j, lambda j: ada_count(m(j)["n"], ADA_POOL - 1) + 1))
                wait_free(pe, T, lambda j: m(j)["t"], j)
                for c in range(2):
                    k = 2 * m_["half"] + c
                    last = pe.matmul(tbank(m_["t"])[:, c:c + 1], asum[:, k * P:(k + 1) * P], ones[:, 0:1],
                                     start=True, stop=True)
                last.then_inc(t_ready, 1)

            def ada_outs(mods):
                for what, m in mods:
                    if what == "ada_out":
                        ada_out(lambda j: m)
                    elif what == "gate":
                        gate(m)

            def mlp(st):
                hb = st["hb"]

                def body(j):
                    for what, e, get in events(st, j):
                        if what == "hidT":
                            tt = e["tt"]
                            wait_emptied(pe, U, lambda j: get(j)["fill"][tt], j)
                            wait_free(pe, T, lambda j: get(j)["t"], j)
                            for c in range(hb // P):
                                last = pe.transpose(tbank(e["t"])[:, c * P:(c + 1) * P],
                                                    hid(tt)[:, c * P:(c + 1) * P], ident[:, :])
                            last.then_inc(t_ready, 1)
                        elif what == "up":
                            slot, end = e["u"] % RING, e["k0"] + e["nk"] == KC
                            use(lambda j: get(j)["u"], j)
                            wv = whi[:, slot, 0:e["nk"] * 512].rearrange("p (a b) -> p a b", b=512)
                            wl = wlo[:, slot, 0:e["nk"] * 512].rearrange("p (a b) -> p a b", b=512)
                            for tt in range(NT):
                                if e["k0"] == 0:
                                    wait_free(pe, U, lambda j: get(j)["fills"][tt], j)
                                for c in range(e["nk"]):
                                    kc = e["k0"] + c
                                    if isinstance(j, int) and j == 0 and tt == 0:
                                        wait_left(st, kc)
                                    last = three(ubank(e["fills"][tt]), aT[:, kc, tt * P:(tt + 1) * P],
                                                 aTl[:, kc, tt * P:(tt + 1) * P], wv[:, c], wl[:, c],
                                                 kc == 0, kc == KC - 1)
                                if end:
                                    last.then_inc(u_ready, 1)
                            if not end:
                                last.then_inc(w_used, 1)
                        elif what == "down":
                            slot = e["u"] % RING
                            use(lambda j: get(j)["u"], j)
                            wait_emptied(pe, T, lambda j: get(j)["t"], j)
                            wv = whi[:, slot, 0:e["nk"] * D].rearrange("p (a b) -> p a b", b=D)
                            wl = wlo[:, slot, 0:e["nk"] * D].rearrange("p (a b) -> p a b", b=D)
                            first = isinstance(j, int) and j == 1 and e["k0"] == 0
                            final = isinstance(j, int) and j == st["n"] and e["last"]
                            order = [(c, bank) for c in range(e["nk"]) for bank in range(4)]
                            if final:
                                order.sort(key=lambda cb: cb[1])
                            for c, bank in order:
                                tt, nb, kc = bank // 2, bank % 2, e["k0"] + c
                                last = three(ACC[:, bank, :], hT[:, kc, tt * P:(tt + 1) * P],
                                             hTl[:, kc, tt * P:(tt + 1) * P], wv[:, c, nb * 512:(nb + 1) * 512],
                                             wl[:, c, nb * 512:(nb + 1) * 512], first and c == 0,
                                             final and c == e["nk"] - 1)
                                if final and c == e["nk"] - 1 and bank < 3:
                                    last.then_inc(w_used, 1)
                            last.then_inc(w_used, 1)
                        elif what == "ada_out":
                            ada_out(get, j)
                        elif what == "gate":
                            gate(e)
                run_steps(pe, st, body)
                ada_outs(st["tail"])

            def turns_of(st):
                kind = st["kind"]
                if kind == "qk1":
                    pe.wait_ge(z_roped, 2)
                elif kind == "qk_mla":
                    pe.wait_ge(packed, 1)
                elif kind == "o_T":
                    if st["ready"] == "diff":
                        pe.wait_ge(dn_done, NT)
                    elif st["ready"] == "nsa":
                        pe.wait_ge(o_stored, sum(g["kind"] == "cmp" or g.get("br") == 1 for g in p.groups))
                    else:
                        wait_emptied(pe, U, lambda j: st["fill"])
                else:
                    wait_emptied(pe, U, lambda j: st["after"])
                for t, items in zip(st["rounds"], transposes(st)[0]):
                    turn(t, items)

            def attend(st):
                gs = st["groups"]
                for t in st["turned"]:
                    wait_emptied(pe, T, lambda j: t)
                if st["which"] == "nsa":
                    pe.wait_ge(kz_zero, 1)

                def scores(g):
                    n = g["g"]
                    if n >= 2:
                        pe.wait_ge(s_taken, n - 1)
                    nk, t, h0, kind = g["nk"], g["t"], g["h0"], g["kind"]
                    q = slice(t * P, (t + 1) * P)
                    if kind == "cmp":
                        sv = sbank(n)[:, 0:8 * 32].rearrange("p (h k) -> p h k", k=32)
                        for i in range(4):
                            last = pe.matmul(sv[:, 2 * i:2 * i + 2, 0:NC], qT[:, h0 // 2 + i, q],
                                             kcz[:, h0 // 8, :].rearrange("p (h k) -> p h k", k=NC),
                                             start=True, stop=True)
                    else:
                        sv = sbank(n).rearrange("p (h k) -> p h k", k=S)
                        if kind == "cross":
                            for i in range(2):
                                for c in range(2):
                                    last = pe.matmul(sv[:, i, :], qT[:, 2 * (h0 + i) + c, q], kz[:, 2 * (h0 + i) + c, :],
                                                     start=c == 0, stop=c == 1)
                        elif kind == "mla":
                            for i in range(4):
                                last = pe.matmul(sv[:, i, 0:nk], qT[0:96, h0 + i, q], kz[0:96, h0 + i, 0:nk],
                                                 start=True, stop=True)
                        else:
                            for i in range(2):
                                if kind == "swa":
                                    qc, k0 = h0 // 2 + i, 2 * (h0 // 4)
                                elif kind == "diff":
                                    qc, k0 = 4 + h0 + i, 4 + 2 * (h0 + i)
                                else:
                                    qc, k0 = h0 // 2 + i, 4 * g["br"] + 2 * (h0 // 8)
                                last = pe.matmul(sv[:, 2 * i:2 * i + 2, 0:nk], qT[:, qc, q], kz[:, k0:k0 + 2, 0:nk],
                                                 start=True, stop=True)
                    last.then_inc(s_ready, 1)

                def turn_probs(g):
                    n = g["g"]
                    if g["kind"] in ("diff", "cmp"):
                        pe.wait_ge(p_mixed, g["mixed"])
                    else:
                        pe.wait_ge(p_ready, n + 1)
                    for r, t in enumerate(g["rounds"]):
                        items = []
                        for k, (h, kc) in enumerate(g["turn"][4 * r:4 * r + 4]):
                            if g["kind"] == "cmp":
                                src = probs(g)[:, h * P:(h + 1) * P]
                            else:
                                src = probs(g)[:, h * S + kc * P:h * S + (kc + 1) * P]
                            items.append((src, k * P, P))
                        turn(t, items)

                def values(g):
                    n, t, h0, kind, f = g["g"], g["t"], g["h0"], g["kind"], g["fill"]
                    for tr in g["rounds"]:
                        wait_emptied(pe, T, lambda j: tr)
                    wait_free(pe, U, lambda j: f)
                    o = ubank(f)
                    if kind == "cmp":
                        for k in range(2):
                            last = pe.matmul(o[:, k * S:(k + 1) * S], pT[:, n % 2, k, :], vcb[:, h0 // 8, :],
                                             start=True, stop=True)
                        last.then_inc(u_ready, 1)
                        return
                    heads = [h for h, kc in g["turn"] if kc == 0]
                    for i, h in enumerate(heads):
                        if kind == "swa":
                            dv, v0, zt = HD, 640 + HD * (h0 // 4), z
                        elif kind == "diff":
                            dv, v0, zt = P, 1792 + P * (h0 + i), z
                        elif kind == "cross":
                            dv, v0, zt = S, D + S * (h0 + i), zc
                        elif kind == "mla":
                            dv, v0, zt = HD, 768 + P * (h0 + i) + HD, z
                        else:
                            dv, v0, zt = HD, D + 256 * (1 + g["br"]) + P + HD * (h0 // 8), z
                        for kc in range(g["nkc"]):
                            last = pe.matmul(o[:, i * dv:(i + 1) * dv], pT[:, n % 2, i * g["nkc"] + kc, :],
                                             zt[:, kc, v0:v0 + dv], start=kc == 0, stop=kc == g["nkc"] - 1)
                    last.then_inc(u_ready, 1)

                scores(gs[0])
                for i in range(len(gs) + 2):
                    if i + 1 < len(gs):
                        scores(gs[i + 1])
                    if i >= 2:
                        values(gs[i - 2])
                    if 1 <= i <= len(gs):
                        turn_probs(gs[i - 1])

            def gate(st):
                pe.wait_ge(diag_ready, st["diag"])
                for r, t in enumerate(st["rounds"]):
                    wait_free(pe, T, lambda j: t)
                    for c in range(4):
                        last = pe.matmul(tbank(t)[:, c * P:(c + 1) * P], ones[:, :],
                                         tmp[:, r, c * P:(c + 1) * P], start=True, stop=True)
                    last.then_inc(t_ready, 1)

            def compress(st):
                r = st["rounds"]
                for kv in range(2):
                    u = st["units"][kv]
                    pe.wait_ge(cmp_rlo, kv + 1)
                    use(lambda j: u)
                    wait_free(pe, T, lambda j: r[kv])
                    wv = whi[:, u % RING, :].rearrange("p (a b) -> p a b", a=16)
                    wl = wlo[:, u % RING, :].rearrange("p (a b) -> p a b", a=16)
                    for c in range(16):
                        last = three(tbank(r[kv])[0:32, 0:P], R[kv][:, c, :], Rl[kv][:, c, :], wv[:, c], wl[:, c],
                                     c == 0, c == 15)
                    last.then_inc(t_ready, 1)
                for kv in range(2):
                    wait_emptied(pe, T, lambda j: r[kv])
                    turn(r[2 + kv], [(hid_rows[0:32, kv, :], 0, 32)])
                for kv in range(2):
                    t = r[4 + kv]
                    wait_emptied(pe, T, lambda j: r[2 + kv])
                    wait_free(pe, T, lambda j: t)
                    if kv == 0:
                        last = pe.matmul(tbank(t)[:, 0:2 * NC], w2s[:, 0, :], hidc[:, 0, 0:2 * NC], start=True, stop=True)
                    else:
                        for g in range(2):
                            last = pe.matmul(tbank(t)[0:NC, g * HD:(g + 1) * HD], hidc[:, 1, g * NC:(g + 1) * NC],
                                             w2s[:, 1, 0:HD], start=True, stop=True)
                    last.then_inc(t_ready, 1)

            table = dict(params=params, norm=norm, linear=linear, mlp=mlp, qk1=turns_of, qk_cross=turns_of,
                         conv_T=turns_of, qk_mla=turns_of, qk_nsa=turns_of, o_T=turns_of, attend=attend,
                         compress=compress)
            for st in p.stages:
                if st["kind"] in table:
                    table[st["kind"]](st)

        @block.scalar
        def _(act):
            def rows(dst, r0, n, src):
                act.dma_start(dst[r0:r0 + n], src).then_inc(prm_loaded, 16)

            pr = prm_rows
            for r0, name in ((G_MIX, "g_mix"), (G_CROSS, "g_cross"), (G_MEM, "g_mem"), (G_MLP, "g_mlp")):
                rows(pr, r0, 8, A[name][0].rearrange("(a b) -> a b", b=P))
            rows(pr, NORM_G, 48, A["norm_g_2"].rearrange("l i (a b) -> (l i a) b", b=P))
            rows(pr, C_COL, 8, A["c_2"][0].rearrange("(a b) -> a b", b=P))
            rows(pr, Q_NORM, 2, A["hy_q_norm_2"][0].rearrange("(a b) -> a b", b=P))
            rows(pr, KV_NORM, 1, A["hy_kv_norm_2"])
            rows(pr, CONV_W, 12, A["hy_conv_w_2"][0].rearrange("k (a b) -> (k a) b", b=P))
            act.dma_start(pe_rows[0:32, :], A["nsa_cmp_pe_2"][0].rearrange("v (c q) d -> (v c) (q d)", q=2)).then_inc(prm_loaded, 16)
            for l in range(2):
                act.dma_start(ab_rows[0:72, l, :], A["ada_b_2"][l].rearrange("(a b) -> a b", b=P)).then_inc(prm_loaded, 16)
            act.dma_start(zc[:, :, 0:D], A["mem"][0].rearrange("(t p) d -> p t d", p=P)).then_inc(mem_loaded, 16)

            for u in range(LEAD):
                split_hi(act, lambda j: u)

            def params(st):
                wait_emptied(act, T, lambda j: st["rounds"][0])
                act.activation(cact[:, :], prm[:, C_COL:C_COL + KC], ACT.Silu).then_inc(cact_ready, 1)

            def tables():
                act.wait_ge(ang_ready, 1)
                act.activation(trig[:, :, :, :], ang[:, :, :, :], ACT.Sin).then_inc(trig_ready, 1)
                act.wait_ge(lam_sums, 2)
                act.activation(lam[:, 0:2], lam[:, 2:4], ACT.Exp).then_inc(lam_exps, 1)

            def norm(st):
                n, w = st["n"], st["width"]
                src, dst = src_of(st), norm_dst(st)
                wait_src(act, st, 0)
                if st["rounds"][0] > 2:
                    act.wait_ge(t_ready, st["rounds"][0])
                act.activation(dst[:, 0, :], src[:, 0, :], ACT.Square, accum_out=ss[:, n, 0:1]).then_inc(ss_act, 1)
                act.wait_ge(rstd_ready, 2 * n + 1)
                act.activation(dst[:, 0, :], src[:, 0, :], ACT.Copy, scale=rstd[:, n, 0:1]).then_inc(xn_act, 1)
                for r, t in enumerate(st["rounds"]):
                    m = min(2, w // P - 2 * r)
                    wait_emptied(act, T, lambda j: t)
                    k = st["chunk0"] + 2 * r
                    act.activation(aT[:, k:k + m, :].rearrange("p a b -> p (a b)"),
                                   tmp[:, (st["lo0"] + r) % 2, 0:m * S], ACT.Copy).then_inc(nhi_ready, 1)

            def ada_load(m, j=0):
                m_ = m(j if isinstance(j, int) else 2)
                if m_["scores"]:
                    act.wait_ge(s_ready, m_["scores"])
                    act.wait_ge(nlo_ready, m_["norms"])
                if m_["prev"] is not None:
                    act.wait_ge(ada_sum, at(j, lambda j: ada_count(m(j)["n"], 0) - 1))
                wv = A["ada_w_2"][m_["layer"]].rearrange("(k p) n -> p k n", p=P)
                for h in range(2):
                    act.dma_start(araw[h], wv[:, 4 * h:4 * h + 4, bass.ds(at(j, lambda j: m(j)["b"] * ADA_W), ADA_W)]
                                  ).then_inc(ada_loaded[h], 16)

            def linear(st):
                for n0, w, parts, fills, mods in st["blocks"]:
                    for what, m in mods:
                        if what == "ada_in":
                            ada_load(lambda j: m)
                    for u, _, _ in parts:
                        split_hi(act, lambda j: u + LEAD)
                    dst = zc if st["dst"] == "zc" else z
                    off = n0 + (768 if st["dst"] == "z768" else 0)
                    for tt in range(NT if st["dst"] != "x" else 0):
                        act.wait_ge(u_ready, fills[tt] + 1)
                        act.activation(dst[:, tt, off:off + w], ubank(fills[tt])[:, 0:w], ACT.Copy).then_inc(u_act, 1)
                    if ("tables", {}) in mods:
                        tables()

            def mlp(st):
                nk = st["hb"] // P

                def body(j):
                    for what, e, get in events(st, j):
                        if what in ("up", "down"):
                            split_hi(act, lambda j: get(j)["u"] + LEAD, j)
                        if what == "hidT":
                            act.wait_ge(t_ready, at(j, lambda j: get(j)["t"] + 1))
                            act.activation(hT[:, 0:nk, e["tt"] * P:(e["tt"] + 1) * P],
                                           tbank(e["t"])[:, 0:nk * P].rearrange("p (a b) -> p a b", b=P),
                                           ACT.Copy).then_inc(t_act, 1)
                        elif what == "up" and e["k0"] + e["nk"] == KC:
                            for tt in range(NT):
                                act.wait_ge(u_ready, at(j, lambda j: get(j)["fills"][tt] + 1))
                                if not isinstance(j, int) or j > 0:
                                    act.wait_ge(u_dve, at(j, lambda j: U.emptied("D", get(j)["fills"][tt] - 2)))
                                bank = ubank(e["fills"][tt])
                                if st["mlp"] == "relu2":
                                    act.activation(part(tt), bank, ACT.Relu).then_inc(r_ready, 1)
                                else:
                                    act.activation(part(tt)[:, 0:HB2], bank[:, 0:HB2], ACT.Silu).then_inc(r_ready, 1)
                        elif what == "ada_in":
                            ada_load(get, j)
                run_steps(act, st, body)

            def turns_of(st):
                for t, dst in zip(st["rounds"], transposes(st)[1]):
                    if "A" in T.who[t]:
                        act.wait_ge(t_ready, t + 1)
                        for i, (to, r0, n, c0, c1) in enumerate(dst):
                            ins = act.activation(to, view(tbank(t)[r0:r0 + n, c0:c1], to), ACT.Copy)
                        ins.then_inc(t_act, 1)

            def o_T(st):
                for r, t in enumerate(st["rounds"]):
                    k = st["chunk0"] + 2 * r
                    act.wait_ge(t_ready, t + 1)
                    act.activation(aT[:, k:k + 2, :].rearrange("p a b -> p (a b)"), tbank(t), ACT.Copy).then_inc(t_act, 1)

            def exps(g):
                n, kind = g["g"], g["kind"]
                sb_ = n % 3
                act.wait_ge(m_ready, n + 1)
                if kind == "cmp":
                    v = probs(g)[:, 0:S].rearrange("p (h k) -> p h k", k=32)[:, :, 0:NC]
                    act.activation(v, v, ACT.Exp, scale=SWA_SCALE).then_inc(p_ready, 1)
                    return
                scale = {"cross": CROSS_SCALE, "mla": MLA_SCALE}.get(kind, SWA_SCALE)
                if kind == "swa":
                    act.activation(dsk[:, sb_, 1, :], dsk[:, sb_, 0, :], ACT.Exp)
                for h in range(g["nh"]):
                    v = probs(g)[:, h * S:h * S + g["nk"]]
                    ins = act.activation(v, v, ACT.Exp, bias=negm[:, sb_, h:h + 1], scale=scale,
                                         accum_out=sums[:, sb_, h:h + 1])
                ins.then_inc(p_ready, 1)

            def probs_out(g):
                for r, t in enumerate(g["rounds"]):
                    m = len(g["turn"][4 * r:4 * r + 4])
                    act.wait_ge(t_ready, t + 1)
                    act.activation(pT[:, g["g"] % 2, 4 * r:4 * r + m, :].rearrange("p a b -> p (a b)"),
                                   tbank(t)[:, 0:m * P], ACT.Copy).then_inc(t_act, 1)

            def attend(st):
                gs = st["groups"]
                for i in range(len(gs) + 1):
                    if i < len(gs):
                        exps(gs[i])
                    if i >= 1:
                        g = gs[i - 1]
                        if i >= 3:
                            act.wait_ge(u_ready, gs[i - 3]["fill"] + 1)
                        probs_out(g)

            def conv(st):
                act.wait_ge(conv_y, 4)
                act.activation(aT[:, 0:4, :], zcf[:, 4:8, :], ACT.Copy).then_inc(conv_hi, 1)

            def compress(st):
                act.wait_ge(gl_ready, 1)
                act.activation(gates[:, :, :], gates[:, :, :], ACT.Sigmoid).then_inc(gates_ready, 1)
                for kv in range(2):
                    act.wait_ge(cmp_r, kv + 1)
                    act.activation(R[kv][:, :, :], Rf[kv][:, :, :], ACT.Copy).then_inc(cmp_rhi, 1)
                for kv in range(2):
                    split_hi(act, lambda j: st["units"][kv] + LEAD)
                    act.wait_ge(t_ready, st["rounds"][kv] + 1)
                    act.activation(hid_rows[0:32, kv, :], tbank(st["rounds"][kv])[0:32, 0:P], ACT.Silu).then_inc(t_act, 1)

            def scale_x(st):
                n = st["n"]
                wait_x(act, st["need"], 0)
                act.wait_ge(t_ready, st["turn"])
                act.activation(xn[:, 0, :], x[:, 0, :], ACT.Square, accum_out=ss[:, n, 0:1]).then_inc(ss_act, 1)

            table = dict(params=params, norm=norm, linear=linear, mlp=mlp, qk1=turns_of, qk_cross=turns_of,
                         conv_T=turns_of, qk_mla=turns_of, qk_nsa=turns_of, o_T=o_T, attend=attend,
                         conv=conv, compress=compress, scale_x=scale_x)
            for st in p.stages:
                if st["kind"] in table:
                    table[st["kind"]](st)

        @block.vector
        def _(dve):
            steps = [0]

            def step(ins):
                steps[0] += 1
                ins.then_inc(v_done, 1)
                return steps[0]

            def link(ins):
                dve.wait_ge(v_done, step(ins))

            def params(st):
                r0, r1 = st["rounds"]
                dve.wait_ge(t_ready, r0 + 1)
                dve.tensor_copy(prm[:, :], tbank(r0)[:, 0:N_PRM]).then_inc(t_dve, 1)
                dve.wait_ge(t_ready, r1 + 1)
                dve.tensor_copy(prm2[:, :], tbank(r1)[:, 0:176]).then_inc(t_dve, 1)
                for u in range(LEAD):
                    split_lo(dve, lambda j: u)

            def tables():
                dve.wait_ge(small_loaded, 16 * N_SMALL)
                link(dve.tensor_copy(posf[:, :, :], pos[:, :, :]))
                for k in range(2):
                    for tt in range(NT):
                        for i, (f0, f1) in enumerate(((0, 32), (32, 48))):
                            n = step(dve.tensor_scalar(ang[:, k, tt, f0:f1], freq[:, f0:f1], posf[:, i, tt:tt + 1], None, ALU.mult))
                dve.wait_ge(v_done, n)
                for k in range(2):
                    n = step(dve.tensor_scalar(flat(kk[:, k]), flat(ang[:, k]), 1 / TWO_PI, 0.25 if k == 0 else 0.0, ALU.mult, ALU.add))
                dve.wait_ge(v_done, n)
                link(dve.tensor_scalar(flat(kk), flat(kk), MAGIC, None, ALU.add))
                link(dve.tensor_scalar(flat(kk), flat(kk), -MAGIC, None, ALU.add))
                for c in (C1, C2):
                    link(dve.scalar_tensor_tensor(flat(ang), flat(kk), -c, flat(ang), ALU.mult, ALU.add))
                link(dve.tensor_scalar(flat(ang[:, 0]), flat(ang[:, 0]), math.pi / 2, None, ALU.add))
                link(dve.scalar_tensor_tensor(flat(ang), flat(kk), -C3, flat(ang), ALU.mult, ALU.add))
                dve.tensor_scalar(flat(ang), flat(ang), -PI_LOW, PI_LOW, ALU.max, ALU.min).then_inc(ang_ready, 1)
                for i in range(2):
                    link(dve.tensor_tensor(lam2[:, i, :], lamb[:, 2 * i, :], lamb[:, 2 * i + 1, :], ALU.mult))
                    dve.tensor_reduce(lam[:, 2 + i:3 + i], lam2[:, i, :], AX.X, ALU.add).then_inc(lam_sums, 1)
                dve.wait_ge(lam_exps, 1)
                link(dve.tensor_tensor(lam[:, 2:3], lam[:, 1:2], lam[:, 0:1], ALU.subtract))
                link(dve.tensor_scalar(lam[:, 2:3], lam[:, 2:3], -LAM_INIT, None, ALU.add))
                step(dve.tensor_scalar(nsink[:, :], sink[:, :], -1.0, None, ALU.mult))
                step(dve.tensor_scalar(gdiff[:, :], gdiff[:, :], 1.0 - LAM_INIT, None, ALU.mult))

            def norm(st):
                n, w = st["n"], st["width"]
                src, dst = src_of(st), norm_dst(st)
                wait_src(dve, st, 1)
                if st["lo0"] > 0:
                    dve.wait_ge(nlo_ready, st["lo0"])
                if st["rounds"][0] > 2:
                    dve.wait_ge(t_ready, st["rounds"][0])
                dve.scalar_tensor_tensor(dst[:, 1, :], src[:, 1, :], 1.0, src[:, 1, :], ALU.mult, ALU.mult,
                                         accum_out=ss[:, n, 1:2]).then_inc(ss_dve, 1)
                dve.wait_ge(rstd_ready, 2 * n + 2)
                dve.tensor_scalar(dst[:, 1, :], src[:, 1, :], rstd[:, n, 1:2], None, ALU.mult).then_inc(xn_dve, 1)
                kind, i = st["scale"]

                def low(r):
                    m = min(2, w // P - 2 * r)
                    k = st["chunk0"] + 2 * r
                    dve.wait_ge(nhi_ready, st["lo0"] + r + 1)
                    dve.tensor_tensor(aTl[:, k:k + m, :].rearrange("p a b -> p (a b)"),
                                      tmp[:, (st["lo0"] + r) % 2, 0:m * S],
                                      aT[:, k:k + m, :].rearrange("p a b -> p (a b)").bitcast(F32),
                                      ALU.subtract).then_inc(nlo_ready, 1)

                for r, t in enumerate(st["rounds"]):
                    m = min(2, w // P - 2 * r)
                    dve.wait_ge(t_ready, t + 1)
                    if st["lo0"] + r >= 2:
                        dve.wait_ge(nlo_ready, st["lo0"] + r - 1)
                    for c in range(m):
                        k = 2 * r + c
                        scale = prm[:, i + k:i + k + 1] if kind == "prm" else msc[:, i, k:k + 1]
                        if st["shift"] is None:
                            args = (scale, None, ALU.mult)
                        else:
                            layer, part_ = st["shift"]
                            args = (scale, mod[:, layer, part_ * 8 + k:part_ * 8 + k + 1], ALU.mult, ALU.add)
                        ins = dve.tensor_scalar(tmp[:, (st["lo0"] + r) % 2, c * S:(c + 1) * S],
                                                tbank(t)[:, c * S:(c + 1) * S], *args)
                        if c < m - 1:
                            continue
                        ins.then_inc(t_dve, 1)
                    if r > 0:
                        low(r - 1)
                low(len(st["rounds"]) - 1)
                dve.wait_ge(nlo_ready, st["lo0"] + len(st["rounds"]))

            def rope(x1, x2, cos, sin, shape, last):
                n = int(np.prod(shape))
                names = " ".join("abc"[:len(shape)])
                dims = {k: v for k, v in zip("abc", shape[:-1])}
                t1, t2, t3 = [f[:, 0:n].rearrange(f"p ({names}) -> p {names}", **dims)
                              for f in (sp[:, 0, :], sp[:, 1, :], tmp[:, :, :].rearrange("p a b -> p (a b)"))]
                return [lambda: step(dve.tensor_tensor(t1, x1, cos, ALU.mult)),
                        lambda: step(dve.tensor_tensor(t2, x2, sin, ALU.mult)),
                        lambda: link(dve.tensor_tensor(t3, x1, sin, ALU.mult)),
                        lambda: link(dve.tensor_tensor(x1, t1, t2, ALU.subtract)),
                        lambda: link(dve.tensor_tensor(t1, x2, cos, ALU.mult)),
                        lambda: last(dve.tensor_tensor(x2, t1, t3, ALU.add))]

            def rope_first():
                jobs = []
                for c0, h in ((0, 10), (768, 16)):
                    v = z[:, :, c0:c0 + HD * h].rearrange("p t (h s f) -> p t h s f", s=2, f=ROPE_HALF)
                    cos, sin = [trig[:, i, :, 0:ROPE_HALF].unsqueeze(2).broadcast_to([P, NT, h, ROPE_HALF])
                                for i in range(2)]
                    jobs += rope(v[:, :, :, 0, :], v[:, :, :, 1, :], cos, sin, (NT, h, ROPE_HALF),
                                 lambda ins: roped(ins))
                return jobs

            n_roped = [0]

            def roped(ins):
                n_roped[0] += 1
                ins.then_inc(z_roped, 1)
                dve.wait_ge(z_roped, n_roped[0])

            def add_to_x(src, tt, c0, w, k, gated, free, signal):
                xs = x[:, tt, c0:c0 + w]
                if gated:
                    tm = tmp[:, k % 2, 0:w]
                    ins = dve.tensor_tensor(tm, src, gbc[:, c0:c0 + w], ALU.mult)
                    if free is None:
                        link(ins)
                    else:
                        ins.then_inc(u_dve, 1)
                        dve.wait_ge(u_dve, free)
                    ins = dve.tensor_tensor(xs, tm, xs, ALU.add)
                    ins.then_inc(x_ready, 1) if signal else step(ins)
                else:
                    ins = dve.tensor_tensor(xs, src, xs, ALU.add)
                    if free is not None:
                        ins.then_inc(u_dve, 1)
                    else:
                        ins.then_inc(x_ready, 1) if signal else step(ins)

            def gate_diag(e):
                wait_x(dve, e["need"])
                dve.wait_ge(t_dve, T.emptied("D", e["last"]))
                for k in range(8):
                    c = 8 * e["m"] + k
                    ins = dve.tensor_scalar(tmp[:, k // 4, (k % 4) * P:(k % 4 + 1) * P], ident[:, :],
                                            mod[:, e["layer"], c:c + 1], e["factor"], ALU.mult, ALU.mult)
                ins.then_inc(diag_ready, 1)

            def gate(e):
                for r, t in enumerate(e["rounds"]):
                    dve.wait_ge(t_ready, t + 1)
                    dve.tensor_copy(gbc[:, r * 512:(r + 1) * 512], tbank(t)).then_inc(t_dve, 1)
                dve.wait_ge(t_dve, T.emptied("D", e["rounds"][-1]))

            def ada_half(m, j=0):
                for h in range(2):
                    dve.wait_ge(ada_loaded[h], at(j, lambda j: 16 * (m(j)["n"] + 1)))
                for q in range(ADA_POOL, KC):
                    w, c = araw[q // 4][:, q % 4, :], cact[:, q:q + 1]
                    if q == ADA_POOL:
                        ins = dve.tensor_scalar(w, w, c, None, ALU.mult)
                    else:
                        dve.wait_ge(ada_mid, at(j, lambda j: (KC - ADA_POOL) * m(j)["n"] + q - ADA_POOL))
                        ins = dve.scalar_tensor_tensor(w, w, c, last, ALU.mult, ALU.add)
                    last = w
                    ins.then_inc(ada_mid, 1)

            def ada_out(m, j=0):
                m_ = m(j if isinstance(j, int) else 2)
                dve.wait_ge(t_ready, at(j, lambda j: m(j)["t"] + 1))
                c = at(j, lambda j: 4 * m(j)["b"] + 2 * m_["half"])
                dve.tensor_tensor(mod[:, m_["layer"], bass.ds(c, 2)], tbank(m_["t"])[:, 0:2],
                                  prm2[:, bass.ds(c + 72 * m_["layer"], 2)], ALU.add).then_inc(t_dve, 1)

            def ada_outs(mods):
                for what, m in mods:
                    if what == "ada_out":
                        ada_out(lambda j: m)
                    elif what == "gate":
                        gate(m)

            def linear(st):
                jobs = []
                if st["side"] is not None:
                    dve.wait_ge(trig_ready, 1)
                    wait_emptied(dve, U, lambda j: st["side"])
                    jobs = rope_first()
                k = 0
                for b, (n0, w, parts, fills, mods) in enumerate(st["blocks"]):
                    for u, _, _ in parts:
                        split_lo(dve, lambda j: u + LEAD)
                        for job in jobs[:2]:
                            job()
                        jobs = jobs[2:]
                        for what, m in mods if u == parts[0][0] else ():
                            if what == "ada_mid":
                                ada_half(lambda j: m)
                            elif what == "gate_diag":
                                gate_diag(m)
                            elif what == "tables":
                                tables()
                    ada_outs(mods)
                    if st["dst"] != "x":
                        continue
                    for tt in range(NT):
                        dve.wait_ge(u_ready, fills[tt] + 1)
                        add_to_x(ubank(fills[tt])[:, 0:w], tt, n0, w, k, st["gate"],
                                 U.emptied("D", fills[tt]), b == len(st["blocks"]) - 1)
                        k += 1
                for job in jobs:
                    job()

            def mlp(st):
                nk = st["hb"] // P

                def body(j):
                    for what, e, get in events(st, j):
                        if what in ("up", "down"):
                            split_lo(dve, lambda j: get(j)["u"] + LEAD, j)
                        if what == "hidT":
                            to = slice(e["tt"] * P, (e["tt"] + 1) * P)
                            dve.wait_ge(t_act, at(j, lambda j: T.emptied("A", get(j)["t"])))
                            dve.tensor_tensor(hTl[:, 0:nk, to], tbank(e["t"])[:, 0:nk * P].rearrange("p (a b) -> p a b", b=P),
                                              hT[:, 0:nk, to].bitcast(F32), ALU.subtract).then_inc(t_dve, 1)
                        elif what == "up" and e["k0"] + e["nk"] == KC:
                            for tt in range(NT):
                                dve.wait_ge(r_ready, at(j, lambda j: st["r0"] + NT * j + tt + 1))
                                bank = ubank(e["fills"][tt])
                                if st["mlp"] == "relu2":
                                    ins = dve.scalar_tensor_tensor(hid(tt), bank, 0.0, part(tt), ALU.max, ALU.mult)
                                else:
                                    ins = dve.tensor_tensor(hid(tt)[:, 0:HB2], bank[:, HB2:2 * HB2],
                                                            part(tt)[:, 0:HB2], ALU.mult)
                                ins.then_inc(u_dve, 1)
                        elif what == "ada_mid":
                            ada_half(get, j)
                        elif what == "ada_out":
                            ada_out(get, j)
                        elif what == "gate_diag":
                            gate_diag(e)
                        elif what == "gate":
                            gate(e)
                run_steps(dve, st, body)
                k = 0
                for tt in range(NT):
                    for nb in range(2):
                        dve.wait_ge(w_used, st["acc_ready"] - 3 + k)
                        add_to_x(ACC[:, 2 * tt + nb, :], tt, nb * 512, 512, k, st["gate"], None, nb == 1)
                        k += 1
                ada_outs(st["tail"])

            def turns_of(st):
                for t, dst in zip(st["rounds"], transposes(st)[1]):
                    if "D" in T.who[t]:
                        dve.wait_ge(t_ready, t + 1)
                        for i, (to, r0, n, c0, c1) in enumerate(dst):
                            ins = dve.tensor_copy(to, view(tbank(t)[r0:r0 + n, c0:c1], to))
                        ins.then_inc(t_dve, 1)

            def o_T(st):
                for r, t in enumerate(st["rounds"]):
                    k = st["chunk0"] + 2 * r
                    dve.wait_ge(t_act, T.emptied("A", t))
                    dve.tensor_tensor(aTl[:, k:k + 2, :].rearrange("p a b -> p (a b)"), tbank(t),
                                      aT[:, k:k + 2, :].rearrange("p a b -> p (a b)").bitcast(F32),
                                      ALU.subtract).then_inc(t_dve, 1)

            def smax(g, prev):
                n, nh, nk, kind, t = g["g"], g["nh"], g["nk"], g["kind"], g["t"]
                b = n % 3
                dve.wait_ge(s_ready, n + 1)
                if prev is not None:
                    dve.wait_ge(t_ready, prev["rounds"][-1] + 1)
                if kind == "cmp":
                    full = probs(g)[:, 0:S]
                    link(dve.memset(full, 0.0))
                    s_ = full.rearrange("p (h k) -> p h k", k=32)[:, :, 0:NC]
                    ps_ = sbank(n)[:, 0:S].rearrange("p (h k) -> p h k", k=32)[:, :, 0:NC]
                    mask = cneg[:, t, :]
                else:
                    s_ = probs(g)[:, 0:nh * S].rearrange("p (h k) -> p h k", k=S)[:, :, 0:nk]
                    ps_ = sbank(n)[:, 0:nh * S].rearrange("p (h k) -> p h k", k=S)[:, :, 0:nk]
                    mask = (band if kind == "swa" else causal)[:, 0:S] if t else causal[:, P:S]
                if kind == "cross":
                    dve.tensor_copy(s_, ps_).then_inc(s_taken, 1)
                else:
                    dve.tensor_tensor(s_, ps_, mask.unsqueeze(1).broadcast_to([P, nh, s_.shape[2]]),
                                      ALU.add).then_inc(s_taken, 1)
                dve.wait_ge(s_taken, n + 1)
                link(dve.tensor_reduce(rmax[:, b, 0:nh], s_, AX.X, ALU.max))
                if kind == "cmp":
                    dve.tensor_tensor(s_, s_, rmax[:, b, 0:nh].unsqueeze(2).broadcast_to([P, nh, NC]),
                                      ALU.subtract).then_inc(m_ready, 1)
                    return
                scale = {"cross": CROSS_SCALE, "mla": MLA_SCALE}.get(kind, SWA_SCALE)
                ins = dve.tensor_scalar(negm[:, b, 0:nh], rmax[:, b, 0:nh], -scale, None, ALU.mult)
                if kind == "swa":
                    h0 = g["h0"]
                    link(ins)
                    link(dve.tensor_tensor(negm[:, b, 0:4], negm[:, b, 0:4], nsink[:, h0:h0 + 4], ALU.min))
                    ins = dve.tensor_tensor(dsk[:, b, 0, :], sink[:, h0:h0 + 4], negm[:, b, 0:4], ALU.add)
                ins.then_inc(m_ready, 1)

            def after(g):
                n, nh, kind, t, h0 = g["g"], g["nh"], g["kind"], g["t"], g["h0"]
                b = n % 3
                dve.wait_ge(p_ready, n + 1)
                if kind == "cmp":
                    v = probs(g)[:, 0:S].rearrange("p (h k) -> p h k", k=32)[:, :, 0:NC]
                    dve.tensor_tensor(v, v, cmask[:, t, :].unsqueeze(1).broadcast_to([P, nh, NC]),
                                      ALU.mult).then_inc(p_mixed, 1)
                    dve.wait_ge(p_mixed, g["mixed"])
                    link(dve.tensor_reduce(sums[:, b, 0:nh], v, AX.X, ALU.add))
                if kind == "swa":
                    link(dve.tensor_tensor(sums[:, b, 0:4], sums[:, b, 0:4], dsk[:, b, 1, :], ALU.add))
                if kind in ("mla", "nsa", "cmp"):
                    link(dve.tensor_scalar(sums[:, b, 0:nh], sums[:, b, 0:nh], 1e-20, None, ALU.max))
                n_ = step(dve.reciprocal(rinv[:, b, 0:nh], sums[:, b, 0:nh]))
                if kind == "diff":
                    dve.wait_ge(v_done, n_)
                    link(dve.tensor_scalar(rg[:, b, 0:2], rinv[:, b, 1:4:2], lam[:, 2:3], None, ALU.mult))
                    nk = g["nk"]
                    for i in range(2):
                        p0 = probs(g)[:, 2 * i * S:2 * i * S + nk]
                        p1 = probs(g)[:, (2 * i + 1) * S:(2 * i + 1) * S + nk]
                        link(dve.tensor_scalar(p1, p1, rg[:, b, i:i + 1], None, ALU.mult))
                        ins = dve.scalar_tensor_tensor(p0, p0, rinv[:, b, 2 * i:2 * i + 1], p1, ALU.mult, ALU.add)
                        if i == 0:
                            step(ins)
                    ins.then_inc(p_mixed, 1)
                if kind in ("nsa", "cmp"):
                    dve.wait_ge(v_done, n_)
                    branch = 0 if kind == "cmp" else 1 + g["br"]
                    dve.wait_ge(gates_ready, 1)
                    gv = gates[:, t, :].rearrange("p (h b) -> p h b", b=3)[:, h0:h0 + nh, branch]
                    n_ = step(dve.tensor_tensor(rg[:, b, 0:nh], rinv[:, b, 0:nh], gv, ALU.mult))
                g["scaled"] = n_

            def o_out(g):
                n, nh, kind, t, h0, f = g["g"], g["nh"], g["kind"], g["t"], g["h0"], g["fill"]
                b = n % 3
                dve.wait_ge(u_ready, f + 1)
                dve.wait_ge(v_done, g["scaled"])
                if kind == "diff":
                    dve.tensor_copy(xn[:, t, 512 + P * h0:512 + P * h0 + S], ubank(f)[:, 0:S]).then_inc(u_dve, 1)
                    return
                dv = S if kind == "cross" else HD
                c0 = dv * h0 + (512 if kind == "mla" else 0)
                o = xn[:, t, c0:c0 + nh * dv]
                bank = ubank(f)[:, 0:nh * dv].rearrange("p (h d) -> p h d", d=dv)
                r = rg if kind in ("nsa", "cmp") else rinv
                to = o
                if kind == "cmp" or g.get("br") == 1:
                    to = tmp[:, n % 2, 0:nh * dv]
                dve.tensor_tensor(to.rearrange("p (h d) -> p h d", d=dv), bank,
                                  r[:, b, 0:nh].unsqueeze(2).broadcast_to([P, nh, dv]), ALU.mult).then_inc(u_dve, 1)
                if to is not o:
                    dve.wait_ge(u_dve, U.emptied("D", f))
                    dve.tensor_tensor(o, o, to, ALU.add).then_inc(o_stored, 1)

            def attend(st):
                gs = st["groups"]
                jobs = []
                dve.wait_ge(t_ready, st["turned"][-1] + 1)
                if st["side"]:
                    for t in st["side"]:
                        wait_emptied(dve, T, lambda j: t)
                    jobs = list(conv_jobs)
                for i in range(len(gs) + 3):
                    if i < len(gs):
                        smax(gs[i], gs[i - 3] if i >= 3 else None)
                    if i >= 3:
                        o_out(gs[i - 3])
                    if 1 <= i <= len(gs):
                        g = gs[i - 1]
                        if i >= 4:
                            dve.wait_ge(u_dve, U.emptied("D", gs[i - 4]["fill"]))
                        after(g)
                    for job in jobs[:4]:
                        job()
                    jobs = jobs[4:]
                assert not jobs

            def diff_norm(st):
                dve.wait_ge(u_dve, U.emptied("D", st["fill"]))
                for tt in range(NT):
                    od = xn[:, tt, 512:D]
                    link(dve.tensor_tensor(tmp[:, tt, :], od, od, ALU.mult))
                    dve.tensor_reduce(dss[:, 0, 4 * tt:4 * tt + 4], tmp[:, tt, :].rearrange("p (h d) -> p h d", d=P),
                                      AX.X, ALU.add).then_inc(dn_ss, 1)
                dve.wait_ge(dn_r, 1)
                for tt in range(NT):
                    od = xn[:, tt, 512:D].rearrange("p (h d) -> p h d", d=P)
                    link(dve.tensor_tensor(od, od, dss[:, 2, 4 * tt:4 * tt + 4].unsqueeze(2).broadcast_to([P, 4, P]), ALU.mult))
                    dve.tensor_tensor(od, od, gdiff[:, :].unsqueeze(1).broadcast_to([P, 4, P]), ALU.mult).then_inc(dn_done, 1)

            def scale_x(st):
                n, last = st["n"], st is p.stages[-1]
                wait_x(dve, st["need"])
                dve.wait_ge(t_ready, st["turn"])
                dve.scalar_tensor_tensor(xn[:, 1, :], x[:, 1, :], 1.0, x[:, 1, :], ALU.mult, ALU.mult,
                                         accum_out=ss[:, n, 1:2]).then_inc(ss_dve, 1)
                dve.wait_ge(rstd_ready, 2 * n + 2)
                dve.wait_ge(gain_loaded, 32 if last else 16)
                dve.wait_ge(ss_dve, n + 1)
                for tt in range(NT):
                    dve.scalar_tensor_tensor((xn if last else x)[:, tt, :], x[:, tt, :], rstd[:, n, tt:tt + 1], gbc[:, :],
                                             ALU.mult, ALU.mult).then_inc(out_ready if last else x_ready, 1)

            def mod_cols(st):
                layer, k = st["layer"], st["k"]
                dve.wait_ge(t_dve, T.emptied("D", st["last"]))
                g0 = NORM_G + 8 * (3 * layer + k)
                link(dve.scalar_tensor_tensor(msc[:, k, :], mod[:, layer, 8 * (3 * k + 1):8 * (3 * k + 2)], 1.0,
                                              prm[:, g0:g0 + 8], ALU.add, ALU.mult))

            def conv_chunk(k):
                u_, y_, g_ = [zcf[:, c + k, :] for c in (0, 4, 8)]
                t_ = z[:, k // 2, (k % 2) * S:(k % 2 + 1) * S]
                w = [prm[:, CONV_W + 4 * tap + k:CONV_W + 4 * tap + k + 1] for tap in range(3)]

                def tap(i):
                    link(dve.scalar_tensor_tensor(u_[:, 2 - i:S], t_[:, 0:S - 2 + i], w[i], u_[:, 2 - i:S], ALU.mult, ALU.add))

                return [lambda: link(dve.tensor_tensor(t_, y_, u_, ALU.mult)),
                        lambda: link(dve.tensor_scalar(u_, t_, w[2], None, ALU.mult)),
                        lambda: tap(1),
                        lambda: tap(0),
                        lambda: dve.tensor_tensor(y_, u_, g_, ALU.mult).then_inc(conv_y, 1)]

            conv_jobs = [job for jobs in zip(*(conv_chunk(k) for k in range(4))) for job in jobs]

            def conv(st):
                y_ = zcf[:, 4:8, :]
                dve.wait_ge(conv_y, 4)
                dve.wait_ge(conv_hi, 1)
                dve.tensor_tensor(aTl[:, 0:4, :], y_, aT[:, 0:4, :].bitcast(F32), ALU.subtract).then_inc(conv_done, 1)

            def mla_pack(st):
                wait_emptied(dve, U, lambda j: st["after"])
                h = 8
                q = z[:, :, 0:768].rearrange("p t (h w) -> p t h w", w=96)
                cos, sin = [trig[:, i, :, 32:48] for i in range(2)]
                cb, sb_ = [v.unsqueeze(2).broadcast_to([P, NT, h, ROPE_HALF_2]) for v in (cos, sin)]
                for job in rope(q[:, :, :, 64:80], q[:, :, :, 80:96], cb, sb_, (NT, h, ROPE_HALF_2), link):
                    job()
                for job in rope(z[:, :, 1920:1936], z[:, :, 1936:1952], cos, sin, (NT, ROPE_HALF_2), link):
                    job()
                for tt in range(NT):
                    kf = kfull[:, tt, :].rearrange("p (h w) -> p h w", w=96)
                    kv = z[:, tt, 768:1792].rearrange("p (h w) -> p h w", w=P)
                    step(dve.tensor_copy(kf[:, :, 0:HD], kv[:, :, 0:HD]))
                    ins = dve.tensor_copy(kf[:, :, HD:96], z[:, tt, 1920:1952].unsqueeze(1).broadcast_to([P, 8, 32]))
                    if tt == 0:
                        step(ins)
                ins.then_inc(packed, 1)

            def compress(st):
                wait_emptied(dve, U, lambda j: st["after"])
                dve.tensor_tensor(gates[:, :, :], z[:, :, 1792:1840], gateb[:, :].unsqueeze(1).broadcast_to([P, NT, 48]),
                                  ALU.add).then_inc(gl_ready, 1)
                wait_emptied(dve, T, lambda j: st["turned"][4])
                for kv in range(2):
                    cT = kz[:, 8 + kv, :]
                    for g in range(2):
                        for par in range(2):
                            for ch in range(2):
                                src = cT[HD * g:HD * g + HD, :].rearrange("p (a c q) -> p c a q", c=8, q=2)
                                step(dve.tensor_copy(Rf[kv][HD * par:HD * par + HD, 8 * ch:8 * ch + 8, g * NC:(g + 1) * NC],
                                                     src[:, :, ch:ch + NC, par]))
                    link(dve.memset(Rf[kv][:, :, 2 * NC:32], 0.0))
                    blocks = Rf[kv][:, :, 0:2 * NC]
                    dve.tensor_tensor(blocks, blocks, prm2[:, 144 + 16 * kv:160 + 16 * kv].unsqueeze(2).broadcast_to(
                        [P, 16, 2 * NC]), ALU.add).then_inc(cmp_r, 1)
                for kv in range(2):
                    dve.wait_ge(cmp_r, kv + 1)
                    dve.wait_ge(cmp_rhi, kv + 1)
                    dve.tensor_tensor(Rl[kv][:, :, :], Rf[kv][:, :, :], R[kv][:, :, :].bitcast(F32),
                                      ALU.subtract).then_inc(cmp_rlo, 1)
                for kv in range(2):
                    split_lo(dve, lambda j: st["units"][kv] + LEAD)
                for kv in range(2):
                    t = st["rounds"][2 + kv]
                    dve.wait_ge(t_ready, t + 1)
                    dve.tensor_copy(hidc[:, kv, :], tbank(t)[:, 0:32]).then_inc(t_dve, 1)
                for kv in range(2):
                    t = st["rounds"][4 + kv]
                    bank = tbank(t)
                    dve.wait_ge(t_ready, t + 1)
                    if kv == 0:
                        for g in range(2):
                            for par in range(2):
                                ins = dve.tensor_copy(kcz[HD * par:HD * par + HD, g, par * NC:(par + 1) * NC],
                                                      bank[HD * par:HD * par + HD, g * NC:(g + 1) * NC])
                    else:
                        dve.wait_ge(kz_zero, 1)
                        for g in range(2):
                            for i in range(4):
                                ins = dve.tensor_copy(vcb[32 * i:32 * i + NC, g, i * HD:(i + 1) * HD],
                                                      bank[0:NC, g * HD:(g + 1) * HD])
                    ins.then_inc(t_dve, 1)

            table = dict(params=params, norm=norm, linear=linear, mlp=mlp, qk1=turns_of, qk_cross=turns_of,
                         conv_T=turns_of, qk_mla=turns_of, qk_nsa=turns_of, o_T=o_T, attend=attend, diff_norm=diff_norm,
                         conv=conv, compress=compress, scale_x=scale_x, mod_cols=mod_cols, mla_pack=mla_pack)
            for st in p.stages:
                table[st["kind"]](st)

        @block.gpsimd
        def _(pool):
            def small(dst, src):
                pool.dma_start(dst, src).then_inc(small_loaded, 16)

            n_set = [0]

            def const(ins, wait=False):
                n_set[0] += 1
                ins.then_inc(consts_set, 1)
                if wait:
                    pool.wait_ge(consts_set, n_set[0])

            const(pool.memset(ident[:, :], 0.0), True)
            const(pool.affine_select(out=ident[:, :], in_=ident[:, :], compare_op=ALU.not_equal, fill=1.0, base=0,
                                     pattern=[[-1, P]], channel_multiplier=1))
            const(pool.memset(ones[:, :], 1.0))
            const(pool.memset(mhalf[:, :], -0.5))
            const(pool.memset(causal[:, :], 0.0))
            const(pool.memset(band[:, :], 0.0))
            const(pool.memset(cmask[:, :, :], 1.0), True)
            const(pool.affine_select(out=causal[:, P:S], in_=causal[:, P:S], compare_op=ALU.is_ge, fill=NEG, base=0,
                                     pattern=[[-1, P]], channel_multiplier=1))
            const(pool.affine_select(out=band[:, P:S], in_=band[:, P:S], compare_op=ALU.is_ge, fill=NEG, base=0,
                                     pattern=[[-1, P]], channel_multiplier=1))
            const(pool.affine_select(out=band[:, 0:P], in_=band[:, 0:P], compare_op=ALU.is_gt, fill=NEG, base=0,
                                     pattern=[[1, P]], channel_multiplier=-1))
            for tt in range(NT):
                const(pool.affine_select(out=cmask[:, tt, :], in_=cmask[:, tt, :], compare_op=ALU.is_ge, fill=0.0,
                                         base=tt * P - 31, pattern=[[-16, NC]], channel_multiplier=1), tt == 1)
            const(pool.tensor_scalar(cneg[:, :, :], cmask[:, :, :], -1.0, -NEG, ALU.add, ALU.mult))
            const(pool.memset(kz[:, :, :], 0.0))
            const(pool.memset(kcz[:, :, :], 0.0), True)
            assert n_set[0] == N_CONST

            for i in range(2):
                for t in range(NT):
                    small(pos[:, i, t:t + 1], A["positions_2" if i else "positions"][0, t * P:(t + 1) * P].rearrange("(p a) -> p a", a=1))
            small(freq[:, :], A["rope_freq"].partition_broadcast(P))
            for i, name in enumerate(("lambda_q1", "lambda_k1", "lambda_q2", "lambda_k2")):
                small(lamb[:, i, :], A[name][0].partition_broadcast(P))
            small(sink[:, :], A["sinks"][0].partition_broadcast(P))
            small(gdiff[:, :], A["g_diff"][0].partition_broadcast(P))
            small(gateb[:, :], A["nsa_gate_b_2"][0].partition_broadcast(P))
            for i in range(2):
                small(w2s[:, 0, i * HD:(i + 1) * HD], A["nsa_cmp_w2_2"][0, 0])
            small(w2s[:, 1, 0:HD], A["nsa_cmp_w2_2"][0, 1])
            pool.dma_start(gbc[:, :], A["g_final"].partition_broadcast(P)).then_inc(gain_loaded, 16)

            def rms(st):
                n = st["n"]
                for tt, squares in ((0, ss_act), (1, ss_dve)):
                    pool.wait_ge(squares, n + 1)
                    g_step(pool.tensor_scalar(ms[:, n % 2, tt:tt + 1], ss[:, n, tt:tt + 1], 1.0 / st.get("width", D),
                                              st["eps"], ALU.mult, ALU.add))
                    pool.tensor_tensor(rstd[:, n, tt:tt + 1], ms[:, n % 2, tt:tt + 1], mhalf[:, 0:1], ALU.pow
                                       ).then_inc(rstd_ready, 1)

            n_steps = [0]

            def g_step(ins):
                n_steps[0] += 1
                ins.then_inc(g_done, 1)
                pool.wait_ge(g_done, n_steps[0])

            def ada_in(m, j=0):
                m_ = m(j if isinstance(j, int) else 2)
                if isinstance(j, int) and m_["n"] == 0:
                    pool.wait_ge(cact_ready, 1)
                if m_["prev"] is not None:
                    pool.wait_ge(t_ready, at(j, lambda j: m(j)["prev"] + 1))
                pool.wait_ge(ada_loaded[0], at(j, lambda j: 16 * (m(j)["n"] + 1)))
                for q in range(ADA_POOL):
                    if q == 4:
                        pool.wait_ge(ada_loaded[1], at(j, lambda j: 16 * (m(j)["n"] + 1)))
                    w = araw[q // 4][:, q % 4, :]
                    pool.tensor_tensor(w if q else asum, w, cact[:, q:q + 1].broadcast_to([P, ADA_W]),
                                       ALU.mult).then_inc(ada_sum, 1)
                    if q:
                        pool.wait_ge(ada_sum, at(j, lambda j: ada_count(m(j)["n"], q) - 1))
                        pool.tensor_tensor(asum, asum, w, ALU.add).then_inc(ada_sum, 1)
                pool.wait_ge(ada_sum, at(j, lambda j: ada_count(m(j)["n"], ADA_POOL - 1)))
                pool.wait_ge(ada_mid, at(j, lambda j: (KC - ADA_POOL) * (m(j)["n"] + 1)))
                pool.tensor_tensor(asum, asum, araw[1][:, 3, :], ALU.add).then_inc(ada_sum, 1)

            for st in p.stages:
                for b in st.get("blocks", ()):
                    for what, m in b[4]:
                        if what == "ada_in":
                            ada_in(lambda j: m)
                if st["kind"] == "mlp" and any(what == "ada_in" for s_ in st["steps"] for what, _ in s_):
                    def body(j):
                        for what, e, get in events(st, j):
                            if what == "ada_in":
                                ada_in(get, j)
                    run_steps(pool, st, body)
                if st["kind"] == "scale_x" and st is p.stages[-1]:
                    pool.wait_ge(x_ready, st["need"][1])
                    pool.dma_start(gbc[:, :], A["final_g_2"].partition_broadcast(P)).then_inc(gain_loaded, 16)
                if st["kind"] in ("norm", "scale_x"):
                    rms(st)
                elif st["kind"] == "diff_norm":
                    pool.wait_ge(dn_ss, NT)
                    g_step(pool.tensor_scalar(dss[:, 1, :], dss[:, 0, :], 1.0 / P, 1e-5, ALU.mult, ALU.add))
                    pool.tensor_tensor(dss[:, 2, :], dss[:, 1, :], mhalf[:, 0:8], ALU.pow).then_inc(dn_r, 1)
                elif st["kind"] == "attend" and st["which"] == "mla":
                    pool.wait_ge(s_ready, st["groups"][-1]["g"] + 1)
                    g_step(pool.memset(vcb, 0.0))
                    g_step(pool.memset(kz[HD:P, 0:8:2, :], 0.0))
                    pool.memset(kz[0:HD, 1:8:2, :], 0.0).then_inc(kz_zero, 1)


_INS = ["x", "mem", "positions", "g_mix", "w_in", "sinks", "lambda_q1", "lambda_k1", "lambda_q2", "lambda_k2",
        "g_diff", "w_out", "g_cross", "g_mem", "w_cq", "w_ckv", "w_co", "g_mlp", "w_up", "w_down", "g_final", "c_2",
        "positions_2", "ada_w_2", "ada_b_2", "norm_g_2", "final_g_2", "ff_w13_2", "ff_w2_2", "hy_w_in_2",
        "hy_conv_w_2", "hy_q_norm_2", "hy_kv_norm_2", "hy_w_uq_2", "hy_w_ukv_2", "hy_w_out_2", "nsa_w_in_2",
        "nsa_cmp_pe_2", "nsa_cmp_w1_2", "nsa_cmp_w2_2", "nsa_gate_b_2", "nsa_w_out_2"]


def kernel(**inputs):
    import concourse.bacc as bacc
    from concourse.bass_utils import run_bass_kernel_spmd

    nc = bacc.Bacc("TRN2", target_bir_lowering=False, num_devices=1)
    arrays = {name: np.ascontiguousarray(inputs[name]) for name in _INS}
    arrays["rope_freq"] = np.array([10000.0 ** (-i / 32) for i in range(32)] + [10000.0 ** (-i / 16) for i in range(16)],
                                   np.float32)
    A = {name: nc.dram_tensor("in_" + name, a.shape, mybir.dt.from_np(a.dtype), kind="ExternalInput").ap()
         for name, a in arrays.items()}
    out = nc.dram_tensor("out", (1, S, D), F32, kind="ExternalOutput").ap()
    build(nc, A, out)
    r = run_bass_kernel_spmd(nc, [{"in_" + name: a for name, a in arrays.items()}], core_ids=[0])
    return r.results[0]["out"]
```
